# Optimizing a Trainium2 kernel written in Bass

```python
import jax, jax.numpy as jnp
from jax import lax
import numpy as np

D_MODEL = 1024
BATCH = 1
SEQ = 512
DEPTH = 2

CHUNK = 64
Q_BLOCK = 128
PLE_DIM = 256
D_FF = 2816
CONV_DIM = 512
CONV_GROUPS = 8
CONV_K = 3
N_HEADS = 8
NOPE_DIM = 128
ROPE_DIM = 64
V_DIM = 128
Q_LORA = 384
KV_LORA = 256
ROPE_THETA = 10000.0
EPS = 1e-6
QK_DIM = NOPE_DIM + ROPE_DIM
ATTN_SCALE = QK_DIM ** -0.5
IN_SPLITS = (CONV_DIM, CONV_DIM, CONV_DIM, Q_LORA, KV_LORA, ROPE_DIM, D_MODEL, D_MODEL)
IN_COLS = sum(IN_SPLITS)


def rmsnorm(x, g):
    xf = x.astype(jnp.float32)
    y = xf * lax.rsqrt(jnp.mean(xf * xf, axis=-1, keepdims=True) + EPS)
    return (y * g.astype(jnp.float32)).astype(x.dtype)

def swiglu(x, w_gu, w_down):
    g, u = jnp.split(x @ w_gu, 2, axis=-1)
    return (jax.nn.silu(g) * u) @ w_down

def rope_tables(positions):
    inv_freq = ROPE_THETA ** (-jnp.arange(0, ROPE_DIM, 2, dtype=jnp.float32) / ROPE_DIM)
    ang = positions.astype(jnp.float32)[..., None] * inv_freq
    return jnp.cos(ang), jnp.sin(ang)

def apply_rope(x, cos, sin):
    half = ROPE_DIM // 2
    xf = x.astype(jnp.float32)
    x1, x2 = xf[..., :half], xf[..., half:]
    return jnp.concatenate([x1 * cos - x2 * sin, x2 * cos + x1 * sin], axis=-1).astype(x.dtype)

def short_conv_branch(b_gate, c_gate, v, conv_w, w_conv_out):
    seq = v.shape[1]
    z = c_gate * v
    zp = jnp.pad(z, ((0, 0), (CONV_K - 1, 0), (0, 0)))
    y = conv_w[0] * zp[:, 0:seq]
    for j in range(1, CONV_K):
        y = y + conv_w[j] * zp[:, j:j + seq]
    return (b_gate * y) @ w_conv_out

def block_causal_attention(q_nope, q_rope, k_nope, k_rope, v):
    seq = q_nope.shape[1]
    outs = []
    for i in range(seq // Q_BLOCK):
        q0, q1 = i * Q_BLOCK, (i + 1) * Q_BLOCK
        kn, kr, vb = k_nope[:, :q1], k_rope[:, :q1], v[:, :q1]
        s = (jnp.einsum('bqhd,bkhd->bhqk', q_nope[:, q0:q1], kn)
             + jnp.einsum('bqhd,bkd->bhqk', q_rope[:, q0:q1], kr)).astype(jnp.float32) * ATTN_SCALE
        q_chunk = (q0 + jnp.arange(Q_BLOCK)) // CHUNK
        k_chunk = jnp.arange(q1) // CHUNK
        mask = k_chunk[None, :] <= q_chunk[:, None]
        s = jnp.where(mask, s, -1e30)
        pr = jax.nn.softmax(s, axis=-1).astype(v.dtype)
        outs.append(jnp.einsum('bhqk,bkhd->bqhd', pr, vb))
    return jnp.concatenate(outs, axis=1)

def mla_branch(q_c, kv_c, k_r, q_norm_g, kv_norm_g, w_uq, w_ukv, w_mla_out, cos, sin):
    b, s, _ = q_c.shape
    q = (rmsnorm(q_c, q_norm_g) @ w_uq).reshape(b, s, N_HEADS, QK_DIM)
    q_nope = q[..., :NOPE_DIM]
    q_rope = apply_rope(q[..., NOPE_DIM:], cos[:, :, None, :], sin[:, :, None, :])
    kv = (rmsnorm(kv_c, kv_norm_g) @ w_ukv).reshape(b, s, N_HEADS, NOPE_DIM + V_DIM)
    k_nope, v = kv[..., :NOPE_DIM], kv[..., NOPE_DIM:]
    k_rope = apply_rope(k_r, cos, sin)
    o = block_causal_attention(q_nope, q_rope, k_nope, k_rope, v)
    return o.reshape(b, s, N_HEADS * V_DIM) @ w_mla_out

def first_inputs(seed: int = 0) -> dict:
    key = jax.random.key(seed)
    ks = jax.random.split(key, 24)
    f32 = jnp.float32

    def w(k, shape, fan_in):
        return jax.random.normal(k, shape, f32) * (fan_in ** -0.5)

    def gain(k, shape):
        return 1.0 + 0.05 * jax.random.normal(k, shape, f32)

    x = jax.random.normal(ks[0], (BATCH, SEQ, D_MODEL), f32)
    p = jax.random.normal(ks[1], (DEPTH, BATCH, SEQ, PLE_DIM), f32)
    offset = jax.random.randint(ks[2], (BATCH, 1), 0, 4096, dtype=jnp.int32)
    positions = offset + jnp.arange(SEQ, dtype=jnp.int32)[None, :]
    return {
        "x": x,
        "p": p,
        "positions": positions,
        "ffn1_norm": gain(ks[3], (DEPTH, D_MODEL)),
        "ffn1_w_gu": w(ks[4], (DEPTH, D_MODEL, 2 * D_FF), D_MODEL),
        "ffn1_w_down": w(ks[5], (DEPTH, D_FF, D_MODEL), D_FF),
        "mix_norm": gain(ks[6], (DEPTH, D_MODEL)),
        "w_in": w(ks[7], (DEPTH, D_MODEL, IN_COLS), D_MODEL),
        "conv_w": w(ks[8], (DEPTH, CONV_K, CONV_DIM), CONV_K),
        "w_conv_out": w(ks[9], (DEPTH, CONV_DIM, D_MODEL), CONV_DIM),
        "q_norm": gain(ks[10], (DEPTH, Q_LORA)),
        "kv_norm": gain(ks[11], (DEPTH, KV_LORA)),
        "w_uq": w(ks[12], (DEPTH, Q_LORA, N_HEADS * QK_DIM), Q_LORA),
        "w_ukv": w(ks[13], (DEPTH, KV_LORA, N_HEADS * (NOPE_DIM + V_DIM)), KV_LORA),
        "w_mla_out": w(ks[14], (DEPTH, N_HEADS * V_DIM, D_MODEL), N_HEADS * V_DIM),
        "w_o": w(ks[15], (DEPTH, D_MODEL, D_MODEL), D_MODEL),
        "ffn2_norm": gain(ks[16], (DEPTH, D_MODEL)),
        "ffn2_w_gu": w(ks[17], (DEPTH, D_MODEL, 2 * D_FF), D_MODEL),
        "ffn2_w_down": w(ks[18], (DEPTH, D_FF, D_MODEL), D_FF),
        "ple_norm": gain(ks[19], (DEPTH, D_MODEL)),
        "w_ple_gate": w(ks[20], (DEPTH, D_MODEL, D_MODEL), D_MODEL),
        "w_ple_proj": w(ks[21], (DEPTH, PLE_DIM, D_MODEL), PLE_DIM),
        "final_norm": gain(ks[22], (D_MODEL,)),
    }

def first_block(x, p, positions, ffn1_norm, ffn1_w_gu, ffn1_w_down, mix_norm, w_in, conv_w,
              w_conv_out, q_norm, kv_norm, w_uq, w_ukv, w_mla_out, w_o, ffn2_norm, ffn2_w_gu,
              ffn2_w_down, ple_norm, w_ple_gate, w_ple_proj, final_norm):
    cos, sin = rope_tables(positions)
    split_pts = list(np.cumsum(IN_SPLITS)[:-1])
    h = x
    for i in range(DEPTH):
        h = h + 0.5 * swiglu(rmsnorm(h, ffn1_norm[i]), ffn1_w_gu[i], ffn1_w_down[i])

        u = rmsnorm(h, mix_norm[i])
        b_g, c_g, v_c, q_c, kv_c, k_r, g_conv, g_mla = jnp.split(u @ w_in[i], split_pts, axis=-1)
        y_conv = short_conv_branch(b_g, c_g, v_c, conv_w[i], w_conv_out[i])
        y_mla = mla_branch(q_c, kv_c, k_r, q_norm[i], kv_norm[i], w_uq[i], w_ukv[i],
                           w_mla_out[i], cos, sin)
        merged = jax.nn.sigmoid(g_conv) * y_conv + jax.nn.sigmoid(g_mla) * y_mla
        h = h + merged @ w_o[i]

        h = h + 0.5 * swiglu(rmsnorm(h, ffn2_norm[i]), ffn2_w_gu[i], ffn2_w_down[i])

        gate = jax.nn.sigmoid(rmsnorm(h, ple_norm[i]) @ w_ple_gate[i])
        h = h + gate * (p[i] @ w_ple_proj[i])
    return rmsnorm(h, final_norm)


DEPTH_2 = 1

D_RNN = D_MODEL // 2
RNN_BLOCKS = 8
RNN_BLOCK = D_RNN // RNN_BLOCKS
CONV_WIDTH = 4
LRU_C = 8.0
HEAD_DIM = 64
N_KV = 2
REP = N_HEADS // N_KV
D_ATT = N_HEADS * HEAD_DIM
CMP_LEN = 32
CMP_STRIDE = 16
CMP_HIDDEN = 256
SLC_BLOCK = 64
SLC_TOPK = 16
WINDOW = 512
Q_BLOCK_2 = 64
D_FF_2 = 4 * D_MODEL
NEG = -1e30
FORCED = 1e4


def rms_norm(x, g):
    xf = x.astype(jnp.float32)
    y = xf * lax.rsqrt(jnp.mean(xf * xf, axis=-1, keepdims=True) + EPS)
    return (y * g.astype(jnp.float32)).astype(x.dtype)

def modulate(h, shift, scale):
    return h * (1.0 + scale[:, None, :]) + shift[:, None, :]

def alibi_slopes():
    return jnp.asarray(2.0 ** (-8.0 * np.arange(1, N_HEADS + 1) / N_HEADS), jnp.float32)

def causal_depthwise_conv(x, w, b):
    y = lax.conv_general_dilated(x, w[:, None, :], window_strides=(1,), padding=[(CONV_WIDTH - 1, 0)],
                                 dimension_numbers=('NWC', 'WIO', 'NWC'), feature_group_count=x.shape[-1])
    return y + b

def block_diag(x, w, b):
    xb = x.reshape(x.shape[:-1] + (RNN_BLOCKS, RNN_BLOCK))
    return jnp.einsum('bsni,nij->bsnj', xb, w.astype(jnp.float32)).reshape(x.shape) + b.astype(jnp.float32)

def rg_lru(x, w_a, b_a, w_x, b_x, lam):
    xf = x.astype(jnp.float32)
    r = jax.nn.sigmoid(block_diag(xf, w_a, b_a))
    i = jax.nn.sigmoid(block_diag(xf, w_x, b_x))
    log_a = -LRU_C * r * jax.nn.softplus(-lam.astype(jnp.float32))
    a = jnp.exp(log_a)
    u = jnp.sqrt(-jnp.expm1(2.0 * log_a)) * (i * xf)

    def combine(e1, e2):
        a1, b1 = e1
        a2, b2 = e2
        return a1 * a2, a2 * b1 + b2

    _, h = lax.associative_scan(combine, (a, u), axis=1)
    return h.astype(x.dtype)

def to_heads(t):
    B, S, _ = t.shape
    return t.reshape(B, S, N_KV, HEAD_DIM).transpose(0, 2, 1, 3)

def compress_blocks(k, pos_emb, w1, w2):
    B, G, S, D = k.shape
    n_cmp = (S - CMP_LEN) // CMP_STRIDE + 1
    idx = CMP_STRIDE * jnp.arange(n_cmp)[:, None] + jnp.arange(CMP_LEN)[None, :]
    blocks = (k[:, :, idx] + pos_emb).reshape(B, G, n_cmp, CMP_LEN * D)
    return jax.nn.gelu(blocks @ w1) @ w2

def nsa_attention(q, k_c, v_c, k_s, v_s, k_w, v_w, gate_logits,
                  cmp_pos_k, cmp_w1_k, cmp_w2_k, cmp_pos_v, cmp_w1_v, cmp_w2_v):
    B, S, _ = q.shape
    f32 = jnp.float32
    n_cmp = (S - CMP_LEN) // CMP_STRIDE + 1
    n_slc = S // SLC_BLOCK
    n_sel = min(SLC_TOPK, n_slc)
    n_qb = S // Q_BLOCK_2
    qh = q.reshape(B, S, N_KV, REP, HEAD_DIM).transpose(0, 2, 3, 1, 4) * (HEAD_DIM ** -0.5)
    kc = compress_blocks(to_heads(k_c), cmp_pos_k, cmp_w1_k, cmp_w2_k)
    vc = compress_blocks(to_heads(v_c), cmp_pos_v, cmp_w1_v, cmp_w2_v).astype(f32)
    ks = to_heads(k_s).reshape(B, N_KV, n_slc, SLC_BLOCK, HEAD_DIM)
    vs = to_heads(v_s).reshape(B, N_KV, n_slc, SLC_BLOCK, HEAD_DIM)
    pad = ((0, 0), (0, 0), (WINDOW, 0), (0, 0))
    kw = jnp.pad(to_heads(k_w), pad)
    vw = jnp.pad(to_heads(v_w), pad)
    gates = jax.nn.sigmoid(gate_logits.astype(f32)).reshape(B, S, 3, N_KV, REP).transpose(2, 0, 3, 4, 1)
    slopes = alibi_slopes().reshape(1, N_KV, REP, 1, 1)
    c_start = CMP_STRIDE * jnp.arange(n_cmp)
    cmp_end = c_start + (CMP_LEN - 1)
    s_start = SLC_BLOCK * jnp.arange(n_slc)
    overlap = ((c_start[:, None] < s_start[None, :] + SLC_BLOCK) &
               (c_start[:, None] + CMP_LEN > s_start[None, :])).astype(f32)
    blk_ids = jnp.arange(n_slc)
    gather = jax.vmap(jax.vmap(lambda kb, ix: kb[ix]))

    def one_block(i):
        q0 = i * Q_BLOCK_2
        qb = lax.dynamic_slice_in_dim(qh, q0, Q_BLOCK_2, axis=3)
        t = q0 + jnp.arange(Q_BLOCK_2)
        d_c = (t[:, None] - cmp_end[None, :]).astype(f32)
        sc = jnp.einsum('bgrqd,bgcd->bgrqc', qb, kc).astype(f32) - slopes * d_c
        sc = jnp.where(d_c >= 0, sc, NEG)
        p_c = jax.nn.softmax(sc, axis=-1) * (t >= CMP_LEN - 1).astype(f32)[:, None]
        o_c = jnp.einsum('bgrqc,bgcd->bgrqd', p_c, vc)
        imp = jnp.einsum('bgrqc,cj->bgqj', p_c, overlap)
        cur = t // SLC_BLOCK
        forced = (blk_ids[None, :] == 0) | (blk_ids[None, :] == cur[:, None]) | (blk_ids[None, :] == cur[:, None] - 1)
        visible = s_start[None, :] <= t[:, None]
        imp = jnp.where(forced, FORCED, jnp.where(visible, imp, NEG))
        _, sel = lax.top_k(imp, n_sel)
        k_sel = gather(ks, sel)
        v_sel = gather(vs, sel).astype(f32)
        pos = sel[..., None] * SLC_BLOCK + jnp.arange(SLC_BLOCK)
        d_s = (t[:, None, None] - pos).astype(f32)[:, :, None]
        ss = jnp.einsum('bgrqd,bgqnkd->bgrqnk', qb, k_sel).astype(f32) - slopes[..., None] * d_s
        ss = jnp.where(d_s >= 0, ss, NEG)
        p_s = jax.nn.softmax(ss.reshape(ss.shape[:4] + (-1,)), axis=-1).reshape(ss.shape)
        o_s = jnp.einsum('bgrqnk,bgqnkd->bgrqd', p_s, v_sel)
        kwb = lax.dynamic_slice_in_dim(kw, q0, WINDOW + Q_BLOCK_2, axis=2)
        vwb = lax.dynamic_slice_in_dim(vw, q0, WINDOW + Q_BLOCK_2, axis=2).astype(f32)
        s_pos = q0 - WINDOW + jnp.arange(WINDOW + Q_BLOCK_2)
        d_w = (t[:, None] - s_pos[None, :]).astype(f32)
        ok = (d_w >= 0) & (d_w < WINDOW) & (s_pos[None, :] >= 0)
        sw = jnp.einsum('bgrqd,bgkd->bgrqk', qb, kwb).astype(f32) - slopes * d_w
        sw = jnp.where(ok, sw, NEG)
        o_w = jnp.einsum('bgrqk,bgkd->bgrqd', jax.nn.softmax(sw, axis=-1), vwb)
        gb = lax.dynamic_slice_in_dim(gates, q0, Q_BLOCK_2, axis=4)[..., None]
        return gb[0] * o_c + gb[1] * o_s + gb[2] * o_w

    out = lax.map(one_block, jnp.arange(n_qb))
    return out.transpose(1, 0, 4, 2, 3, 5).reshape(B, S, D_ATT).astype(q.dtype)

def hybrid_mixer(h, w_in, conv_w, conv_b, lru_wa, lru_ba, lru_wx, lru_bx, lru_lambda,
                 cmp_pos_k, cmp_w1_k, cmp_w2_k, cmp_pos_v, cmp_w1_v, cmp_w2_v,
                 norm_rnn_out, norm_att_out, w_out):
    sizes = [D_RNN, D_RNN, D_ATT] + [N_KV * HEAD_DIM] * 6 + [3 * N_HEADS]
    splits = np.cumsum(sizes)[:-1].tolist()
    z = h @ w_in
    g_rnn, x_rnn, q, k_c, v_c, k_s, v_s, k_w, v_w, gate_logits = jnp.split(z, splits, axis=-1)
    rnn = jax.nn.gelu(g_rnn) * rg_lru(causal_depthwise_conv(x_rnn, conv_w, conv_b),
                                      lru_wa, lru_ba, lru_wx, lru_bx, lru_lambda)
    att = nsa_attention(q, k_c, v_c, k_s, v_s, k_w, v_w, gate_logits,
                        cmp_pos_k, cmp_w1_k, cmp_w2_k, cmp_pos_v, cmp_w1_v, cmp_w2_v)
    y = jnp.concatenate([rms_norm(rnn, norm_rnn_out), rms_norm(att, norm_att_out)], axis=-1)
    return y @ w_out

def second_inputs(seed: int = 0) -> dict:
    key = jax.random.key(seed)
    ks = jax.random.split(key, 32)
    L = DEPTH_2
    f32 = jnp.float32

    def nrm(k, shape, scale):
        return jax.random.normal(k, shape, f32) * scale

    def gain(k, n):
        return 1.0 + 0.05 * jax.random.normal(k, (L, n), f32)

    d_in = 2 * D_RNN + D_ATT + 6 * N_KV * HEAD_DIM + 3 * N_HEADS
    u = jax.random.uniform(ks[31], (L, D_RNN), f32, minval=0.9, maxval=0.999)
    a0 = u ** (1.0 / LRU_C)
    lam = jnp.log(a0) - jnp.log1p(-a0)
    return {
        'x': nrm(ks[0], (BATCH, SEQ, D_MODEL), 1.0),
        'c': nrm(ks[1], (BATCH, D_MODEL), 1.0),
        'ada_w': nrm(ks[2], (L, D_MODEL, 6 * D_MODEL), 0.1 * D_MODEL ** -0.5),
        'ada_b': nrm(ks[3], (L, 6 * D_MODEL), 0.01),
        'pre_norm_mix': gain(ks[4], D_MODEL),
        'w_in': nrm(ks[5], (L, D_MODEL, d_in), D_MODEL ** -0.5),
        'conv_w': nrm(ks[6], (L, CONV_WIDTH, D_RNN), CONV_WIDTH ** -0.5),
        'conv_b': nrm(ks[7], (L, D_RNN), 0.01),
        'lru_wa': nrm(ks[8], (L, RNN_BLOCKS, RNN_BLOCK, RNN_BLOCK), RNN_BLOCK ** -0.5),
        'lru_ba': nrm(ks[9], (L, D_RNN), 0.01),
        'lru_wx': nrm(ks[10], (L, RNN_BLOCKS, RNN_BLOCK, RNN_BLOCK), RNN_BLOCK ** -0.5),
        'lru_bx': nrm(ks[11], (L, D_RNN), 0.01),
        'lru_lambda': lam,
        'cmp_pos_k': nrm(ks[12], (L, CMP_LEN, HEAD_DIM), 0.1),
        'cmp_w1_k': nrm(ks[13], (L, CMP_LEN * HEAD_DIM, CMP_HIDDEN), (CMP_LEN * HEAD_DIM) ** -0.5),
        'cmp_w2_k': nrm(ks[14], (L, CMP_HIDDEN, HEAD_DIM), CMP_HIDDEN ** -0.5),
        'cmp_pos_v': nrm(ks[15], (L, CMP_LEN, HEAD_DIM), 0.1),
        'cmp_w1_v': nrm(ks[16], (L, CMP_LEN * HEAD_DIM, CMP_HIDDEN), (CMP_LEN * HEAD_DIM) ** -0.5),
        'cmp_w2_v': nrm(ks[17], (L, CMP_HIDDEN, HEAD_DIM), CMP_HIDDEN ** -0.5),
        'norm_rnn_out': gain(ks[18], D_RNN),
        'norm_att_out': gain(ks[19], D_ATT),
        'w_out': nrm(ks[20], (L, D_RNN + D_ATT, D_MODEL), (D_RNN + D_ATT) ** -0.5),
        'post_norm_mix': gain(ks[21], D_MODEL),
        'pre_norm_mlp': gain(ks[22], D_MODEL),
        'w_ff1': nrm(ks[23], (L, D_MODEL, D_FF_2), D_MODEL ** -0.5),
        'w_ff2': nrm(ks[24], (L, D_FF_2, D_MODEL), D_FF_2 ** -0.5),
        'post_norm_mlp': gain(ks[25], D_MODEL),
    }

def second_block(x, c, ada_w, ada_b, pre_norm_mix, w_in, conv_w, conv_b, lru_wa, lru_ba, lru_wx, lru_bx,
              lru_lambda, cmp_pos_k, cmp_w1_k, cmp_w2_k, cmp_pos_v, cmp_w1_v, cmp_w2_v,
              norm_rnn_out, norm_att_out, w_out, post_norm_mix, pre_norm_mlp, w_ff1, w_ff2, post_norm_mlp):
    for l in range(DEPTH_2):
        mod = jax.nn.silu(c) @ ada_w[l] + ada_b[l]
        sh1, sc1, g1, sh2, sc2, g2 = jnp.split(mod, 6, axis=-1)
        h = modulate(rms_norm(x, pre_norm_mix[l]), sh1, sc1)
        y = hybrid_mixer(h, w_in[l], conv_w[l], conv_b[l], lru_wa[l], lru_ba[l], lru_wx[l], lru_bx[l],
                         lru_lambda[l], cmp_pos_k[l], cmp_w1_k[l], cmp_w2_k[l], cmp_pos_v[l], cmp_w1_v[l],
                         cmp_w2_v[l], norm_rnn_out[l], norm_att_out[l], w_out[l])
        x = x + (1.0 + g1[:, None, :]) * rms_norm(y, post_norm_mix[l])
        h = modulate(rms_norm(x, pre_norm_mlp[l]), sh2, sc2)
        y = jnp.square(jax.nn.relu(h @ w_ff1[l])) @ w_ff2[l]
        x = x + (1.0 + g2[:, None, :]) * rms_norm(y, post_norm_mlp[l])
    return x


def setup_inputs(seed=0):
    out = dict(first_inputs(seed))
    for name, value in second_inputs(seed + 1).items():
        if name != "x":
            out[name + "_2"] = value
    return out


def reference(
    x, p, positions, ffn1_norm, ffn1_w_gu, ffn1_w_down, mix_norm, w_in, conv_w, w_conv_out,
    q_norm, kv_norm, w_uq, w_ukv, w_mla_out, w_o, ffn2_norm, ffn2_w_gu, ffn2_w_down, ple_norm,
    w_ple_gate, w_ple_proj, final_norm, c_2, ada_w_2, ada_b_2, pre_norm_mix_2, w_in_2, conv_w_2,
    conv_b_2, lru_wa_2, lru_ba_2, lru_wx_2, lru_bx_2, lru_lambda_2, cmp_pos_k_2, cmp_w1_k_2,
    cmp_w2_k_2, cmp_pos_v_2, cmp_w1_v_2, cmp_w2_v_2, norm_rnn_out_2, norm_att_out_2, w_out_2,
    post_norm_mix_2, pre_norm_mlp_2, w_ff1_2, w_ff2_2, post_norm_mlp_2,
):
    x = first_block(
        x, p, positions, ffn1_norm, ffn1_w_gu, ffn1_w_down, mix_norm, w_in, conv_w, w_conv_out,
        q_norm, kv_norm, w_uq, w_ukv, w_mla_out, w_o, ffn2_norm, ffn2_w_gu, ffn2_w_down,
        ple_norm, w_ple_gate, w_ple_proj, final_norm,
    )
    return second_block(
        x, c_2, ada_w_2, ada_b_2, pre_norm_mix_2, w_in_2, conv_w_2, conv_b_2, lru_wa_2,
        lru_ba_2, lru_wx_2, lru_bx_2, lru_lambda_2, cmp_pos_k_2, cmp_w1_k_2, cmp_w2_k_2,
        cmp_pos_v_2, cmp_w1_v_2, cmp_w2_v_2, norm_rnn_out_2, norm_att_out_2, w_out_2,
        post_norm_mix_2, pre_norm_mlp_2, w_ff1_2, w_ff2_2, post_norm_mlp_2,
    )


_drawn_inputs = setup_inputs


def setup_inputs(seed=0):
    import zlib

    import numpy as np

    out = dict(_drawn_inputs(seed))
    spreads = {}
    factors = {'q_norm': 8.0,
     'kv_norm': 5.792,
     'ple_norm': 4.188,
     'lru_ba_2': 55.245,
     'lru_bx_2': 26.533,
     'cmp_pos_k_2': 8.0}
    for name, (base, spread) in spreads.items():
        noise = np.random.default_rng([zlib.crc32(name.encode()), seed]).standard_normal(out[name].shape)
        drawn = base * np.exp(spread * noise) if base else spread * noise
        out[name] = __import__('jax').numpy.asarray(drawn.astype(out[name].dtype))
    for name, factor in factors.items():
        out[name] = (out[name] * factor).astype(out[name].dtype)
    return out
```

```python
import numpy as np
import concourse.bass as bass
from concourse import mybir
from contextlib import ExitStack

F32 = mybir.dt.float32
F32R = mybir.dt.float32r
I32 = mybir.dt.int32
ALU = mybir.AluOpType
ACT = mybir.ActivationFunctionType
AX = mybir.AxisListType.X

P = 128
S = 512
D = 1024
KD = D // P
DEPTH = 2
D_FF = 2816
FF_TILES = D_FF // P
FF_GROUPS = [8, 8, 6]
HEADS = 8
NOPE, ROPE = 128, 64
Q_LORA, KV_LORA, CONV, PLE = 384, 256, 512, 256
EPS = 1e-6
SCALE1 = float(NOPE + ROPE) ** -0.5
NEG = -1e30
QT = S // P

RING = 4
AHEAD = 2

FFN_SLOTS = [2 * f for f in FF_GROUPS]
K_TILES = []
STAGE = {}


def _stage(name, tiles):
    STAGE[name] = len(K_TILES)
    K_TILES.extend(tiles)


def _ffn(name):
    for g, f in enumerate(FF_GROUPS):
        _stage(f"{name}_up{g}", [KD] * (2 * f))
        _stage(f"{name}_down{g}", [f] * KD)


_ffn("ffn1")
_stage("lora", [KD] * 6)
_stage("conv", [KD] * 12)
_stage("gates", [KD] * 16)
_stage("heads", [Q_LORA // P, Q_LORA // P, KV_LORA // P, KV_LORA // P] * HEADS)
_stage("branch_out", [CONV // P, KD] * KD)
_stage("mix_out", [KD] * KD)
_ffn("ffn2")
_stage("ple_gate", [KD] * KD)
_stage("ple_proj", [PLE // P] * KD)
LAYER_SLOTS = len(K_TILES)
LAYER_STEP = -(-LAYER_SLOTS // RING) * RING
LOADS = [len(range(p, LAYER_SLOTS, RING)) for p in range(RING)]

FF2_TILES = 4 * D // P
FF2_GROUPS = FF2_TILES // KD
IN2 = 19
B2_IN, B2_OUT = 0, IN2
B2_FF = B2_OUT + KD
B2_SLOTS = B2_FF + FF2_GROUPS * 2 * KD

V_MIX, V_FFN2, V_PLE, V_NEXT, V_Q, V_KV, V_CONV = 0, 8, 16, 24, 32, 35, 37
N_VEC = 49
C_PRE, C_POST, C_PREM, C_POSTM, C_RNN, C_ATT = 0, 8, 16, 24, 32, 36
C_CW, C_CB, C_BA, C_BX, C_LAM, C_ADAB = 40, 56, 60, 64, 68, 72
N_COL2 = 120
ADA_BATCH = 6
N_CMP, CMP_K = 31, 16
SLOPES = [2.0 ** -(h + 1) for h in range(HEADS)]
TWO_PI = float(2 * np.pi)
PI_A = 6.28125
PI_B = float(np.float32(np.float32((TWO_PI - PI_A) * 4096 * 64).round() / (4096 * 64)))
PI_C = float(TWO_PI - PI_A - PI_B)
ROUND = 12582912.0


class Slot:

    def __init__(self, layer, s, it=0, step=0):
        last = s == LAYER_SLOTS - 1 and not (isinstance(layer, int) and layer == DEPTH)
        if s >= LAYER_SLOTS and not (isinstance(layer, int) and layer == DEPTH):
            layer, s = layer + 1, s - LAYER_SLOTS
        in_b2 = isinstance(layer, int) and layer == DEPTH
        self.tiles = KD if in_b2 else K_TILES[s]
        self.number = layer * LAYER_STEP + s + step * it
        self.pos = s % RING
        self.loads = (layer * LOADS[self.pos] + s // RING + 1 + (step // RING) * it) * 16
        self.inc = LAYER_STEP - LAYER_SLOTS + 1 if last else 1

    @property
    def free(self):
        return self.number + 1

    @property
    def done(self):
        return self.number + RING + 1


def same_ahead(s0, n, step):
    return all((K_TILES + [KD] * AHEAD)[s0 + n * step + j] == K_TILES[s0 + j] for j in range(AHEAD))


def repeat(eng, s0, n, step, body):
    m = n if same_ahead(s0, n, step) else n - 1
    with eng.Fori(0, m) as it:
        body(it)
    if m < n:
        body(m)


def build(nc, I, out_t):
    ctx = ExitStack()
    with ctx:
        def sem(name):
            return ctx.enter_context(nc.semaphore(name))

        def sb(name, shape, dt=F32):
            return ctx.enter_context(nc.sbuf_tensor(name, shape, dt))

        def ps(name, shape):
            return ctx.enter_context(nc.psum_tensor(name, shape, F32))

        base = [-(-nc.sbuf_base // 32) * 32]

        def place(name, cols, dt=F32, at=None):
            o = base[0] if at is None else at
            t = nc.alloc_sbuf_tensor_at(name, [P, cols], dt, offset=o)
            if at is None:
                base[0] += -(-cols * 4 // 32) * 32
            return t, o

        def tiles(t):
            return lambda i: t[:, i * S:(i + 1) * S]

        raw, _ = place("raw", RING * KD * P)
        w_hi, _ = place("w_hi", RING * KD * P, F32R)
        w_lo, _ = place("w_lo", RING * KD * P, F32R)
        h_t, _ = place("h", KD * S)
        u_hi_t, u_at = place("u_hi", KD * S, F32R)
        u_lo_t, _ = place("u_lo", KD * S, F32R)
        a_hi_t, a_at = place("a_hi", 9 * S, F32R)
        a_lo_t, _ = place("a_lo", 9 * S, F32R)
        gate_t, g_at = place("gate", 2 * KD * S)
        merged_t, _ = place("merged", 2 * KD * S, F32R, at=g_at)
        ux_t, _ = place("ux", 2 * KD * S, at=u_at)
        ax_t, _ = place("ax", 18 * S, at=a_at)
        work_t, _ = place("work", 16 * S)
        sq_t, _ = place("sq", S)
        acc_t, _ = place("acc", S)
        rs_t, _ = place("rs", S)
        cs_t, _ = place("rope_table", S)
        ones, _ = place("ones", P)
        ident, _ = place("ident", P)
        fold, _ = place("fold", P)
        ident_r, _ = place("ident_r", P, F32R)
        cmask_r, _ = place("chunk_mask_r", P, F32R)
        vec, _ = place("vec", N_VEC)
        stat_t, _ = place("row_stats", 72)
        mod_t, _ = place("mod", 48)
        c_t, _ = place("c_cols", 2 * KD)
        col2, _ = place("col2", N_COL2)
        modc, _ = place("mod_cols", 32)
        h, u_hi, u_lo, a_hi, a_lo = map(tiles, (h_t, u_hi_t, u_lo_t, a_hi_t, a_lo_t))
        gate, ux, ax, work = map(tiles, (gate_t, ux_t, ax_t, work_t))
        sq, acc, rs, cs = sq_t[:, :], acc_t[:, :], rs_t[:, :], cs_t[:, :]
        vec0 = modc[:, 0:KD]
        small2 = stat_t[:, 32:64]
        eps_t = small2[:, 28:29]
        cmask = work(2)[:, 0:P]
        merged_hi = lambda m: merged_t[:, 2 * m * S:(2 * m + 1) * S]
        merged_lo = lambda m: merged_t[:, (2 * m + 1) * S:(2 * m + 2) * S]

        def wt(t, slot, n, k=None):
            o = slot.pos * KD * P
            return t[:, o:o + n * P] if k is None else t[:, o + k * P:o + (k + 1) * P]

        proj = ps("proj", [P, RING, S])
        sc = ps("sc", [P, 2, S])
        tr = ps("tr", [P, S])
        ot = ps("ot", [P, S])

        raw_in = [sem(f"raw_in{p}") for p in range(RING)]
        w_hi_ready = sem("w_hi_ready")
        w_lo_ready = sem("w_lo_ready")
        slot_done = sem("slot_done")
        slot_read = sem("slot_read")
        b2_in, w1_in, w2_in = sem("b2_in"), sem("w1_in"), sem("w2_in")
        mods_ready, hf_ready, tmp_ready = sem("mods_ready"), sem("hf_ready"), sem("tmp_ready")
        xf_ready, rg_done, rg_tanh, la_ready = sem("xf_ready"), sem("rg_done"), sem("rg_tanh"), sem("la_ready")
        decay_ready, v2_ready, ix_ready, sqrt_ready = (sem(n) for n in ("decay_ready", "v2_ready", "ix_ready", "sqrt_ready"))
        gel_sq, gel_in, gel_tanh, rnn_ready = sem("gel_sq"), sem("gel_in"), sem("gel_tanh"), sem("rnn_ready")
        x_built, hid_done, hid_in, hid_tanh, hid_ready = (sem(n) for n in ("x_built", "hid_done", "hid_in", "hid_tanh", "hid_ready"))
        kv_cmp_done, kv_cmp_ready = sem("kv_cmp_done"), sem("kv_cmp_ready")
        g_tanh, g_turned, g_cols, g_ready = sem("g_tanh"), sem("g_turned"), sem("g_cols"), sem("g_ready")
        v2_turned, v2_copied, bias_step, bias_ready = (sem(n) for n in ("v2_turned", "v2_copied", "bias_step", "bias_ready"))
        q_ready, cs_done, cs_exp, pc_step, pc_ready = (sem(n) for n in ("q_ready", "cs_done", "cs_exp", "pc_step", "pc_ready"))
        cs_sub, tc_done, ptc_ready = sem("cs_sub"), sem("tc_done"), sem("ptc_ready")
        s2_done, max2, nmax2, exp2, inv2 = sem("s2_done"), sem("max2"), sem("nmax2"), sem("exp2"), sem("inv2")
        ginv2, p2_ready, t2_done, pt2_ready, o2_done, o2_ready = (sem(n) for n in ("ginv2", "p2_ready", "t2_done", "pt2_ready", "o2_done", "o2_ready"))
        mix_sq, mix_stat, mix_rms, mix_rs, mix_norm = (sem(n) for n in ("mix_sq", "mix_stat", "mix_rms", "mix_rs", "mix_norm"))
        y_scaled, h2_ready, y_zero = sem("y_scaled"), sem("h2_ready"), sem("y_zero")
        relu_sq, h_out = sem("relu_sq"), sem("h_out")
        x_in, const_in, vec_in, p_in, ada_in = (sem(n) for n in ("x_in", "const_in", "vec_in", "p_in", "ada_in"))
        consts_ready = sem("consts_ready")
        start_step = sem("start_step")
        pos_ready, sin_ready, c_tanh, lam_exp = (sem(n) for n in ("pos_ready", "sin_ready", "c_tanh", "lam_exp"))
        u_hi_ready, u_ready = sem("u_hi_ready"), sem("u_ready")
        sq_ready, sum_ready = sem("sq_ready"), sem("sum_ready")
        stat_done, rms_ready, rs_ready = sem("stat_done"), sem("rms_ready"), sem("rs_ready")
        tanh_ready, sil_ready, act_ready = sem("tanh_ready"), sem("sil_ready"), sem("act_ready")
        a_hi_ready, a_lo_ready = sem("a_hi_ready"), sem("a_lo_ready")
        ada_done, mod_read = sem("ada_done"), sem("mod_read")
        lora_sq, lora_stat, lora_rms, lora_rs = (sem(n) for n in ("lora_sq", "lora_stat", "lora_rms", "lora_rs"))
        lora_norm, lora_hi, lora_ready = sem("lora_norm"), sem("lora_hi"), sem("lora_ready")
        kr_rope, kr_fold, kr_ready = sem("kr_rope"), sem("kr_fold"), sem("kr_ready")
        z_step, conv_y, conv_hi, conv_ready = sem("z_step"), sem("conv_y"), sem("conv_hi"), sem("conv_ready")
        gate_tanh = sem("gate_tanh")
        v_turned, v_ready = sem("v_turned"), sem("v_ready")
        s_done, mx_ready, nmax_ready, exp_ready = sem("s_done"), sem("mx_ready"), sem("nmax_ready"), sem("exp_ready")
        rinv_ready, p_ready, t_done, pt_ready = sem("rinv_ready"), sem("p_ready"), sem("t_done"), sem("pt_ready")
        o_done, o_hi_ready, o_ready = sem("o_done"), sem("o_hi_ready"), sem("o_ready")
        mg_step, mg_ready, mg_hi, merged_ready = sem("mg_step"), sem("mg_ready"), sem("mg_hi"), sem("merged_ready")
        p_hi_ready, p_split, ple_tanh, ple_step = sem("p_hi_ready"), sem("p_split"), sem("ple_tanh"), sem("ple_step")
        out_done = sem("out_done")

        block = ctx.enter_context(nc.Block())

        def norm_no(layer, e):
            return 4 * layer + e + 1

        L2 = DEPTH
        xr, gr = (lambda j: ax(j)), (lambda j: ax(4 + j))
        KC, VC, KS, VS, KW, VW = (ax(8 + i) for i in range(6))
        q2 = lambda j: ax(14 + j)
        gT = rs
        w1 = lambda kv, kt, m: gate_t[:, ((kv * CMP_K + kt) * 2 + m) * P:((kv * CMP_K + kt) * 2 + m + 1) * P]
        pos2 = lambda kv: sq_t[:, 384 + 32 * kv:416 + 32 * kv]
        w2k = lambda m: sq_t[:, m * P:(m + 1) * P]
        w2v = lambda m: sq_t[:, 256 + 64 * m:320 + 64 * m]
        X = lambda kv: ux_t[:, (10 + 2 * kv) * S:(10 + 2 * kv) * S + CMP_K * 62]
        hid = lambda kv, m: acc_t[:, (2 * kv + m) * 62:(2 * kv + m + 1) * 62]
        kcmp = cs_t[:, 0:N_CMP]
        vcmp = cs_t[0:N_CMP, 64:192]
        gcols = cs_t[:, 192:288]
        bias_c = ux_t[:, 8 * S:8 * S + HEADS * QT * N_CMP]
        vn_s, vn_w = ux(14), ux(15)
        qbuf, p_c, pt_c = ux(10), ux_t[:, 12 * S:12 * S + QT * N_CMP], ux(13)

        @block.sync
        def _(sp):
            def load(slot, src):
                sp.wait_ge(w_lo_ready, slot.free)
                sp.dma_start(wt(raw, slot, slot.tiles), src).then_inc(raw_in[slot.pos], 16)

            sp.dma_start(h_t[:, :], I["x_t"]).then_inc(x_in, 16)
            sp.dma_start(vec0[:, :], I["vec0"]).then_inc(x_in, 16)
            sp.dma_start(work(0).bitcast(I32), I["positions"].partition_broadcast(P)).then_inc(const_in, 16)
            sp.dma_start(stat_t[:, 0:2], I["rope_consts"]).then_inc(const_in, 16)
            sp.dma_start(c_t[:, 0:KD], I["c_t"]).then_inc(const_in, 16)
            sp.dma_start(col2[:, :], I["col2"]).then_inc(const_in, 16)

            def loads(layer, name, n, src, per=1):
                s0 = STAGE[name]
                if n > RING:
                    with sp.Fori(0, n // RING) as it:
                        for j in range(RING):
                            load(Slot(layer, s0 + j, it, RING), src(it * RING + j))
                else:
                    for j in range(n):
                        load(Slot(layer, s0 + j), src(j))

            def ffn(layer, f):
                name = f"ffn{f + 1}"
                for g, ft in enumerate(FF_GROUPS):
                    f0 = sum(FF_GROUPS[:g])
                    loads(layer, f"{name}_up{g}", 2 * ft, lambda i: I[f"{name}_gu"][layer, 2 * f0 + i])
                    if f == 0 and g == 0:
                        sp.wait_ge(u_ready, KD * (4 * layer + 1))
                        sp.dma_start(vec[:, :], I["vec"][layer]).then_inc(vec_in, 16)
                    if g < 2:
                        b = layer * 4 + f * 2 + g
                        if g == 0:
                            sp.wait_ge(slot_read, Slot(layer, STAGE[f"{name}_up0"]).done - 1)
                            sp.wait_ge(slot_done, Slot(layer, STAGE[f"{name}_up0"]).done - 1)
                        else:
                            sp.wait_ge(ada_done, b)
                        sp.dma_start(gate_t[:, 0:ADA_BATCH * D], I["ada"][b]).then_inc(ada_in, 16)
                    dn = "dn8" if ft == KD else "dn6"
                    loads(layer, f"{name}_down{g}", KD, lambda i: I[f"{name}_{dn}"][layer, (KD * g if ft == KD else 0) + i])

            with sp.Fori(0, DEPTH) as layer:
                ffn(layer, 0)
                for i in range(6):
                    load(Slot(layer, STAGE["lora"] + i), I["in_w"][layer, i])
                loads(layer, "conv", 12, lambda i: I["in_w"][layer, i + 6])
                loads(layer, "gates", 16, lambda i: I["in_w"][layer, i + 18])
                with sp.Fori(0, HEADS) as hd:
                    for j in range(2):
                        load(Slot(layer, STAGE["heads"] + j, hd, 4), I["head_q"][layer, hd * 2 + j])
                    for j in range(2):
                        load(Slot(layer, STAGE["heads"] + 2 + j, hd, 4), I["head_kv"][layer, hd * 2 + j])
                with sp.Fori(0, KD // 2) as it:
                    for j in range(2):
                        load(Slot(layer, STAGE["branch_out"] + 2 * j, it, 4), I["conv_out"][layer, it * 2 + j])
                        load(Slot(layer, STAGE["branch_out"] + 2 * j + 1, it, 4), I["mla_out"][layer, it * 2 + j])
                sp.wait_ge(o_ready, HEADS * (layer + 1))
                sp.dma_start(work_t[:, 12 * S:14 * S].rearrange("p (t s) -> p t s", t=2), I["p_t"][layer]).then_inc(p_in, 16)
                loads(layer, "mix_out", KD, lambda i: I["mix_out"][layer, i])
                ffn(layer, 1)
                loads(layer, "ple_gate", KD, lambda i: I["ple_gate"][layer, i])
                loads(layer, "ple_proj", KD, lambda i: I["ple_proj"][layer, i])

            for j in range(RING):
                load(Slot(L2, j), I["in2"][j])
            sp.wait_ge(slot_read, Slot(L2, 0).done - 1)
            sp.wait_ge(ple_step, KD * DEPTH)
            sp.dma_start(gate_t[:, :], I["cmp_w1"]).then_inc(w1_in, 16)
            sp.dma_start(work_t[:, 0:2 * S], I["lru_w"]).then_inc(b2_in, 16)
            sp.wait_ge(sum_ready, 10 * KD)
            sp.dma_start(sq_t[:, 0:448], I["cmp_w2"]).then_inc(w2_in, 16)
            for j in range(4, IN2):
                load(Slot(L2, j), I["in2"][j])
            for m in range(KD):
                load(Slot(L2, B2_OUT + m), I["out2"][m])
            with sp.Fori(0, FF2_GROUPS) as g:
                for j in range(KD):
                    load(Slot(L2, B2_FF + j, g, 2 * KD), I["ff1"][g * KD + j])
                for m in range(KD):
                    load(Slot(L2, B2_FF + KD + m, g, 2 * KD), I["ff2"][g * KD + m])
            for m in range(KD):
                sp.wait_ge(h_out, m + 1)
                sp.dma_start(out_t[:, m, :], h(m)).then_inc(out_done, 16)
            sp.wait_ge(out_done, 16 * KD)

        @block.gpsimd
        def _(pool):
            pool.memset(ones[:, :], 1.0).then_inc(consts_ready, 1)
            pool.memset(ident[:, :], 0.0).then_inc(consts_ready, 1)
            pool.memset(fold[:, :], 0.0).then_inc(consts_ready, 1)
            pool.memset(cmask, 0.0).then_inc(consts_ready, 1)
            pool.memset(eps_t[:, :], EPS).then_inc(consts_ready, 1)
            pool.wait_ge(consts_ready, 5)
            pool.memset(cmask[0:64, 64:P], NEG).then_inc(consts_ready, 1)
            pool.affine_select(out=ident[:, :], in_=ident[:, :], compare_op=ALU.not_equal, fill=1.0, base=0,
                               pattern=[[-1, P]], channel_multiplier=1).then_inc(consts_ready, 1)
            for i, off in enumerate((0, 64, -64)):
                pool.affine_select(out=fold[:, :], in_=fold[:, :], compare_op=ALU.not_equal, fill=1.0, base=off,
                                   pattern=[[-1, P]], channel_multiplier=1).then_inc(consts_ready, 1)
                pool.wait_ge(consts_ready, 8 + i)
            pool.tensor_copy(ident_r[:, :], ident[:, :]).then_inc(consts_ready, 1)
            pool.tensor_copy(cmask_r[:, :], cmask).then_inc(consts_ready, 1)

            def squares(n, ready, x=h):
                for m in range(KD):
                    ready(m)
                    if m == 0:
                        if not isinstance(n, int) or n:
                            pool.wait_ge(rs_ready, n)
                        pool.tensor_tensor(acc, x(0), x(0), ALU.mult).then_inc(sum_ready, 1)
                        continue
                    pool.wait_ge(sum_ready, n * KD + m)
                    pool.tensor_tensor(sq, x(m), x(m), ALU.mult).then_inc(sq_ready, 1)
                    pool.wait_ge(sq_ready, n * (KD - 1) + m)
                    pool.tensor_tensor(acc, acc, sq, ALU.add).then_inc(sum_ready, 1)

            squares(0, lambda m: pool.wait_ge(x_in, 32))
            with pool.Fori(0, DEPTH) as layer:
                for e, name in enumerate(("ffn1_down2", "mix_out", "ffn2_down2", "ple_proj")):
                    squares(norm_no(layer, e),
                            (lambda m: pool.wait_ge(ple_step, KD * layer + m + 1)) if e == 3 else
                            (lambda m: pool.wait_ge(slot_read, Slot(layer, STAGE[name] + m).done)))

            squares(9, lambda m: pool.wait_ge(hf_ready, m + 1))
            pool.wait_ge(rg_tanh, 8)
            pool.iota(work(1), [[-1, S]], base=S - P, channel_multiplier=1, allow_small_or_imprecise_dtypes=True)\
                .then_inc(bias_step, 1)
            pool.iota(work(0)[:, 0:QT * N_CMP], [[P, QT], [-16, N_CMP]], base=-31, channel_multiplier=1,
                      allow_small_or_imprecise_dtypes=True).then_inc(bias_step, 1)
            pool.wait_ge(bias_step, 2)
            pool.wait_ge(slot_done, Slot(L2, IN2 - 1).done)
            for n in range(HEADS):
                pool.tensor_scalar(ux(n), work(1), -SLOPES[n], None, ALU.mult).then_inc(bias_step, 1)
            for n in range(HEADS):
                bc = bias_c[:, n * QT * N_CMP:(n + 1) * QT * N_CMP]
                pool.tensor_scalar(bc, work(0)[:, 0:QT * N_CMP], -SLOPES[n], None, ALU.mult).then_inc(bias_step, 1)
            pool.wait_ge(bias_step, 2 + 2 * HEADS)
            for n in range(HEADS):
                pool.affine_select(out=u_hi(n), in_=ux(n), compare_op=ALU.is_ge, fill=NEG, base=S - P,
                                   pattern=[[-1, S]], channel_multiplier=1).then_inc(bias_ready, 1)
                bc = bias_c[:, n * QT * N_CMP:(n + 1) * QT * N_CMP]
                pool.affine_select(out=bc, in_=bc, compare_op=ALU.is_ge, fill=NEG, base=-31,
                                   pattern=[[P, QT], [-16, N_CMP]], channel_multiplier=1).then_inc(bias_ready, 1)
            pool.wait_ge(g_cols, 1)
            pool.affine_select(out=gcols[:, 0:HEADS], in_=gcols[:, 0:HEADS], compare_op=ALU.is_ge, fill=0.0, base=-31,
                               pattern=[[0, HEADS]], channel_multiplier=1).then_inc(g_ready, 1)
            squares(10, lambda m: pool.wait_ge(slot_read, Slot(L2, B2_OUT + m).done), gate)
            squares(11, lambda m: pool.wait_ge(h2_ready, m + 1))
            for m in range(KD):
                pool.memset(gate(m), 0.0).then_inc(y_zero, 1)
            squares(12, lambda m: pool.wait_ge(slot_read, Slot(L2, B2_SLOTS - KD + m).done), gate)

        @block.scalar
        def _(act):
            def split_hi(slot):
                act.wait_ge(raw_in[slot.pos], slot.loads)
                act.wait_ge(slot_done, slot.free)
                act.activation(wt(w_hi, slot, slot.tiles), wt(raw, slot, slot.tiles), ACT.Copy)\
                   .then_inc(w_hi_ready, slot.inc)

            def prep_hi(n, m, gain, slot):
                if slot is not None:
                    act.wait_ge(slot_read, slot.done)
                act.activation(u_hi(m), h(m), ACT.Copy, scale=gain[:, m:m + 1]).then_inc(u_hi_ready, 1)

            def rms(n, src=ot, width=D):
                act.wait_ge(stat_done, n + 1)
                act.activation(acc, src[:, :], ACT.Sqrt, scale=1.0 / width, bias=eps_t[:, 0:1]).then_inc(rms_ready, 1)

            act.wait_ge(pos_ready, 1)
            act.activation(cs, work(0), ACT.Sin).then_inc(sin_ready, 1)
            act.wait_ge(const_in, 64)
            act.activation(c_t[:, KD:2 * KD], c_t[:, 0:KD], ACT.Tanh, scale=0.5).then_inc(c_tanh, 1)
            act.wait_ge(pos_ready, 2)
            act.activation(small2[:, 8:12], small2[:, 8:12], ACT.Exp, scale=-1.0).then_inc(lam_exp, 1)
            act.wait_ge(x_in, 32)
            for m in range(KD):
                prep_hi(0, m, vec0, None)
            for j in range(AHEAD):
                split_hi(Slot(0, j))

            def ffn(layer, f, e):
                name = f"ffn{f + 1}"
                no = layer * 2 + f
                for g, ft in enumerate(FF_GROUPS):
                    s0 = STAGE[f"{name}_up{g}"]
                    f0 = sum(FF_GROUPS[:g])
                    if g == 0:
                        rms(norm_no(layer, e) - 1)

                    def up(it):
                        for q in range(2):
                            i = no * FF_TILES + f0 + 2 * it + q + 1
                            split_hi(Slot(layer, s0 + 2 * q + AHEAD, it, RING))
                            gated = Slot(layer, s0 + 2 * q, it, RING)
                            act.wait_ge(slot_read, gated.done)
                            act.activation(work(2 + q), work(q), ACT.Tanh, scale=0.5).then_inc(tanh_ready, 1)
                            split_hi(Slot(layer, s0 + 2 * q + 1 + AHEAD, it, RING))
                            act.wait_ge(act_ready, i)
                            act.activation(a_hi_t[:, bass.ds((2 * it + q) * S, S)], work(8 + q), ACT.Copy)\
                               .then_inc(a_hi_ready, 1)
                    repeat(act, s0, ft // 2, RING, up)
                    s0 = STAGE[f"{name}_down{g}"]
                    if g < 2:
                        def down(it):
                            for j in range(RING):
                                split_hi(Slot(layer, s0 + j + AHEAD, it, RING))
                        repeat(act, s0, KD // RING, RING, down)
                        continue
                    act.wait_ge(vec_in, 16 * (layer + 1))
                    for m in range(KD):
                        split_hi(Slot(layer, s0 + m + AHEAD))
                        prep_hi(norm_no(layer, e), m, vec[:, (V_MIX if f == 0 else V_PLE):], Slot(layer, s0 + m))

            def core(layer, hd, q, slots):
                n = layer * HEADS + hd
                for qt in range(QT):
                    if qt >= 2:
                        copy_pt(n, qt - 2)
                    act.wait_ge(nmax_ready, n * QT + qt + 1)
                    act.activation(work_t[:, (9 + qt % 2) * S:(9 + qt % 2) * S + (qt + 1) * P], sc[:, qt % 2, 0:(qt + 1) * P],
                                   ACT.Exp, bias=stat_t[:, 8 + qt:9 + qt], scale=SCALE1,
                                   accum_out=stat_t[:, 16 + qt:17 + qt]).then_inc(exp_ready, 1)
                    if qt >= 1 and slots:
                        split_hi(slots[qt - 1])
                if slots:
                    split_hi(slots[3])
                copy_pt(n, 2)
                copy_pt(n, 3)
                act.wait_ge(o_done, n + 1)
                act.activation(u_hi_t[:, bass.ds(hd * S, S)], ot[:, :], ACT.Copy).then_inc(o_hi_ready, 1)

            def copy_pt(n, qt):
                act.wait_ge(t_done, n * QT + qt + 1)
                dst = work_t[:, 11 * S:15 * S].rearrange("p (k s) -> p k s", s=S)[:, 0:qt + 1, qt * P:(qt + 1) * P]
                act.activation(dst, tr[:, 0:(qt + 1) * P].rearrange("p (k s) -> p k s", s=P), ACT.Copy)\
                   .then_inc(pt_ready, 1)

            with act.Fori(0, DEPTH) as layer:
                ffn(layer, 0, 0)
                rms(norm_no(layer, 0))
                s0 = STAGE["lora"]
                for j in range(6):
                    split_hi(Slot(layer, s0 + j + AHEAD))
                    if j < 5:
                        act.wait_ge(slot_read, Slot(layer, s0 + j).done)
                        act.activation(work(8 if j == 4 else 11 + j), work(j), ACT.Square).then_inc(lora_sq, 1)
                s0 = STAGE["conv"]
                for j in range(12):
                    split_hi(Slot(layer, s0 + j + AHEAD))
                    if j == 0:
                        act.wait_ge(lora_stat, 2 * layer + 1)
                        act.activation(work(11), ot[:, :], ACT.Sqrt, scale=1.0 / Q_LORA, bias=eps_t[:, 0:1])\
                           .then_inc(lora_rms, 1)
                        act.wait_ge(lora_stat, 2 * layer + 2)
                        act.activation(work(13), tr[:, :], ACT.Sqrt, scale=1.0 / KV_LORA, bias=eps_t[:, 0:1])\
                           .then_inc(lora_rms, 1)
                    if j >= 3 and j < 8:
                        act.wait_ge(lora_norm, 5 * layer + j - 2)
                        act.activation(a_hi(j - 3), work(j - 3), ACT.Copy).then_inc(lora_hi, 1)
                    if j % 3 == 2:
                        act.wait_ge(conv_y, 4 * layer + j // 3 + 1)
                        act.activation(a_hi(5 + j // 3), work(7), ACT.Copy).then_inc(conv_hi, 1)
                s0 = STAGE["gates"]

                def gates(it):
                    for j in range(RING):
                        split_hi(Slot(layer, s0 + j + AHEAD, it, RING))
                        act.wait_ge(slot_read, Slot(layer, s0 + j, it, RING).done)
                        act.activation(gate_t[:, bass.ds((it * RING + j) * S, S)], work(13 + j % 2), ACT.Tanh,
                                       scale=0.5).then_inc(gate_tanh, 1)
                repeat(act, s0, 4, RING, gates)
                s0 = STAGE["heads"]
                for j in range(4):
                    split_hi(Slot(layer, s0 + j + AHEAD))

                def heads(it):
                    for q in range(2):
                        last = isinstance(it, int) and q == 1
                        slots = [Slot(layer, s0 + 4 * (q + 1) + j + AHEAD + (24 if isinstance(it, int) else 0),
                                      0 if isinstance(it, int) else it, 8) for j in range(4)]
                        core(layer, 2 * it + q, q, None if last else slots)
                with act.Fori(0, HEADS // 2 - 1) as it:
                    heads(it)
                heads(HEADS // 2 - 1)
                s0 = STAGE["branch_out"]
                for m in range(KD):
                    split_hi(Slot(layer, s0 + 2 * m + AHEAD))
                    split_hi(Slot(layer, s0 + 2 * m + 1 + AHEAD))
                    act.wait_ge(mg_ready, KD * layer + m + 1)
                    act.activation(merged_hi(m), work(4 + m % 2), ACT.Copy).then_inc(mg_hi, 1)
                s0 = STAGE["mix_out"]
                for m in range(KD):
                    split_hi(Slot(layer, s0 + m + AHEAD))
                    prep_hi(norm_no(layer, 1), m, vec[:, V_FFN2:], Slot(layer, s0 + m))
                ffn(layer, 1, 2)
                rms(norm_no(layer, 2))
                act.wait_ge(p_in, 16 * (layer + 1))
                act.wait_ge(slot_read, Slot(layer, STAGE["ple_gate"]).done - 1)
                act.activation(a_hi_t[:, 0:2 * S], work_t[:, 12 * S:14 * S], ACT.Copy).then_inc(p_hi_ready, 1)
                s0 = STAGE["ple_gate"]
                for m in range(KD):
                    split_hi(Slot(layer, s0 + m + AHEAD))
                    act.wait_ge(slot_read, Slot(layer, s0 + m).done)
                    act.activation(gate(m), work(m % 2), ACT.Tanh, scale=0.5).then_inc(ple_tanh, 1)
                s0 = STAGE["ple_proj"]
                for m in range(KD):
                    split_hi(Slot(layer, s0 + m + AHEAD))
                    act.wait_ge(ple_step, KD * layer + m + 1)
                    act.activation(u_hi(m), h(m), ACT.Copy, scale=vec[:, V_NEXT + m:V_NEXT + m + 1])\
                       .then_inc(u_hi_ready, 1)

            def ahead(s):
                if s + AHEAD < B2_SLOTS:
                    split_hi(Slot(L2, s + AHEAD))

            def shifted(n, sh):
                for m in range(KD):
                    act.wait_ge(tmp_ready, KD * (n == 11) + m + 1)
                    act.activation(u_hi(m), work(2 + m), ACT.Identity, bias=mod_t[:, sh + m:sh + m + 1]).then_inc(u_hi_ready, 1)

            rms(8)
            rms(9)
            shifted(9, 0)
            for s in range(IN2):
                ahead(s)
                if 5 <= s <= 8:
                    j = s - 5
                    act.wait_ge(mods_ready, 1)
                    act.wait_ge(rg_done, j + 1)
                    act.activation(work(6 + j), sc[:, 0, :], ACT.Tanh, scale=0.5, bias=small2[:, 20 + j:21 + j]).then_inc(rg_tanh, 1)
                    act.activation(work(10 + j), sc[:, 1, :], ACT.Tanh, scale=0.5, bias=small2[:, 24 + j:25 + j]).then_inc(rg_tanh, 1)
                if 7 <= s <= 10:
                    j = s - 7
                    act.wait_ge(la_ready, j + 1)
                    if j >= 2:
                        act.wait_ge(v2_ready, j - 1)
                    act.activation(work(14 + j % 2), work(6 + j), ACT.Exp, scale=2.0).then_inc(decay_ready, 1)
                    act.activation(xr(j), work(6 + j), ACT.Exp).then_inc(decay_ready, 1)
                    act.wait_ge(decay_ready, 3 * j + 2)
                    act.activation(work(6 + j), work(6 + j), ACT.Tanh, scale=-1.0).then_inc(decay_ready, 1)
                if s == 12:
                    for j in range(4):
                        act.wait_ge(v2_ready, j + 1)
                        act.activation(work(6 + j), work(6 + j), ACT.Sqrt).then_inc(sqrt_ready, 1)
                if s == 15:
                    act.wait_ge(slot_read, Slot(L2, 14).done)
                    act.activation(gT, gT, ACT.Tanh, scale=0.5).then_inc(g_tanh, 1)
            act.wait_ge(ix_ready, 4)
            for j in range(4):
                act.wait_ge(slot_read, Slot(L2, 15 + j).done)
                act.activation(work(2 + j), gr(j), ACT.Square).then_inc(gel_sq, 1)
            for j in range(4):
                act.wait_ge(gel_in, j + 1)
                act.activation(work(2 + j), work(2 + j), ACT.Tanh, scale=0.7978845608028654).then_inc(gel_tanh, 1)
            act.wait_ge(hid_in, 1)
            act.activation(acc_t[:, 248:496], acc_t[:, 248:496], ACT.Tanh, scale=0.7978845608028654).then_inc(hid_tanh, 1)

            def copy_pt2(n, qt):
                for br, bank in enumerate((tr[:, :], proj[:, 3, :])):
                    act.wait_ge(t2_done, 2 * (n * QT + qt) + br + 1)
                    dst = work_t[:, (4 + 4 * br) * S:(8 + 4 * br) * S].rearrange("p (k s) -> p k s", s=S)[:, 0:qt + 1, qt * P:(qt + 1) * P]
                    act.activation(dst, bank[:, 0:(qt + 1) * P].rearrange("p (k s) -> p k s", s=P), ACT.Copy).then_inc(pt2_ready, 1)

            with act.Fori(0, QT) as j:
                for par in range(2):
                    n = 2 * j + par
                    act.wait_ge(cs_sub, n + 1)
                    act.activation(p_c, p_c, ACT.Exp).then_inc(cs_exp, 1)
                    for qt in range(QT):
                        if qt >= 2:
                            copy_pt2(n, qt - 2)
                        act.wait_ge(nmax2, n * QT + qt + 1)
                        for br in range(2):
                            w = (qt + 1) * P
                            act.activation(work(2 * br + qt % 2)[:, 0:w], (sc, proj)[br][:, qt % 2, 0:w], ACT.Exp, bias=stat_t[:, 8 + 2 * (qt % 2) + br:9 + 2 * (qt % 2) + br],
                                           accum_out=stat_t[:, 12 + 2 * (qt % 2) + br:13 + 2 * (qt % 2) + br]).then_inc(exp2, 1)
                    copy_pt2(n, 2)
                    copy_pt2(n, 3)
                    act.wait_ge(tc_done, n + 1)
                    act.activation(pt_c[0:N_CMP, :], proj[0:N_CMP, 2, :], ACT.Copy).then_inc(ptc_ready, 1)
            for k in range(KD):
                if k == 4:
                    act.wait_ge(o2_ready, HEADS)
                act.wait_ge(rnn_ready, 4)
                if k == 0:
                    act.wait_ge(o2_done, HEADS)
                act.activation(work(k), gr(k) if k < 4 else work(8 + k), ACT.Square).then_inc(mix_sq, 1)
            for i in range(2):
                act.wait_ge(mix_stat, i + 1)
                act.activation(work(8 + i), sc[:, i, :], ACT.Sqrt, scale=1.0 / 512, bias=eps_t[:, 0:1]).then_inc(mix_rms, 1)
            for k in range(KD):
                act.wait_ge(mix_norm, k + 1)
                act.activation(u_hi(k), gr(k) if k < 4 else work(8 + k), ACT.Copy).then_inc(u_hi_ready, 1)
            for m in range(KD):
                ahead(B2_OUT + m)
            rms(10)
            rms(11)
            shifted(11, 24)

            def ff(g):
                end = isinstance(g, int)
                for i in range(2 * KD):
                    if not (end and i >= 2 * KD - AHEAD):
                        split_hi(Slot(L2, B2_FF + i + AHEAD, g, 2 * KD))
                    if i < KD:
                        act.wait_ge(slot_read, Slot(L2, B2_FF + i, g, 2 * KD).done)
                        act.activation(work(4 + i % 4), work(i % 4), ACT.Square).then_inc(relu_sq, 1)
                        act.wait_ge(relu_sq, KD * g + i + 1)
                        act.activation(a_hi(i), work(4 + i % 4), ACT.Copy).then_inc(a_hi_ready, 1)
            with act.Fori(0, FF2_GROUPS - 1) as g:
                ff(g)
            ff(FF2_GROUPS - 1)
            rms(12)

        @block.tensor
        def _(pe):
            def three(out, w_h, w_l, x_h, x_l, first, last):
                pe.matmul(out, w_h, x_h, start=first, stop=False)
                pe.matmul(out, w_h, x_l, start=False, stop=False)
                return pe.matmul(out, w_l, x_h, start=False, stop=last)

            def slot_mm(slot, operand, before=None):
                pe.wait_ge(w_lo_ready, slot.done)
                pe.wait_ge(slot_read, slot.free)
                for k in range(slot.tiles):
                    if before:
                        before(k)
                    x_h, x_l = operand(k)
                    mm = three(proj[:, slot.pos, :], wt(w_hi, slot, 1, k), wt(w_lo, slot, 1, k), x_h, x_l,
                               k == 0, k == slot.tiles - 1)
                mm.then_inc(slot_done, slot.inc)

            u_of = lambda k: (u_hi(k), u_lo(k))
            a_of = lambda k: (a_hi(k), a_lo(k))

            def stat(n):
                pe.wait_ge(sum_ready, (n + 1) * KD)
                pe.matmul(ot[:, :], ones[:, :], acc, start=True, stop=True).then_inc(stat_done, 1)

            def first_u(n, slot):
                slot_mm(slot, u_of, lambda k: pe.wait_ge(u_ready, n * KD + k + 1))
                stat(n)

            pe.wait_ge(consts_ready, 12)

            def ffn(layer, f, e):
                name = f"ffn{f + 1}"
                no = layer * 2 + f
                for g, ft in enumerate(FF_GROUPS):
                    s0 = STAGE[f"{name}_up{g}"]
                    if g == 0:
                        first_u(norm_no(layer, e) - 1, Slot(layer, s0))
                        for j in range(1, RING):
                            slot_mm(Slot(layer, s0 + j), u_of)
                        s0 += RING
                    with pe.Fori(0, ft // 2 - (g == 0)) as it:
                        for j in range(RING):
                            slot_mm(Slot(layer, s0 + j, it, RING), u_of)
                    if g < 2:
                        b = no * 2 + g
                        pe.wait_ge(ada_in, 16 * (b + 1))
                        if g == 0:
                            pe.wait_ge(c_tanh, 2)
                        for j in range(ADA_BATCH):
                            for k in range(KD):
                                mm = pe.matmul(tr[:, j:j + 1], gate_t[:, (j * KD + k) * P:(j * KD + k + 1) * P],
                                               c_t[:, KD + k:KD + k + 1], start=k == 0, stop=k == KD - 1)
                        mm.then_inc(ada_done, 1)
                    s0 = STAGE[f"{name}_down{g}"]
                    f_done = no * FF_TILES + sum(FF_GROUPS[:g + 1])
                    with pe.Fori(0, KD // RING) as it:
                        pe.wait_ge(a_lo_ready, f_done)
                        for j in range(RING):
                            slot_mm(Slot(layer, s0 + j, it, RING), a_of)

            def scores(n, q, qt):
                w = (qt + 1) * P
                pe.wait_ge(p_ready, n * QT + qt + 1)
                pe.matmul(sc[:, qt % 2, 0:w], work(q)[:, qt * P:w], work(4 + q)[:, 0:w], start=True, stop=False)
                pe.matmul(sc[:, qt % 2, qt * P:w], ident_r[:, :], cmask_r[:, :], start=False, stop=False)
                pe.matmul(sc[:, qt % 2, 0:w], work(2 + q)[:, qt * P:w], work(15)[:, 0:w], start=False, stop=True)\
                  .then_inc(s_done, 1)

            def turn(n, qt):
                pe.wait_ge(p_ready, 2 + n * QT + qt + 1)
                if qt == 0:
                    pe.wait_ge(v_ready, n + 1)
                else:
                    pe.wait_ge(pt_ready, n * QT + qt)
                for k in range(qt + 1):
                    mm = pe.transpose(tr[:, k * P:(k + 1) * P], work(9 + qt % 2)[:, k * P:(k + 1) * P], ident[:, :])
                mm.then_inc(t_done, 1)

            def core(layer, hd, q, slots):
                n = layer * HEADS + hd
                run = [lambda s=s, j=j: slot_mm(s, (lambda k: (a_hi(k), a_lo(k))) if j < 2 else
                                                (lambda k: (a_hi(3 + k), a_lo(3 + k))))
                       for j, s in enumerate(slots)] if slots else [lambda: None] * 4
                first = Slot(layer, STAGE["heads"]).number + RING + 4 * (hd + 1)
                pe.wait_ge(slot_read, first)
                pe.wait_ge(pt_ready, n * QT)
                for t in range(QT):
                    mm = pe.transpose(tr[:, t * P:(t + 1) * P], work(6)[:, t * P:(t + 1) * P], ident[:, :])
                mm.then_inc(v_turned, 1)
                scores(n, q, 0)
                scores(n, q, 1)
                run[0]()
                turn(n, 0)
                scores(n, q, 2)
                run[1]()
                turn(n, 1)
                scores(n, q, 3)
                run[2]()
                turn(n, 2)
                run[3]()
                turn(n, 3)
                pe.wait_ge(pt_ready, n * QT + QT)
                pe.wait_ge(o_ready, n)
                for k in range(QT):
                    mm = pe.matmul(ot[:, k * P:S], work(7 + q)[:, k * P:(k + 1) * P], work(11 + k)[:, k * P:S],
                                   start=k == 0, stop=True, skip_group_check=True)
                mm.then_inc(o_done, 1)

            with pe.Fori(0, DEPTH) as layer:
                ffn(layer, 0, 0)
                s0 = STAGE["lora"]
                first_u(norm_no(layer, 0), Slot(layer, s0))
                for j in range(1, 6):
                    slot_mm(Slot(layer, s0 + j), u_of)
                pe.wait_ge(rms_ready, norm_no(layer, 0) + 1)
                for j in range(5):
                    pe.wait_ge(lora_sq, 5 * layer + j + 1)
                    bank = ot if j < 3 else tr
                    mm = pe.matmul(bank[:, :], ones[:, :], work(8 if j == 4 else 11 + j), start=j in (0, 3), stop=j in (2, 4))
                    if j in (2, 4):
                        mm.then_inc(lora_stat, 1)
                s0 = STAGE["conv"]
                for j in range(12):
                    slot_mm(Slot(layer, s0 + j), u_of)
                    if j == 0:
                        pe.wait_ge(kr_rope, layer + 1)
                        pe.matmul(sc[:, 0, :], fold[:, :], work(5), start=True, stop=True).then_inc(kr_fold, 1)
                s0 = STAGE["gates"]
                with pe.Fori(0, 4) as it:
                    for j in range(RING):
                        slot_mm(Slot(layer, s0 + j, it, RING), u_of)
                s0 = STAGE["heads"]
                pe.wait_ge(lora_ready, 5 * (layer + 1))
                pe.wait_ge(kr_ready, layer + 1)
                for j in range(4):
                    slot_mm(Slot(layer, s0 + j), lambda k, o=0 if j < 2 else 3: (a_hi(o + k), a_lo(o + k)))
                with pe.Fori(0, HEADS // 2 - 1) as it:
                    for q in range(2):
                        core(layer, 2 * it + q, q, [Slot(layer, s0 + 4 * (q + 1) + j, it, 8) for j in range(4)])
                core(layer, HEADS - 2, 0, [Slot(layer, s0 + 28 + j) for j in range(4)])
                core(layer, HEADS - 1, 1, None)
                s0 = STAGE["branch_out"]
                pe.wait_ge(conv_ready, 4 * (layer + 1))
                slot_mm(Slot(layer, s0), lambda k: (a_hi(5 + k), a_lo(5 + k)))
                pe.wait_ge(o_ready, HEADS * (layer + 1))
                for m in range(KD):
                    if m:
                        slot_mm(Slot(layer, s0 + 2 * m), lambda k: (a_hi(5 + k), a_lo(5 + k)))
                    slot_mm(Slot(layer, s0 + 2 * m + 1), u_of)
                s0 = STAGE["mix_out"]
                slot_mm(Slot(layer, s0), lambda k: (merged_hi(k), merged_lo(k)),
                        lambda k: pe.wait_ge(merged_ready, KD * layer + k + 1))
                for m in range(1, KD):
                    slot_mm(Slot(layer, s0 + m), lambda k: (merged_hi(k), merged_lo(k)))
                ffn(layer, 1, 2)
                s0 = STAGE["ple_gate"]
                first_u(norm_no(layer, 2), Slot(layer, s0))
                for m in range(1, KD):
                    slot_mm(Slot(layer, s0 + m), u_of)
                s0 = STAGE["ple_proj"]
                pe.wait_ge(p_split, layer + 1)
                for m in range(KD):
                    slot_mm(Slot(layer, s0 + m), a_of)

            stat(8)
            stat(9)
            for s in range(IN2):
                slot_mm(Slot(L2, s), u_of, (lambda k: pe.wait_ge(u_ready, 9 * KD + k + 1)) if s == 0 else None)
                if 5 <= s <= 8:
                    j = s - 5
                    pe.wait_ge(b2_in, 16)
                    pe.wait_ge(xf_ready, j + 1)
                    if j:
                        pe.wait_ge(rg_tanh, 2 * j)
                    pe.matmul(sc[:, 0, :], work_t[:, j * P:(j + 1) * P], work(2 + j), start=True, stop=True)
                    pe.matmul(sc[:, 1, :], work_t[:, (4 + j) * P:(5 + j) * P], work(2 + j), start=True, stop=True)\
                      .then_inc(rg_done, 1)
                if s == 16:
                    pe.wait_ge(g_tanh, 1)
                    for t in range(QT):
                        mm = pe.transpose(tr[:, t * P:(t + 1) * P], gT[:, t * P:(t + 1) * P], ident[:, :])
                    mm.then_inc(g_turned, 1)
            pe.wait_ge(slot_read, Slot(L2, IN2 - 1).done)
            for i, v in enumerate((VS, VW)):
                for t in range(QT):
                    mm = pe.transpose(proj[:, i, t * P:(t + 1) * P], v[:, t * P:(t + 1) * P], ident[:, :])
                mm.then_inc(v2_turned, 1)
            pe.wait_ge(w1_in, 16)
            pe.wait_ge(x_built, 8)
            for kv in range(2):
                for m in range(2):
                    for kt in range(CMP_K):
                        mm = pe.matmul(ot[:, (2 * kv + m) * 64:(2 * kv + m) * 64 + 62], w1(kv, kt, m),
                                       X(kv)[:, kt * 62:(kt + 1) * 62], start=kt == 0, stop=kt == CMP_K - 1)
            mm.then_inc(hid_done, 1)
            pe.wait_ge(hid_ready, 1)
            for m in range(2):
                pe.matmul(sc[:, 0, 0:62], w2k(m), hid(0, m), start=m == 0, stop=m == 1)
            for g in range(2):
                for m in range(2):
                    mm = pe.matmul(sc[0:N_CMP, 1, g * 64:(g + 1) * 64], hid(1, m)[:, g * N_CMP:(g + 1) * N_CMP], w2v(m),
                                   start=m == 0, stop=m == 1)
            mm.then_inc(kv_cmp_done, 1)
            pe.wait_ge(kv_cmp_ready, 3)
            pe.wait_ge(v2_copied, 2)

            def scores2(n, j, par, rows, qt):
                w = (qt + 1) * P
                for br, (k, bank) in enumerate(((KS, sc), (KW, proj))):
                    pe.wait_ge(exp2, 2 * (n * QT + qt) + br + 1)
                    pe.matmul(bank[:, qt % 2, 0:w], ident_r[:, :], u_hi_t[:, bass.ds((4 * par + j) * S + S - w, w)],
                              start=True, stop=False)
                    pe.matmul(bank[:, qt % 2, 0:w], qbuf[rows, qt * P:w], k[rows, 0:w], start=False, stop=True)\
                      .then_inc(s2_done, 1)

            def turn2(n, qt):
                for br, bank in enumerate((tr[:, :], proj[:, 3, :])):
                    pe.wait_ge(p2_ready, 2 * (n * QT + qt) + br + 1)
                    pe.wait_ge(pt2_ready, 2 * (n * QT + qt) + br + 1)
                    for k in range(qt + 1):
                        mm = pe.transpose(bank[:, k * P:(k + 1) * P], work(2 * br + qt % 2)[:, k * P:(k + 1) * P], ident[:, :])
                    mm.then_inc(t2_done, 1)

            pe.wait_ge(bias_ready, 2 * HEADS)
            with pe.Fori(0, QT) as j:
                pe.wait_ge(q_ready, j + 1)
                for par in range(2):
                    n = 2 * j + par
                    rows = slice(64 * par, 64 * par + 64)
                    for t in range(QT):
                        mm = pe.matmul(proj[:, 2, t * N_CMP:(t + 1) * N_CMP], qbuf[rows, t * P:(t + 1) * P], kcmp[rows, :],
                                       start=True, stop=True)
                    mm.then_inc(cs_done, 1)
                    scores2(n, j, par, rows, 0)
                    scores2(n, j, par, rows, 1)
                    turn2(n, 0)
                    scores2(n, j, par, rows, 2)
                    turn2(n, 1)
                    scores2(n, j, par, rows, 3)
                    pe.wait_ge(pc_ready, n + 1)
                    for t in range(QT):
                        mm = pe.transpose(proj[0:N_CMP, 2, t * P:(t + 1) * P], p_c[:, t * N_CMP:(t + 1) * N_CMP], ident[:, :])
                    mm.then_inc(tc_done, 1)
                    turn2(n, 2)
                    turn2(n, 3)
                    pe.wait_ge(ptc_ready, n + 1)
                    pe.wait_ge(pt2_ready, 2 * (n + 1) * QT + 2)
                    pe.wait_ge(o2_ready, n)
                    out = ot[rows, :]
                    pe.matmul(out, vcmp[:, rows], pt_c[0:N_CMP, :], start=True, stop=True)
                    for br, vn in enumerate((vn_s, vn_w)):
                        for k in range(QT):
                            mm = pe.matmul(ot[rows, k * P:S], vn[:, k * P + 64 * par:k * P + 64 * par + 64],
                                           work(4 + 4 * br + k)[:, k * P:S], start=False, stop=True,
                                           skip_group_check=True)
                    mm.then_inc(o2_done, 1)
            for k in range(KD):
                pe.wait_ge(mix_sq, k + 1)
                mm = pe.matmul(sc[:, k // 4, :], ones[:, :], work(k), start=k % 4 == 0, stop=k % 4 == 3)
                if k % 4 == 3:
                    mm.then_inc(mix_stat, 1)
            for m in range(KD):
                slot_mm(Slot(L2, B2_OUT + m), u_of, (lambda k: pe.wait_ge(u_ready, 10 * KD + k + 1)) if m == 0 else None)
            stat(10)
            stat(11)
            pe.wait_ge(u_ready, 12 * KD)
            with pe.Fori(0, FF2_GROUPS) as g:
                for j in range(KD):
                    slot_mm(Slot(L2, B2_FF + j, g, 2 * KD), u_of)
                first = FF_TILES * 2 * DEPTH + 1
                for m in range(KD):
                    slot_mm(Slot(L2, B2_FF + KD + m, g, 2 * KD), a_of,
                            (lambda k: pe.wait_ge(a_lo_ready, KD * g + first + k)) if m == 0 else None)
            stat(12)

        @block.vector
        def _(dve):
            steps = [0]

            def link(ins):
                steps[0] += 1
                ins.then_inc(start_step, 1)
                dve.wait_ge(start_step, steps[0])

            def split_lo(slot):
                dve.wait_ge(w_hi_ready, slot.number + slot.inc)
                dve.tensor_tensor(wt(w_lo, slot, slot.tiles), wt(raw, slot, slot.tiles),
                                  wt(w_hi, slot, slot.tiles).bitcast(F32), ALU.subtract).then_inc(w_lo_ready, slot.inc)

            def prep_lo(n, m, gain):
                dve.wait_ge(u_hi_ready, KD * n + m + 1)
                dve.scalar_tensor_tensor(u_lo(m), h(m), gain[:, m:m + 1], u_hi(m).bitcast(F32), ALU.mult,
                                         ALU.subtract).then_inc(u_ready, 1)

            def inv_rms(n):
                dve.wait_ge(rms_ready, n + 1)
                dve.reciprocal(rs, acc).then_inc(rs_ready, 1)

            def normed(slot, dst, n):
                dve.wait_ge(rs_ready, n + 1)
                dve.wait_ge(slot_done, slot.done)
                return dve.tensor_tensor(dst, proj[:, slot.pos, :], rs, ALU.mult)

            dve.memset(stat_t[:, 64:65], 0.0).then_inc(w_lo_ready, RING)
            dve.memset(stat_t[:, 65:66], 0.0).then_inc(slot_done, RING)
            dve.memset(stat_t[:, 66:67], 0.0).then_inc(slot_read, RING)
            dve.memset(stat_t[:, 67:68], 0.0).then_inc(p_ready, 2)
            dve.memset(stat_t[:, 68:69], 0.0).then_inc(gate_tanh, 2)
            dve.memset(stat_t[:, 69:70], 0.0).then_inc(exp2, 4)
            dve.memset(stat_t[:, 70:71], 0.0).then_inc(pt2_ready, 2)
            dve.wait_ge(const_in, 64)
            wa, wb = work(0), work(1)
            link(dve.tensor_copy(wb, wa.bitcast(I32)))
            link(dve.tensor_scalar(wa, wb, stat_t[:, 0:1], None, ALU.mult))
            link(dve.tensor_scalar(wb, wa, 1.0 / TWO_PI, ROUND, ALU.mult, ALU.add))
            link(dve.tensor_scalar(wb, wb, -ROUND, None, ALU.add))
            for part in (PI_A, PI_B, PI_C):
                link(dve.scalar_tensor_tensor(wa, wb, -part, wa, ALU.mult, ALU.add))
            link(dve.tensor_scalar(wa, wa, stat_t[:, 1:2], None, ALU.add))
            link(dve.tensor_scalar(wb, wa, TWO_PI / 2, -TWO_PI, ALU.is_gt, ALU.mult))
            link(dve.tensor_tensor(wa, wa, wb, ALU.add))
            dve.tensor_scalar(wa, wa, float(np.float32(3.1415925)), -float(np.float32(3.1415925)), ALU.min, ALU.max)\
               .then_inc(pos_ready, 1)
            lam = col2[:, C_LAM:C_LAM + 4]
            top, z, zz = (small2[:, 4 * i:4 * i + 4] for i in range(1, 4))
            link(dve.tensor_scalar(top, lam, -1.0, None, ALU.mult))
            link(dve.tensor_tensor(z, lam, top, ALU.max))
            dve.tensor_scalar(top, top, 0.0, None, ALU.max).then_inc(pos_ready, 1)
            dve.wait_ge(c_tanh, 1)
            link(dve.scalar_tensor_tensor(c_t[:, KD:2 * KD], c_t[:, KD:2 * KD], 1.0, c_t[:, 0:KD], ALU.add, ALU.mult))
            dve.tensor_scalar(c_t[:, KD:2 * KD], c_t[:, KD:2 * KD], 0.5, None, ALU.mult).then_inc(c_tanh, 1)
            dve.wait_ge(lam_exp, 1)
            link(dve.tensor_scalar(zz, z, 2.0, None, ALU.add))
            link(dve.reciprocal(zz, zz))
            link(dve.tensor_tensor(z, z, zz, ALU.mult))
            link(dve.tensor_tensor(zz, z, z, ALU.mult))
            poly = small2[:, 16:20]
            link(dve.tensor_scalar(poly, zz, 1.0 / 15, 1.0 / 13, ALU.mult, ALU.add))
            for d in (11, 9, 7, 5, 3, 1):
                link(dve.tensor_tensor(poly, poly, zz, ALU.mult))
                link(dve.tensor_scalar(poly, poly, 1.0 / d, None, ALU.add))
            link(dve.tensor_tensor(poly, poly, z, ALU.mult))
            link(dve.scalar_tensor_tensor(top, poly, 2.0, top, ALU.mult, ALU.add))
            link(dve.tensor_scalar(small2[:, 0:4], top, -4.0, None, ALU.mult))

            for m in range(KD):
                prep_lo(0, m, vec0)
            for j in range(AHEAD):
                split_lo(Slot(0, j))

            def ffn(layer, f, e):
                name = f"ffn{f + 1}"
                no = layer * 2 + f
                norm = norm_no(layer, e) - 1
                for g, ft in enumerate(FF_GROUPS):
                    s0 = STAGE[f"{name}_up{g}"]
                    f0 = sum(FF_GROUPS[:g])
                    if g == 0:
                        inv_rms(norm)

                    def up(it):
                        for q in range(2):
                            i = no * FF_TILES + f0 + 2 * it + q + 1
                            split_lo(Slot(layer, s0 + 2 * q + AHEAD, it, RING))
                            normed(Slot(layer, s0 + 2 * q, it, RING), work(q), norm).then_inc(slot_read, 1)
                            split_lo(Slot(layer, s0 + 2 * q + 1 + AHEAD, it, RING))
                            up_slot = Slot(layer, s0 + 2 * q + 1, it, RING)
                            normed(up_slot, work(6 + q), norm).then_inc(slot_read, 1)
                            dve.wait_ge(tanh_ready, i)
                            dve.scalar_tensor_tensor(work(4 + q), work(2 + q), 1.0, work(q), ALU.add, ALU.mult)\
                               .then_inc(sil_ready, 1)
                            dve.wait_ge(slot_read, up_slot.done)
                            dve.wait_ge(sil_ready, i)
                            dve.tensor_tensor(work(8 + q), work(4 + q), work(6 + q), ALU.mult).then_inc(act_ready, 1)
                            dve.wait_ge(a_hi_ready, i)
                            at = bass.ds((2 * it + q) * S, S)
                            dve.tensor_tensor(a_lo_t[:, at], work(8 + q), a_hi_t[:, at].bitcast(F32), ALU.subtract)\
                               .then_inc(a_lo_ready, 1)
                    repeat(dve, s0, ft // 2, RING, up)
                    if g < 2:
                        b = no * 2 + g
                        dve.wait_ge(ada_done, b + 1)
                        dve.tensor_copy(mod_t[:, bass.ds(b * ADA_BATCH, ADA_BATCH)], tr[:, 0:ADA_BATCH]).then_inc(mod_read, 1)
                    s0 = STAGE[f"{name}_down{g}"]

                    def add(slot, at):
                        dve.wait_ge(slot_done, slot.done)
                        dve.scalar_tensor_tensor(at, proj[:, slot.pos, :], 0.25, at, ALU.mult, ALU.add)\
                           .then_inc(slot_read, slot.inc)
                    if g < 2:
                        def down(it):
                            for j in range(RING):
                                split_lo(Slot(layer, s0 + j + AHEAD, it, RING))
                                add(Slot(layer, s0 + j, it, RING), h_t[:, bass.ds((it * RING + j) * S, S)])
                        repeat(dve, s0, KD // RING, RING, down)
                        continue
                    if f == 0:
                        dve.wait_ge(vec_in, 16 * (layer + 1))
                    gain = vec[:, (V_MIX if f == 0 else V_PLE):]
                    for m in range(KD):
                        split_lo(Slot(layer, s0 + m + AHEAD))
                        add(Slot(layer, s0 + m), h(m))
                        if m:
                            prep_lo(norm_no(layer, e), m - 1, gain)
                    prep_lo(norm_no(layer, e), KD - 1, gain)

            def evac(slot, dst, by=None):
                dve.wait_ge(slot_done, slot.done)
                if by is None:
                    dve.tensor_copy(dst, proj[:, slot.pos, :]).then_inc(slot_read, slot.inc)
                else:
                    dve.tensor_tensor(dst, proj[:, slot.pos, :], by, ALU.mult).then_inc(slot_read, slot.inc)

            def head_evac(slot, j, q):
                evac(slot, work((0, 2, 4, 6)[j] + (q if j < 3 else 0)), cs if j == 1 else None)

            def row_max(n, qt):
                dve.wait_ge(s_done, n * QT + qt + 1)
                dve.tensor_reduce(stat_t[:, 4 + qt:5 + qt], sc[:, qt % 2, 0:(qt + 1) * P], AX, ALU.max)\
                   .then_inc(mx_ready, 1)
                dve.wait_ge(mx_ready, n * QT + qt + 1)
                dve.tensor_scalar(stat_t[:, 8 + qt:9 + qt], stat_t[:, 4 + qt:5 + qt], -SCALE1, None, ALU.mult)\
                   .then_inc(nmax_ready, 1)

            def row_norm(n, qt):
                dve.wait_ge(exp_ready, n * QT + qt + 1)
                dve.reciprocal(stat_t[:, 20 + qt:21 + qt], stat_t[:, 16 + qt:17 + qt]).then_inc(rinv_ready, 1)
                dve.wait_ge(rinv_ready, n * QT + qt + 1)
                p = work(9 + qt % 2)[:, 0:(qt + 1) * P]
                dve.tensor_scalar(p, p, stat_t[:, 20 + qt:21 + qt], None, ALU.mult).then_inc(p_ready, 1)

            def core(layer, hd, q, slots, ahead):
                n = layer * HEADS + hd

                def side(j):
                    if slots:
                        split_lo(ahead[j])
                        head_evac(slots[j], j, 1 - q)
                dve.wait_ge(v_turned, n + 1)
                dve.tensor_copy(work(7 + q), tr[:, :]).then_inc(v_ready, 1)
                row_max(n, 0)
                row_max(n, 1)
                side(0)
                row_norm(n, 0)
                row_max(n, 2)
                side(1)
                row_norm(n, 1)
                row_max(n, 3)
                side(2)
                row_norm(n, 2)
                side(3)
                row_norm(n, 3)
                dve.wait_ge(o_hi_ready, n + 1)
                at = bass.ds(hd * S, S)
                dve.tensor_tensor(u_lo_t[:, at], ot[:, :], u_hi_t[:, at].bitcast(F32), ALU.subtract).then_inc(o_ready, 1)

            with dve.Fori(0, DEPTH) as layer:
                ffn(layer, 0, 0)
                s0 = STAGE["lora"]
                for j in range(6):
                    split_lo(Slot(layer, s0 + j + AHEAD))
                    if j == 0:
                        inv_rms(norm_no(layer, 0))
                    slot = Slot(layer, s0 + j)
                    normed(slot, work(j), norm_no(layer, 0)).then_inc(slot_read, 1)
                dve.wait_ge(sin_ready, 1)
                dve.wait_ge(slot_read, Slot(layer, s0 + 5).done)
                dve.tensor_tensor(work(5), work(5), cs, ALU.mult).then_inc(kr_rope, 1)
                zs = [0]

                def zlink(ins):
                    zs[0] += 1
                    ins.then_inc(z_step, 1)
                    dve.wait_ge(z_step, Z_STEPS * layer + zs[0])
                Z_STEPS = 4 * 4

                def side(i):
                    if i < 2:
                        dve.wait_ge(lora_rms, 2 * layer + i + 1)
                        t = work(11 + 2 * i)
                        dve.reciprocal(t, t).then_inc(lora_rs, 1)
                    elif i < 7:
                        j = i - 2
                        dve.wait_ge(lora_rs, 2 * layer + 2)
                        g = V_Q + j
                        dve.scalar_tensor_tensor(work(j), work(j), vec[:, g:g + 1], work(11 if j < 3 else 13), ALU.mult,
                                                 ALU.mult).then_inc(lora_norm, 1)
                    else:
                        j = i - 7
                        dve.wait_ge(lora_hi, 5 * layer + j + 1)
                        dve.tensor_tensor(a_lo(j), work(j), a_hi(j).bitcast(F32), ALU.subtract).then_inc(lora_ready, 1)
                s0 = STAGE["conv"]
                for j in range(12):
                    t, part = divmod(j, 3)
                    split_lo(Slot(layer, s0 + j + AHEAD))
                    slot = Slot(layer, s0 + j)
                    if part == 0:
                        dve.wait_ge(conv_ready, 4 * layer + t)
                    normed(slot, work((6, 7, 10)[part]), norm_no(layer, 0)).then_inc(slot_read, 1)
                    if j == 1:
                        dve.wait_ge(kr_fold, layer + 1)
                        dve.tensor_copy(work(15), sc[:, 0, :]).then_inc(kr_ready, 1)
                    side(j)
                    if part == 1:
                        dve.wait_ge(slot_read, slot.done)
                        zlink(dve.tensor_tensor(work(9), work(6), work(7), ALU.mult))
                    if part == 2:
                        w = lambda tap: vec[:, V_CONV + 4 * tap + t:V_CONV + 4 * tap + t + 1]
                        y, z1 = work(6), work(9)
                        zlink(dve.tensor_scalar(y, z1, w(2), None, ALU.mult))
                        for back in (1, 2):
                            zlink(dve.scalar_tensor_tensor(y[:, back:S], z1[:, 0:S - back], w(2 - back), y[:, back:S],
                                                           ALU.mult, ALU.add))
                        dve.wait_ge(slot_read, slot.done)
                        dve.tensor_tensor(work(7), work(10), y, ALU.mult).then_inc(conv_y, 1)
                        dve.wait_ge(conv_hi, 4 * layer + t + 1)
                        dve.tensor_tensor(a_lo(5 + t), work(7), a_hi(5 + t).bitcast(F32), ALU.subtract)\
                           .then_inc(conv_ready, 1)
                s0 = STAGE["gates"]

                def gates(it):
                    for j in range(RING):
                        split_lo(Slot(layer, s0 + j + AHEAD, it, RING))
                        dve.wait_ge(gate_tanh, 16 * layer + it * RING + j + 1)
                        normed(Slot(layer, s0 + j, it, RING), work(13 + j % 2), norm_no(layer, 0)).then_inc(slot_read, 1)
                repeat(dve, s0, 4, RING, gates)
                s0 = STAGE["heads"]
                for j in range(4):
                    split_lo(Slot(layer, s0 + j + AHEAD))
                    head_evac(Slot(layer, s0 + j), j, 0)

                def heads(it):
                    end = isinstance(it, int)
                    for q in range(2):
                        o = s0 + 4 * (q + 1) + (24 if end else 0)
                        r = 0 if end else it
                        slots = [Slot(layer, o + j, r, 8) for j in range(4)]
                        ahead = [Slot(layer, o + j + AHEAD, r, 8) for j in range(4)]
                        core(layer, 2 * it + q, q, None if end and q else slots, ahead)
                with dve.Fori(0, HEADS // 2 - 1) as it:
                    heads(it)
                heads(HEADS // 2 - 1)
                s0 = STAGE["branch_out"]
                for m in range(KD):
                    q = m % 2
                    for br in range(2):
                        slot = Slot(layer, s0 + 2 * m + br)
                        split_lo(Slot(layer, s0 + 2 * m + br + AHEAD))
                        dve.wait_ge(gate_tanh, 16 * (layer + 1) + 2)
                        dve.wait_ge(slot_done, slot.done)
                        dve.scalar_tensor_tensor(work(2 * q + br), gate(2 * m + br), 1.0, proj[:, slot.pos, :], ALU.add,
                                                 ALU.mult).then_inc(slot_read, 1)
                    dve.wait_ge(slot_read, slot.done)
                    dve.tensor_tensor(work(4 + q), work(2 * q), work(2 * q + 1), ALU.add).then_inc(mg_ready, 1)
                    dve.wait_ge(mg_hi, KD * layer + m + 1)
                    dve.tensor_tensor(merged_lo(m), work(4 + q), merged_hi(m).bitcast(F32), ALU.subtract)\
                       .then_inc(merged_ready, 1)
                s0 = STAGE["mix_out"]
                for m in range(KD):
                    slot = Slot(layer, s0 + m)
                    split_lo(Slot(layer, s0 + m + AHEAD))
                    dve.wait_ge(slot_done, slot.done)
                    dve.scalar_tensor_tensor(h(m), proj[:, slot.pos, :], 0.5, h(m), ALU.mult, ALU.add).then_inc(slot_read, 1)
                    if m:
                        prep_lo(norm_no(layer, 1), m - 1, vec[:, V_FFN2:])
                prep_lo(norm_no(layer, 1), KD - 1, vec[:, V_FFN2:])
                ffn(layer, 1, 2)
                s0 = STAGE["ple_gate"]
                for m in range(KD):
                    split_lo(Slot(layer, s0 + m + AHEAD))
                    if m == 0:
                        inv_rms(norm_no(layer, 2))
                    if m == 1:
                        dve.wait_ge(p_hi_ready, layer + 1)
                        dve.tensor_tensor(a_lo_t[:, 0:2 * S], work_t[:, 12 * S:14 * S], a_hi_t[:, 0:2 * S].bitcast(F32),
                                          ALU.subtract).then_inc(p_split, 1)
                    if m >= 2:
                        dve.wait_ge(ple_tanh, KD * layer + m - 1)
                    normed(Slot(layer, s0 + m), work(m % 2), norm_no(layer, 2)).then_inc(slot_read, 1)
                s0 = STAGE["ple_proj"]
                for m in range(KD):
                    slot = Slot(layer, s0 + m)
                    split_lo(Slot(layer, s0 + m + AHEAD))
                    dve.wait_ge(ple_tanh, KD * (layer + 1))
                    dve.wait_ge(slot_done, slot.done)
                    dve.scalar_tensor_tensor(work(2 + m % 2), gate(m), 1.0, proj[:, slot.pos, :], ALU.add, ALU.mult)\
                       .then_inc(slot_read, slot.inc)
                    dve.wait_ge(slot_read, slot.done)
                    dve.scalar_tensor_tensor(h(m), work(2 + m % 2), 0.5, h(m), ALU.mult, ALU.add).then_inc(ple_step, 1)
                    if m:
                        prep_lo(norm_no(layer, 3), m - 1, vec[:, V_NEXT:])
                prep_lo(norm_no(layer, 3), KD - 1, vec[:, V_NEXT:])

            def ahead(s):
                if s + AHEAD < B2_SLOTS:
                    split_lo(Slot(L2, s + AHEAD))

            c2 = lambda at, n=1: col2[:, at:at + n]
            dve.wait_ge(mod_read, 8)
            link(dve.tensor_tensor(mod_t[:, :], mod_t[:, :], c2(C_ADAB, 48), ALU.add))
            for i, (gain, part) in enumerate(((C_PRE, 1), (C_POST, 2), (C_PREM, 4), (C_POSTM, 5))):
                link(dve.scalar_tensor_tensor(modc[:, 8 * i:8 * i + 8], mod_t[:, 8 * part:8 * part + 8], 1.0, c2(gain, 8),
                                              ALU.add, ALU.mult))
            dve.tensor_scalar(small2[:, 20:28], c2(C_BA, 8), 0.5, None, ALU.mult).then_inc(mods_ready, 1)

            inv_rms(8)
            dve.wait_ge(rs_ready, 9)
            for m in range(KD):
                dve.scalar_tensor_tensor(h(m), h(m), vec[:, V_NEXT + m:V_NEXT + m + 1], rs, ALU.mult, ALU.mult).then_inc(hf_ready, 1)

            def modulated(n, gain, sh):
                inv_rms(n)
                dve.wait_ge(rs_ready, n + 1)
                for m in range(KD + 1):
                    if m < KD:
                        dve.scalar_tensor_tensor(work(2 + m), h(m), modc[:, gain + m:gain + m + 1], rs, ALU.mult, ALU.mult)\
                           .then_inc(tmp_ready, 1)
                    if m:
                        dve.wait_ge(u_hi_ready, n * KD + m)
                        dve.scalar_tensor_tensor(u_lo(m - 1), work(1 + m), mod_t[:, sh + m - 1:sh + m], u_hi(m - 1).bitcast(F32),
                                                 ALU.add, ALU.subtract).then_inc(u_ready, 1)
            modulated(9, 0, 0)
            dst = [xr(j) for j in range(4)] + [KC, VC, KS, VS, KW, VW] + [q2(j) for j in range(4)] + [gT] + [gr(j) for j in range(4)]
            for s in range(IN2):
                ahead(s)
                slot = Slot(L2, s)
                if 10 <= s <= 13:
                    dve.wait_ge(slot_done, slot.done)
                    dve.tensor_scalar(dst[s], proj[:, slot.pos, :], 0.125, None, ALU.mult).then_inc(slot_read, 1)
                else:
                    evac(slot, dst[s])
                if 4 <= s <= 7:
                    j = s - 4
                    dve.wait_ge(slot_read, Slot(L2, j).done)
                    xf = work(2 + j)
                    w = lambda tap: c2(C_CW + 4 * tap + j)
                    link(dve.tensor_scalar(xf, xr(j), w(3), c2(C_CB + j), ALU.mult, ALU.add))
                    for back in (1, 2, 3):
                        i = dve.scalar_tensor_tensor(xf[:, back:S], xr(j)[:, 0:S - back], w(3 - back), xf[:, back:S], ALU.mult, ALU.add)
                        if back < 3:
                            link(i)
                    i.then_inc(xf_ready, 1)
                if 6 <= s <= 9:
                    j = s - 6
                    dve.wait_ge(rg_tanh, 2 * j + 2)
                    dve.tensor_scalar(work(6 + j), work(6 + j), 1.0, small2[:, j:j + 1], ALU.add, ALU.mult).then_inc(la_ready, 1)
                if 8 <= s <= 11:
                    j = s - 8
                    dve.wait_ge(decay_ready, 3 * j + 3)
                    dve.scalar_tensor_tensor(work(6 + j), work(14 + j % 2), 1.0, work(6 + j), ALU.add, ALU.mult).then_inc(v2_ready, 1)
                    dve.wait_ge(xf_ready, j + 1)
                    dve.scalar_tensor_tensor(work(10 + j), work(10 + j), 1.0, work(2 + j), ALU.add, ALU.mult).then_inc(ix_ready, 1)
                if 13 <= s <= 16:
                    j = s - 13
                    dve.wait_ge(sqrt_ready, j + 1)
                    link(dve.scalar_tensor_tensor(work(10 + j), work(10 + j), 0.5, work(6 + j), ALU.mult, ALU.mult))
                    link(dve.tensor_tensor_scan(work(6 + j), xr(j), work(10 + j), 0.0, ALU.mult, ALU.add))
            dve.wait_ge(slot_done, Slot(L2, IN2 - 1).done)
            dve.wait_ge(w2_in, 16)
            for kv, src in enumerate((KC, VC)):
                xv = X(kv).rearrange("p (t c) -> p t c", c=62)
                for g in range(2):
                    for half in range(2):
                        gp, hp = slice(64 * g, 64 * g + 64), slice(64 * half, 64 * half + 64)
                        rows = src[gp, half:half + 1]
                        tok = bass.AP(rows.tensor, rows.offset, [rows.ap[0], (2, CMP_K), (16, N_CMP)])
                        pos = pos2(kv)[gp, half:32:2].unsqueeze(2).to_broadcast([64, CMP_K, N_CMP])
                        dve.tensor_tensor(xv[hp, :, g * N_CMP:(g + 1) * N_CMP], tok, pos, ALU.add).then_inc(x_built, 1)
            for i, (d, bank) in enumerate(((vn_s, 0), (vn_w, 1))):
                dve.wait_ge(v2_turned, i + 1)
                dve.tensor_copy(d, proj[:, bank, :]).then_inc(v2_copied, 1)
            dve.wait_ge(g_turned, 1)
            dve.tensor_scalar(gcols.rearrange("p (t c) -> p t c", t=QT), tr[:, :].rearrange("p (t c) -> p t c", t=QT)[:, :, 0:24],
                              1.0, 0.5, ALU.add, ALU.mult).then_inc(g_cols, 1)
            for j in range(4):
                dve.wait_ge(gel_sq, j + 1)
                link(dve.tensor_scalar(work(2 + j), work(2 + j), 0.044715, 1.0, ALU.mult, ALU.add))
                dve.tensor_tensor(work(2 + j), work(2 + j), gr(j), ALU.mult).then_inc(gel_in, 1)
            for j in range(4):
                dve.wait_ge(gel_tanh, j + 1)
                link(dve.scalar_tensor_tensor(gr(j), work(2 + j), 1.0, gr(j), ALU.add, ALU.mult))
                dve.scalar_tensor_tensor(gr(j), gr(j), 0.5, work(6 + j), ALU.mult, ALU.mult).then_inc(rnn_ready, 1)
            dve.wait_ge(hid_done, 1)
            x, t = acc_t[:, 0:248], acc_t[:, 248:496]
            link(dve.tensor_copy(x.rearrange("p (i c) -> p i c", i=4), ot[:, 0:256].rearrange("p (i c) -> p i c", i=4)[:, :, 0:62]))
            link(dve.tensor_tensor(t, x, x, ALU.mult))
            link(dve.tensor_scalar(t, t, 0.044715, 1.0, ALU.mult, ALU.add))
            dve.tensor_tensor(t, t, x, ALU.mult).then_inc(hid_in, 1)
            dve.wait_ge(hid_tanh, 1)
            link(dve.scalar_tensor_tensor(x, t, 1.0, x, ALU.add, ALU.mult))
            dve.tensor_scalar(x, x, 0.5, None, ALU.mult).then_inc(hid_ready, 1)
            dve.wait_ge(kv_cmp_done, 1)
            dve.tensor_copy(kcmp[0:64, :], sc[0:64, 0, 0:N_CMP]).then_inc(kv_cmp_ready, 1)
            dve.tensor_copy(kcmp[64:P, :], sc[64:P, 0, N_CMP:62]).then_inc(kv_cmp_ready, 1)
            dve.tensor_copy(vcmp, sc[0:N_CMP, 1, 0:P]).then_inc(kv_cmp_ready, 1)
            dve.wait_ge(bias_ready, 2 * HEADS)
            dve.wait_ge(g_ready, 1)

            gates2 = gcols.rearrange("p (t c) -> p t c", t=QT)

            def cmp_softmax(n, head):
                dve.wait_ge(cs_done, n + 1)
                dve.wait_ge(tc_done, n)
                pc3 = p_c.rearrange("p (t c) -> p t c", c=N_CMP)
                mx = stat_t[:, 24:28]
                dve.tensor_tensor(p_c, proj[:, 2, 0:QT * N_CMP], bias_c[:, bass.ds(head * QT * N_CMP, QT * N_CMP)], ALU.add)\
                   .then_inc(pc_step, 1)
                dve.wait_ge(pc_step, 6 * n + 1)
                dve.tensor_reduce(mx, pc3, AX, ALU.max).then_inc(pc_step, 1)
                dve.wait_ge(pc_step, 6 * n + 2)
                dve.tensor_tensor(pc3, pc3, mx.unsqueeze(2).to_broadcast([P, QT, N_CMP]), ALU.subtract).then_inc(cs_sub, 1)

            def cmp_norm(n, head):
                pc3 = p_c.rearrange("p (t c) -> p t c", c=N_CMP)
                sm = stat_t[:, 28:32]
                dve.wait_ge(cs_exp, n + 1)
                dve.tensor_reduce(sm, pc3, AX, ALU.add).then_inc(pc_step, 1)
                dve.wait_ge(pc_step, 6 * n + 3)
                dve.reciprocal(sm, sm).then_inc(pc_step, 1)
                dve.wait_ge(pc_step, 6 * n + 4)
                dve.tensor_tensor(sm.unsqueeze(2), sm.unsqueeze(2), gates2[:, :, bass.ds(head, 1)], ALU.mult).then_inc(pc_step, 2)
                dve.wait_ge(pc_step, 6 * n + 6)
                dve.tensor_tensor(pc3, pc3, sm.unsqueeze(2).to_broadcast([P, QT, N_CMP]), ALU.mult).then_inc(pc_ready, 1)

            def row_max2(n, qt):
                w, q = (qt + 1) * P, qt % 2
                for br, bank in enumerate((sc, proj)):
                    dve.wait_ge(s2_done, 2 * (n * QT + qt) + br + 1)
                    dve.tensor_reduce(stat_t[:, 4 + 2 * q + br:5 + 2 * q + br], bank[:, q, 0:w], AX, ALU.max).then_inc(max2, 1)
                dve.wait_ge(max2, 2 * (n * QT + qt + 1))
                dve.tensor_scalar(stat_t[:, 8 + 2 * q:10 + 2 * q], stat_t[:, 4 + 2 * q:6 + 2 * q], -1.0, None, ALU.mult)\
                   .then_inc(nmax2, 1)

            def row_norm2(n, head, qt):
                w, q = (qt + 1) * P, qt % 2
                dve.wait_ge(exp2, 4 + 2 * (n * QT + qt + 1))
                inv = stat_t[:, 16 + 2 * q:18 + 2 * q]
                dve.reciprocal(inv, stat_t[:, 12 + 2 * q:14 + 2 * q]).then_inc(inv2, 1)
                dve.wait_ge(inv2, n * QT + qt + 1)
                for br in range(2):
                    dve.tensor_tensor(inv[:, br:br + 1], inv[:, br:br + 1], gates2[:, qt, bass.ds(head + HEADS * (br + 1), 1)],
                                      ALU.mult).then_inc(ginv2, 1)
                dve.wait_ge(ginv2, 2 * (n * QT + qt + 1))
                for br in range(2):
                    pt = work(2 * br + q)[:, 0:w]
                    dve.tensor_scalar(pt, pt, inv[:, br:br + 1], None, ALU.mult).then_inc(p2_ready, 1)

            with dve.Fori(0, QT) as j:
                dve.wait_ge(s2_done, 2 * 2 * QT * j)
                dve.tensor_copy(qbuf, ax_t[:, bass.ds((14 + j) * S, S)]).then_inc(q_ready, 1)
                for par in range(2):
                    n = 2 * j + par
                    head = 4 * par + j
                    cmp_softmax(n, head)
                    row_max2(n, 0)
                    row_max2(n, 1)
                    cmp_norm(n, head)
                    row_norm2(n, head, 0)
                    dve.wait_ge(t2_done, 2 * (n * QT) + 2)
                    row_max2(n, 2)
                    row_norm2(n, head, 1)
                    dve.wait_ge(t2_done, 2 * (n * QT + 1) + 2)
                    row_max2(n, 3)
                    row_norm2(n, head, 2)
                    row_norm2(n, head, 3)
                    rows = slice(64 * par, 64 * par + 64)
                    dve.wait_ge(o2_done, n + 1)
                    dve.tensor_copy(work_t[rows, bass.ds((12 + j) * S, S)], ot[rows, :]).then_inc(o2_ready, 1)
            for i in range(2):
                dve.wait_ge(mix_rms, i + 1)
                dve.reciprocal(work(8 + i), work(8 + i)).then_inc(mix_rs, 1)
            dve.wait_ge(mix_rs, 2)
            for k in range(KD + 1):
                src = lambda k: gr(k) if k < 4 else work(8 + k)
                if k < KD:
                    dve.scalar_tensor_tensor(src(k), src(k), c2(C_RNN + k), work(8 + k // 4), ALU.mult, ALU.mult).then_inc(mix_norm, 1)
                if k:
                    dve.wait_ge(u_hi_ready, 10 * KD + k)
                    dve.tensor_tensor(u_lo(k - 1), src(k - 1), u_hi(k - 1).bitcast(F32), ALU.subtract).then_inc(u_ready, 1)
            for m in range(KD):
                ahead(B2_OUT + m)
                evac(Slot(L2, B2_OUT + m), gate(m))

            def residual(n, gain, done):
                inv_rms(n)
                dve.wait_ge(rs_ready, n + 1)
                for m in range(KD + 1):
                    if m < KD:
                        dve.scalar_tensor_tensor(gate(m), gate(m), modc[:, gain + m:gain + m + 1], rs, ALU.mult, ALU.mult)\
                           .then_inc(y_scaled, 1)
                    if m:
                        dve.wait_ge(y_scaled, KD * (n == 12) + m)
                        dve.tensor_tensor(h(m - 1), h(m - 1), gate(m - 1), ALU.add).then_inc(done, 1)
            residual(10, 8, h2_ready)
            modulated(11, 16, 24)

            def ff(g):
                end = isinstance(g, int)
                for i in range(2 * KD):
                    slot = Slot(L2, B2_FF + i, g, 2 * KD)
                    if not (end and i >= 2 * KD - AHEAD):
                        split_lo(Slot(L2, B2_FF + i + AHEAD, g, 2 * KD))
                    dve.wait_ge(slot_done, slot.done)
                    if i < KD:
                        dve.tensor_scalar(work(i % 4), proj[:, slot.pos, :], 0.0, None, ALU.max).then_inc(slot_read, 1)
                        if i:
                            lo(g, i - 1)
                        if i == KD - 1:
                            lo(g, i)
                    else:
                        m = i - KD
                        dve.wait_ge(y_zero, KD)
                        dve.tensor_tensor(gate(m), gate(m), proj[:, slot.pos, :], ALU.add).then_inc(slot_read, 1)

            def lo(g, i):
                dve.wait_ge(a_hi_ready, FF_TILES * 2 * DEPTH + KD * g + i + 1)
                dve.tensor_tensor(a_lo(i), work(4 + i % 4), a_hi(i).bitcast(F32), ALU.subtract).then_inc(a_lo_ready, 1)
            with dve.Fori(0, FF2_GROUPS - 1) as g:
                ff(g)
            ff(FF2_GROUPS - 1)
            residual(12, 24, h_out)


def columns(v):
    v = np.asarray(v)
    return np.moveaxis(v.reshape(*v.shape[:-1], -1, P), -1, -2)


def slots_of(w, width=P):
    K, N = w.shape
    return np.ascontiguousarray(w.reshape(K // P, P, N // width, width).transpose(2, 1, 0, 3)).reshape(N // width, P, -1)


def turned(x):
    t, f = x.shape
    return np.ascontiguousarray(x.T.reshape(f // P, P, t).transpose(1, 0, 2))


def lay_out(i):
    c = np.ascontiguousarray
    stack = lambda f: c(np.stack([f(l) for l in range(DEPTH)]))
    o = {}
    o["x_t"] = turned(i["x"][0]).reshape(P, -1)
    o["positions"] = c(i["positions"])
    o["p_t"] = stack(lambda l: turned(i["p"][l, 0]))
    o["vec0"] = c(columns(i["ffn1_norm"][0]))
    nxt = [i["ffn1_norm"][1], i["final_norm"]]
    o["vec"] = stack(lambda l: np.concatenate(
        [columns(v) for v in (i["mix_norm"][l], i["ffn2_norm"][l], i["ple_norm"][l], nxt[l], i["q_norm"][l], i["kv_norm"][l])]
        + [columns(i["conv_w"][l, t]) for t in range(3)], axis=1))
    for f in ("ffn1", "ffn2"):
        def up(l):
            g = slots_of(i[f + "_w_gu"][l])
            return np.stack([g[:FF_TILES], g[FF_TILES:]], axis=1).reshape(2 * FF_TILES, P, -1)
        o[f + "_gu"] = stack(up)
        w = i[f + "_w_down"]
        o[f + "_dn8"] = stack(lambda l: np.concatenate([slots_of(w[l, :D]), slots_of(w[l, D:2 * D])]))
        o[f + "_dn6"] = stack(lambda l: slots_of(w[l, 2 * D:]))

    def w_in(l):
        w = i["w_in"][l]
        b, cc, v = (slots_of(w[:, n * CONV:(n + 1) * CONV]) for n in range(3))
        at = 3 * CONV
        lora = slots_of(w[:, at:at + Q_LORA + KV_LORA])
        at += Q_LORA + KV_LORA
        r = w[:, at:at + ROPE]
        kr = slots_of(np.concatenate([r, r[:, 32:], r[:, :32]], axis=1))
        at += ROPE
        gc, gm = slots_of(w[:, at:at + D]), slots_of(w[:, at + D:])
        return np.concatenate([lora, kr, np.stack([cc, v, b], axis=1).reshape(12, P, -1),
                               np.stack([gc, gm], axis=1).reshape(16, P, -1)])
    o["in_w"] = stack(w_in)

    def head_q(l):
        w = i["w_uq"][l].reshape(Q_LORA, HEADS, NOPE + ROPE)
        r = w[:, :, NOPE:]
        w = np.concatenate([w[:, :, :NOPE], r, r[:, :, 32:], r[:, :, :32]], axis=2)
        return slots_of(w.reshape(Q_LORA, -1))
    o["head_q"] = stack(head_q)
    o["head_kv"] = stack(lambda l: slots_of(i["w_ukv"][l]))
    o["conv_out"] = stack(lambda l: slots_of(i["w_conv_out"][l]))
    o["mla_out"] = stack(lambda l: slots_of(i["w_mla_out"][l]))
    o["mix_out"] = stack(lambda l: slots_of(i["w_o"][l]))
    o["ple_gate"] = stack(lambda l: slots_of(i["w_ple_gate"][l]))
    o["ple_proj"] = stack(lambda l: slots_of(i["w_ple_proj"][l]))
    freq = (np.float32(10000.0) ** (-np.arange(0, ROPE, 2, dtype=np.float32) / np.float32(ROPE))).astype(np.float32)
    phase = np.repeat(np.array([np.pi / 2, np.pi / 2, np.pi, 0.0], np.float32), 32)
    o["rope_consts"] = c(np.stack([np.tile(freq, 4), phase], axis=1))
    o["c_t"] = c(columns(i["c_2"][0]))
    o["ada"] = c(slots_of(i["ada_w_2"][0]).reshape(8, ADA_BATCH, P, D).transpose(0, 2, 1, 3)).reshape(8, P, ADA_BATCH * D)

    def by_group(v):
        s = v.shape[:-1]
        return v.reshape(*s, 2, 4, 64).swapaxes(-3, -2).reshape(*s, 512)
    o["col2"] = c(np.concatenate(
        [columns(i[n][0]) for n in ("pre_norm_mix_2", "post_norm_mix_2", "pre_norm_mlp_2", "post_norm_mlp_2", "norm_rnn_out_2")]
        + [columns(by_group(i["norm_att_out_2"][0]))] + [columns(i["conv_w_2"][0, t]) for t in range(4)]
        + [columns(i[n][0]) for n in ("conv_b_2", "lru_ba_2", "lru_bx_2", "lru_lambda_2", "ada_b_2")], axis=1))
    w = i["w_in_2"][0]
    g_rnn, x_rnn, q, kvs, gates = np.split(w, [512, 1024, 1536, 1536 + 768], axis=1)
    gates = np.concatenate([gates, np.zeros((D, P - gates.shape[1]), w.dtype)], axis=1)
    o["in2"] = c(np.concatenate([slots_of(a) for a in (x_rnn, kvs, by_group(q), gates, g_rnn)]))
    bd = np.zeros((P, 8, P), w.dtype)
    for n, name in enumerate(("lru_wa_2", "lru_wx_2")):
        for b in range(8):
            r = 64 * (b % 2)
            bd[r:r + 64, 4 * n + b // 2, r:r + 64] = i[name][0, b]
    o["lru_w"] = bd.reshape(P, -1)
    w1 = np.stack([i["cmp_w1_k_2"][0], i["cmp_w1_v_2"][0]]).reshape(2, CMP_K, P, 256)
    o["cmp_w1"] = c(w1.transpose(2, 0, 1, 3)).reshape(P, -1)
    w2k, w2v = i["cmp_w2_k_2"][0].reshape(2, P, 64), i["cmp_w2_v_2"][0].reshape(2, P, 64)
    pos = [np.tile(i[n][0].T, (2, 1)) for n in ("cmp_pos_k_2", "cmp_pos_v_2")]
    o["cmp_w2"] = c(np.concatenate([w2k[0], w2k[0], w2k[1], w2k[1], w2v[0], w2v[1]] + pos, axis=1))
    wo = i["w_out_2"][0]
    wo = np.concatenate([wo[:512], by_group(wo[512:].T).T])
    o["out2"] = slots_of(wo)
    o["ff1"] = slots_of(i["w_ff1_2"][0])
    o["ff2"] = c(np.concatenate([slots_of(i["w_ff2_2"][0][g * D:(g + 1) * D]) for g in range(FF2_GROUPS)]))
    return o


def kernel(**inputs):
    import concourse.bacc as bacc
    from concourse.bass_utils import run_bass_kernel_spmd

    nc = bacc.Bacc("TRN2", target_bir_lowering=False, num_devices=1)
    arrays = {"in_" + n: np.ascontiguousarray(a) for n, a in lay_out({n: np.asarray(a) for n, a in inputs.items()}).items()}
    aps = {n[3:]: nc.dram_tensor(n, a.shape, mybir.dt.from_np(a.dtype), kind="ExternalInput").ap() for n, a in arrays.items()}
    out = nc.dram_tensor("out_t", (P, KD, S), F32, kind="ExternalOutput").ap()
    build(nc, aps, out)
    r = run_bass_kernel_spmd(nc, [arrays], core_ids=[0])
    got = r.results[0]["out_t"]
    return np.ascontiguousarray(got.transpose(1, 0, 2).reshape(D, S).T)[None]
```

```python
import numpy as np
import concourse.bass as bass
from concourse import mybir
from contextlib import ExitStack

F32 = mybir.dt.float32
F32R = mybir.dt.float32r
I32 = mybir.dt.int32
ALU = mybir.AluOpType
ACT = mybir.ActivationFunctionType
AX = mybir.AxisListType.X

P = 128
S = 512
D = 1024
KD = D // P
DEPTH = 2
D_FF = 2816
FF_TILES = D_FF // P
FF_GROUPS = [8, 8, 6]
HEADS = 8
NOPE, ROPE = 128, 64
Q_LORA, KV_LORA, CONV, PLE = 384, 256, 512, 256
EPS = 1e-6
SCALE1 = float(NOPE + ROPE) ** -0.5
NEG = -1e30
FAR = 3e32
QT = S // P

RING = 4
AHEAD = 2

FFN_SLOTS = [2 * f for f in FF_GROUPS]
K_TILES = []
STAGE = {}


def _stage(name, tiles):
    STAGE[name] = len(K_TILES)
    K_TILES.extend(tiles)


def _ffn(name):
    for g, f in enumerate(FF_GROUPS):
        _stage(f"{name}_up{g}", [KD] * (2 * f))
        _stage(f"{name}_down{g}", [f] * KD)


_ffn("ffn1")
_stage("lora", [KD] * 6)
_stage("conv", [KD] * 12)
_stage("gates", [KD] * 16)
_stage("heads", [Q_LORA // P, Q_LORA // P, KV_LORA // P, KV_LORA // P] * HEADS)
_stage("branch_out", [CONV // P, KD] * KD)
_stage("mix_out", [KD] * KD)
_ffn("ffn2")
_stage("ple", [KD, PLE // P] * KD)
LAYER_SLOTS = len(K_TILES)
LAYER_STEP = -(-LAYER_SLOTS // RING) * RING
LOADS = [len(range(p, LAYER_SLOTS, RING)) for p in range(RING)]

FF2_TILES = 4 * D // P
FF2_GROUPS = FF2_TILES // KD
IN2 = 19
B2_IN, B2_OUT = 0, IN2
B2_FF = B2_OUT + KD
B2_SLOTS = B2_FF + FF2_GROUPS * 2 * KD

V_MIX, V_FFN2, V_PLE, V_NEXT, V_Q, V_KV, V_CONV = 0, 8, 16, 24, 32, 35, 37
N_VEC = 49
C_PRE, C_POST, C_PREM, C_POSTM, C_RNN, C_ATT = 0, 8, 16, 24, 32, 36
C_CW, C_CB, C_BA, C_BX, C_LAM, C_ADAB = 40, 56, 60, 64, 68, 72
N_COL2 = 120
ADA_BATCH = 6
N_CMP, CMP_K = 31, 16
SLOPES = [2.0 ** -(h + 1) for h in range(HEADS)]
TWO_PI = float(2 * np.pi)
PI_A = 6.28125
PI_B = float(np.float32(np.float32((TWO_PI - PI_A) * 4096 * 64).round() / (4096 * 64)))
PI_C = float(TWO_PI - PI_A - PI_B)
ROUND = 12582912.0


class Slot:

    def __init__(self, layer, s, it=0, step=0):
        last = s == LAYER_SLOTS - 1 and not (isinstance(layer, int) and layer == DEPTH)
        if s >= LAYER_SLOTS and not (isinstance(layer, int) and layer == DEPTH):
            layer, s = layer + 1, s - LAYER_SLOTS
        in_b2 = isinstance(layer, int) and layer == DEPTH
        self.tiles = KD if in_b2 else K_TILES[s]
        self.number = layer * LAYER_STEP + s + step * it
        self.pos = s % RING
        self.loads = (layer * LOADS[self.pos] + s // RING + 1 + (step // RING) * it) * 16
        self.inc = LAYER_STEP - LAYER_SLOTS + 1 if last else 1

    @property
    def free(self):
        return self.number + 1

    @property
    def done(self):
        return self.number + RING + 1


def same_ahead(s0, n, step):
    return all((K_TILES + [KD] * AHEAD)[s0 + n * step + j] == K_TILES[s0 + j] for j in range(AHEAD))


def repeat(eng, s0, n, step, body):
    m = n if same_ahead(s0, n, step) else n - 1
    with eng.Fori(0, m) as it:
        body(it)
    if m < n:
        body(m)


def build(nc, I, out_t):
    ctx = ExitStack()
    with ctx:
        def sem(name):
            return ctx.enter_context(nc.semaphore(name))

        def sb(name, shape, dt=F32):
            return ctx.enter_context(nc.sbuf_tensor(name, shape, dt))

        def ps(name, shape):
            return ctx.enter_context(nc.psum_tensor(name, shape, F32))

        base = [-(-nc.sbuf_base // 32) * 32]

        def place(name, cols, dt=F32, at=None):
            o = base[0] if at is None else at
            t = nc.alloc_sbuf_tensor_at(name, [P, cols], dt, offset=o)
            if at is None:
                base[0] += -(-cols * 4 // 32) * 32
            return t, o

        def tiles(t):
            return lambda i: t[:, i * S:(i + 1) * S]

        raw, _ = place("raw", RING * KD * P)
        w_hi, _ = place("w_hi", RING * KD * P, F32R)
        w_lo, _ = place("w_lo", RING * KD * P, F32R)
        h_t, _ = place("h", KD * S)
        u_hi_t, u_at = place("u_hi", KD * S, F32R)
        u_lo_t, _ = place("u_lo", KD * S, F32R)
        a_hi_t, a_at = place("a_hi", 9 * S, F32R)
        a_lo_t, _ = place("a_lo", 9 * S, F32R)
        gate_t, g_at = place("gate", 2 * KD * S)
        merged_t, _ = place("merged", 2 * KD * S, F32R, at=g_at)
        ux_t, _ = place("ux", 2 * KD * S, at=u_at)
        ax_t, _ = place("ax", 18 * S, at=a_at)
        work_t, _ = place("work", 16 * S)
        sq_t, _ = place("sq", S)
        acc_t, _ = place("acc", S)
        rs_t, _ = place("rs", S)
        cs_t, _ = place("rope_table", S)
        ones, _ = place("ones", P)
        ident, _ = place("ident", P)
        fold, _ = place("fold", P)
        ident_r, _ = place("ident_r", P, F32R)
        cmask_r, _ = place("chunk_mask_r", P, F32R)
        vec, _ = place("vec", N_VEC)
        stat_t, _ = place("row_stats", 72)
        mod_t, _ = place("mod", 48)
        col2, _ = place("col2", N_COL2)
        modc, _ = place("mod_cols", 32)
        h, u_hi, u_lo, a_hi, a_lo = map(tiles, (h_t, u_hi_t, u_lo_t, a_hi_t, a_lo_t))
        gate, ux, ax, work = map(tiles, (gate_t, ux_t, ax_t, work_t))
        sq, acc, rs, cs = sq_t[:, :], acc_t[:, :], rs_t[:, :], cs_t[:, :]
        vec0 = modc[:, 0:KD]
        small2 = stat_t[:, 32:64]
        eps_t = small2[:, 28:29]
        cmask = work(2)[:, 0:P]
        merged_hi = lambda m: merged_t[:, 2 * m * S:(2 * m + 1) * S]
        merged_lo = lambda m: merged_t[:, (2 * m + 1) * S:(2 * m + 2) * S]

        def wt(t, slot, n, k=None):
            o = slot.pos * KD * P
            return t[:, o:o + n * P] if k is None else t[:, o + k * P:o + (k + 1) * P]

        c_b = gate_t[:, ADA_BATCH * D:(ADA_BATCH + 1) * D]
        c_th = gate_t[:, (ADA_BATCH + 1) * D:(ADA_BATCH + 2) * D]

        proj = ps("proj", [P, RING, S])
        sc = ps("sc", [P, 2, S])
        tr = ps("tr", [P, S])
        ot = ps("ot", [P, S])

        raw_in = [sem(f"raw_in{p}") for p in range(RING)]
        w_hi_ready = sem("w_hi_ready")
        w_lo_ready = sem("w_lo_ready")
        slot_done = sem("slot_done")
        slot_read = sem("slot_read")
        b2_in, w1_in, w2_in = sem("b2_in"), sem("w1_in"), sem("w2_in")
        mods_ready, hf_ready, tmp_ready = sem("mods_ready"), sem("hf_ready"), sem("tmp_ready")
        xf_ready, rg_done, rg_tanh, la_ready = sem("xf_ready"), sem("rg_done"), sem("rg_tanh"), sem("la_ready")
        decay_ready, v2_ready, ix_ready, sqrt_ready = (sem(n) for n in ("decay_ready", "v2_ready", "ix_ready", "sqrt_ready"))
        gel_sq, gel_in, gel_tanh, rnn_ready = sem("gel_sq"), sem("gel_in"), sem("gel_tanh"), sem("rnn_ready")
        x_built, hid_in, hid_tanh, hid_ready = (sem(n) for n in ("x_built", "hid_in", "hid_tanh", "hid_ready"))
        hid_turned, hid_cols = sem("hid_turned"), sem("hid_cols")
        kv_cmp_done, kv_cmp_ready = sem("kv_cmp_done"), sem("kv_cmp_ready")
        g_tanh, g_turned, g_cols, g_ready = sem("g_tanh"), sem("g_turned"), sem("g_cols"), sem("g_ready")
        v2_turned, v2_copied, bias_step, bias_ready = (sem(n) for n in ("v2_turned", "v2_copied", "bias_step", "bias_ready"))
        dist_ready, hid_part = sem("dist_ready"), sem("hid_part")
        q_ready, cs_done, cs_exp, pc_step, pc_ready = (sem(n) for n in ("q_ready", "cs_done", "cs_exp", "pc_step", "pc_ready"))
        cs_sub, tc_done, ptc_ready = sem("cs_sub"), sem("tc_done"), sem("ptc_ready")
        s2_done, max2, nmax2, exp2, inv2 = sem("s2_done"), sem("max2"), sem("nmax2"), sem("exp2"), sem("inv2")
        ginv2, p2_ready, t2_done, pt2_ready, o2_done, o2_ready = (sem(n) for n in ("ginv2", "p2_ready", "t2_done", "pt2_ready", "o2_done", "o2_ready"))
        mix_sq, mix_stat, mix_rms, mix_norm = (sem(n) for n in ("mix_sq", "mix_stat", "mix_rms", "mix_norm"))
        h_scaled, y_timed, h_out_pool = sem("h_scaled"), sem("y_timed"), sem("h_out_pool")
        y_timed_pool = sem("y_timed_pool")
        y_scaled, h2_ready, y_zero = sem("y_scaled"), sem("h2_ready"), sem("y_zero")
        relu_sq, h_out = sem("relu_sq"), sem("h_out")
        x_in = [sem(f"x_in{i}") for i in range(4)]
        vec0_in, const_in, col2_in, vec_in, p_in, ada_in = (
            sem(n) for n in ("vec0_in", "const_in", "col2_in", "vec_in", "p_in", "ada_in"))
        sqs_ready, comb_ready, sh_ready = sem("sqs_ready"), sem("comb_ready"), sem("sh_ready")
        consts_ready = sem("consts_ready")
        start_step = sem("start_step")
        pos_ready, sin_ready, c_tanh, lam_exp = (sem(n) for n in ("pos_ready", "sin_ready", "c_tanh", "lam_exp"))
        u_hi_ready, u_ready = sem("u_hi_ready"), sem("u_ready")
        sq_ready, sum_ready = sem("sq_ready"), sem("sum_ready")
        stat_done, rms_ready, rs_ready = sem("stat_done"), sem("rms_ready"), sem("rs_ready")
        tanh_ready, sil_ready, act_ready = sem("tanh_ready"), sem("sil_ready"), sem("act_ready")
        a_hi_ready, a_lo_ready = sem("a_hi_ready"), sem("a_lo_ready")
        ada_done = sem("ada_done")
        c_in, silu_ready, ada_sum = sem("c_in"), sem("silu_ready"), sem("ada_sum")
        lora_sq, lora_stat, lora_rms, lora_rs = (sem(n) for n in ("lora_sq", "lora_stat", "lora_rms", "lora_rs"))
        lora_norm, lora_hi, lora_ready = sem("lora_norm"), sem("lora_hi"), sem("lora_ready")
        kr_rope, kr_fold, kr_ready = sem("kr_rope"), sem("kr_fold"), sem("kr_ready")
        z_step, conv_y, conv_hi, conv_ready = sem("z_step"), sem("conv_y"), sem("conv_hi"), sem("conv_ready")
        gate_tanh = sem("gate_tanh")
        v_turned, v_ready = sem("v_turned"), sem("v_ready")
        s_done, mx_ready, nmax_ready, exp_ready = sem("s_done"), sem("mx_ready"), sem("nmax_ready"), sem("exp_ready")
        rinv_ready, p_ready, t_done, pt_ready = sem("rinv_ready"), sem("p_ready"), sem("t_done"), sem("pt_ready")
        o_done, o_hi_ready, o_ready = sem("o_done"), sem("o_hi_ready"), sem("o_ready")
        mg_ready, mg_hi, merged_ready = sem("mg_ready"), sem("mg_hi"), sem("merged_ready")
        p_hi_ready, p_split, ple_tanh, ple_step = sem("p_hi_ready"), sem("p_split"), sem("ple_tanh"), sem("ple_step")
        out_done = sem("out_done")

        block = ctx.enter_context(nc.Block())

        def norm_no(layer, e):
            return 4 * layer + e + 1

        ADDS = KD - 1
        LAYER_SUMS = 3 * KD + 2 * ADDS
        sums_x = lambda layer: ADDS + LAYER_SUMS * layer
        sums_done = lambda layer, e: sums_x(layer) + KD * (e + 1)
        sums_2 = lambda n: sums_x(DEPTH) + ADDS * (n - 9)
        sqs = lambda m: work(4 + m)
        sqs_gained = lambda m: ax(2 + m) if m < KD - 1 else ax(11)

        L2 = DEPTH
        xr, gr = (lambda j: ax(j)), (lambda j: ax(4 + j))
        KC, VC, KS, VS, KW, VW = (ax(8 + i) for i in range(6))
        q2 = lambda j: ax(14 + j)
        rms8 = ax(17)
        POST = 5
        gT = acc
        w1 = lambda kv, kt: gate_t[:, (kv * CMP_K + kt) * 2 * P:(kv * CMP_K + kt + 1) * 2 * P]
        pos2 = lambda kv: sq_t[:, 384 + 32 * kv:416 + 32 * kv]
        w2k = lambda m: sq_t[:, m * P:(m + 1) * P]
        w2v = lambda m: sq_t[:, 256 + 64 * m:320 + 64 * m]
        blocks = work_t[:, 14 * S:14 * S + CMP_K * 62]
        hid_x, hid_t = ax(8)[0:62, :], ax(9)[0:62, :]
        hid_c = acc[:, 0:248]
        hid = lambda kv, m: hid_c[:, (2 * kv + m) * 62:(2 * kv + m + 1) * 62]
        kcmp = cs_t[:, 0:N_CMP]
        vcmp = cs_t[0:N_CMP, 64:192]
        gcols = cs_t[:, 192:288]
        bias_c = ux_t[:, 8 * S:8 * S + HEADS * QT * N_CMP]
        vn_s, vn_w = ux(14), ux(15)
        pt_b = lambda par, k: work(8 + k) if par == 0 else gate(k)
        qbuf, p_c, pt_c = ux(10), ux_t[:, 12 * S:12 * S + QT * N_CMP], ux(13)

        @block.sync
        def _(sp):
            def load(slot, src):
                sp.wait_ge(w_lo_ready, slot.free)
                sp.dma_start(wt(raw, slot, slot.tiles), src).then_inc(raw_in[slot.pos], 16)

            sp.dma_start(work(0).bitcast(I32), I["positions"].partition_broadcast(P)).then_inc(const_in, 16)
            sp.dma_start(stat_t[:, 0:2], I["rope_consts"]).then_inc(const_in, 16)
            sp.dma_start(vec0, I["vec0"]).then_inc(vec0_in, 16)
            load(Slot(0, 0), I["first_slots"][0])
            for i in range(4):
                at = slice(2 * i * S, 2 * (i + 1) * S)
                sp.dma_start(h_t[:, at], I["x_t"][:, at]).then_inc(x_in[i], 16)

            def loads(layer, name, n, src, per=1):
                s0 = STAGE[name]
                if n > RING:
                    with sp.Fori(0, n // RING) as it:
                        for j in range(RING):
                            load(Slot(layer, s0 + j, it, RING), src(it * RING + j))
                else:
                    for j in range(n):
                        load(Slot(layer, s0 + j), src(j))

            def ffn(layer, f):
                name = f"ffn{f + 1}"
                for g, ft in enumerate(FF_GROUPS):
                    f0 = sum(FF_GROUPS[:g])
                    up_w = lambda i: I["ffn_gu"][f, layer, 2 * f0 + i]
                    first = (2 if g == 0 else 1) * RING if g < 2 else 0
                    for i in range(1 if f == 0 and g == 0 else 0, first):
                        load(Slot(layer, STAGE[f"{name}_up{g}"] + i), up_w(i))
                    if g < 2:
                        b = layer * 4 + f * 2 + g
                        if g == 0:
                            sp.wait_ge(slot_read, Slot(layer, STAGE[f"{name}_up0"]).done - 1)
                            sp.wait_ge(slot_done, Slot(layer, STAGE[f"{name}_up0"]).done - 1)
                            sp.dma_start(c_b, I["c_row"].partition_broadcast(P)).then_inc(c_in, 16)
                        sp.wait_ge(ada_done, b + 1)
                        sp.dma_start(gate_t[:, 0:ADA_BATCH * D], I["ada"][b]).then_inc(ada_in, 16)
                    with sp.Fori(0, 2 * ft // RING - first // RING) as it:
                        for j in range(RING):
                            load(Slot(layer, STAGE[f"{name}_up{g}"] + first + j, it, RING), up_w(first + it * RING + j))
                    if f == 0 and g == 0:
                        sp.wait_ge(u_ready, KD * (4 * layer + 1))
                        sp.dma_start(vec[:, :], I["vec"][layer]).then_inc(vec_in, 16)
                    dn = "dn8" if ft == KD else "dn6"
                    loads(layer, f"{name}_down{g}", KD, lambda i: I[f"{name}_{dn}"][layer, (KD * g if ft == KD else 0) + i])

            with sp.Fori(0, DEPTH) as layer:
                ffn(layer, 0)
                for i in range(6):
                    load(Slot(layer, STAGE["lora"] + i), I["in_w"][layer, i])
                loads(layer, "conv", 12, lambda i: I["in_w"][layer, i + 6])
                loads(layer, "gates", 16, lambda i: I["in_w"][layer, i + 18])
                with sp.Fori(0, HEADS) as hd:
                    for j in range(2):
                        load(Slot(layer, STAGE["heads"] + j, hd, 4), I["head_q"][layer, hd * 2 + j])
                    for j in range(2):
                        load(Slot(layer, STAGE["heads"] + 2 + j, hd, 4), I["head_kv"][layer, hd * 2 + j])
                with sp.Fori(0, KD // 2) as it:
                    for j in range(2):
                        load(Slot(layer, STAGE["branch_out"] + 2 * j, it, 4), I["conv_out"][layer, it * 2 + j])
                        load(Slot(layer, STAGE["branch_out"] + 2 * j + 1, it, 4), I["mla_out"][layer, it * 2 + j])
                sp.wait_ge(o_ready, 1 + HEADS * (layer + 1))
                sp.dma_start(work_t[:, 12 * S:14 * S].rearrange("p (t s) -> p t s", t=2), I["p_t"][layer]).then_inc(p_in, 16)
                loads(layer, "mix_out", KD, lambda i: I["mix_out"][layer, i])
                ffn(layer, 1)
                with sp.Fori(0, KD // 2) as it:
                    for j in range(2):
                        load(Slot(layer, STAGE["ple"] + 2 * j, it, 4), I["ple_gate"][layer, it * 2 + j])
                        load(Slot(layer, STAGE["ple"] + 2 * j + 1, it, 4), I["ple_proj"][layer, it * 2 + j])
                load(Slot(layer, LAYER_SLOTS), I["first_slots"][layer + 1])

            for j in range(1, RING):
                load(Slot(L2, j), I["in2"][j])
            sp.dma_start(col2[:, :], I["col2"]).then_inc(col2_in, 16)
            sp.wait_ge(slot_read, Slot(L2, 0).done - 1)
            sp.wait_ge(ple_step, KD * DEPTH)
            sp.dma_start(gate_t[:, :], I["cmp_w1"]).then_inc(w1_in, 16)
            sp.dma_start(work_t[:, 0:2 * S], I["lru_w"]).then_inc(b2_in, 16)
            sp.wait_ge(stat_done, 10)
            sp.dma_start(sq_t[:, 0:448], I["cmp_w2"]).then_inc(w2_in, 16)
            for j in range(4, IN2):
                load(Slot(L2, j), I["in2"][j])
            for m in range(KD):
                load(Slot(L2, B2_OUT + m), I["out2"][m])
            with sp.Fori(0, FF2_GROUPS) as g:
                for j in range(KD):
                    load(Slot(L2, B2_FF + j, g, 2 * KD), I["ff1"][g * KD + j])
                for m in range(KD):
                    load(Slot(L2, B2_FF + KD + m, g, 2 * KD), I["ff2"][g * KD + m])
            for m in range(KD):
                if m < POST:
                    sp.wait_ge(h_out, m + 1)
                else:
                    sp.wait_ge(h_out_pool, m + 1 - POST)
                sp.dma_start(out_t[:, m, :], h(m)).then_inc(out_done, 16)
            sp.wait_ge(out_done, 16 * KD)

        @block.gpsimd
        def _(pool):
            pool.memset(ones[:, :], 1.0).then_inc(consts_ready, 1)
            pool.memset(ident[:, :], 0.0).then_inc(consts_ready, 1)
            pool.memset(fold[:, :], 0.0).then_inc(consts_ready, 1)
            pool.memset(cmask, 0.0).then_inc(consts_ready, 1)
            pool.memset(eps_t[:, :], EPS).then_inc(consts_ready, 1)
            pool.wait_ge(consts_ready, 5)
            pool.memset(cmask[0:64, 64:P], NEG).then_inc(consts_ready, 1)
            pool.affine_select(out=ident[:, :], in_=ident[:, :], compare_op=ALU.not_equal, fill=1.0, base=0,
                               pattern=[[-1, P]], channel_multiplier=1).then_inc(consts_ready, 1)
            for i, off in enumerate((0, 64, -64)):
                pool.affine_select(out=fold[:, :], in_=fold[:, :], compare_op=ALU.not_equal, fill=1.0, base=off,
                                   pattern=[[-1, P]], channel_multiplier=1).then_inc(consts_ready, 1)
                pool.wait_ge(consts_ready, 8 + i)
            pool.tensor_copy(ident_r[:, :], ident[:, :]).then_inc(consts_ready, 1)
            pool.tensor_copy(cmask_r[:, :], cmask).then_inc(consts_ready, 1)

            def squares(n, i, start, ready, x=h):
                for m in range(KD):
                    ready(m)
                    if m == 0:
                        if not isinstance(n, int) or n:
                            pool.wait_ge(rs_ready, n)
                        pool.tensor_tensor(acc, x(0), x(0), ALU.mult).then_inc(sum_ready, 1)
                        continue
                    pool.wait_ge(sum_ready, start + m)
                    pool.tensor_tensor(sq, x(m), x(m), ALU.mult).then_inc(sq_ready, 1)
                    pool.wait_ge(sq_ready, i * (KD - 1) + m)
                    pool.tensor_tensor(acc, acc, sq, ALU.add).then_inc(sum_ready, 1)

            def sums(start, squares_done, src, free=None):
                for m in range(1, KD):
                    pool.wait_ge(sqs_ready, squares_done + m + 1)
                    if m == 1 and free:
                        free()
                    if m > 1:
                        pool.wait_ge(sum_ready, start + m - 1)
                    pool.tensor_tensor(acc, src(0) if m == 1 else acc, src(m), ALU.add).then_inc(sum_ready, 1)

            sums(0, 0, sqs)
            with pool.Fori(0, DEPTH) as layer:
                for e, name in enumerate(("ffn1_down2", "mix_out", "ffn2_down2")):
                    squares(norm_no(layer, e), 3 * layer + e, sums_done(layer, e) - KD,
                            lambda m: pool.wait_ge(slot_read, Slot(layer, STAGE[name] + m).done))
                start = sums_done(layer, 2)
                pool.wait_ge(rs_ready, norm_no(layer, 3))
                for m in range(1, KD):
                    pool.wait_ge(sqs_ready, KD + 2 * KD * layer + 2 * (m + 1))
                    pool.wait_ge(sum_ready, start + 2 * (m - 1))
                    pool.tensor_tensor(acc, sqs(0) if m == 1 else acc, sqs(m), ALU.add).then_inc(sum_ready, 1)
                    pool.tensor_tensor(sq, sqs_gained(0) if m == 1 else sq, sqs_gained(m), ALU.add).then_inc(sum_ready, 1)

            pool.wait_ge(rg_tanh, 8)
            pool.iota(work(1), [[-1, S]], base=S - P, channel_multiplier=1, allow_small_or_imprecise_dtypes=True)\
                .then_inc(bias_step, 1)
            pool.iota(work(0)[:, 0:QT * N_CMP], [[P, QT], [-16, N_CMP]], base=-31, channel_multiplier=1,
                      allow_small_or_imprecise_dtypes=True).then_inc(bias_step, 1)
            pool.wait_ge(bias_step, 2)
            pool.affine_select(out=work(1), in_=work(1), compare_op=ALU.is_ge, fill=FAR, base=S - P,
                               pattern=[[-1, S]], channel_multiplier=1).then_inc(dist_ready, 1)
            dist_c = work(0)[:, 0:QT * N_CMP]
            pool.affine_select(out=dist_c, in_=dist_c, compare_op=ALU.is_ge, fill=FAR, base=-31,
                               pattern=[[P, QT], [-16, N_CMP]], channel_multiplier=1).then_inc(dist_ready, 1)
            pool.wait_ge(g_cols, 1)
            pool.affine_select(out=gcols[:, 0:HEADS], in_=gcols[:, 0:HEADS], compare_op=ALU.is_ge, fill=0.0, base=-31,
                               pattern=[[0, HEADS]], channel_multiplier=1).then_inc(g_ready, 1)
            sums(sums_2(9), 5 * KD, lambda m: work(8 + m), lambda: pool.wait_ge(slot_read, Slot(L2, B2_OUT).done))
            pool.wait_ge(h2_ready, KD)
            for m in range(KD):
                pool.memset(gate(m), 0.0).then_inc(y_zero, 1)
            sums(sums_2(10), 7 * KD, lambda m: work(8 + m), lambda: pool.wait_ge(rs_ready, 11))
            pool.wait_ge(rs_ready, 13)
            pool.wait_ge(y_scaled, 2 * KD)
            pool.wait_ge(hf_ready, 2 * KD)
            for m in range(POST, KD):
                pool.tensor_tensor(gate(m), gate(m), rs, ALU.mult).then_inc(y_timed_pool, 1)
                pool.wait_ge(y_timed_pool, m + 1 - POST)
                pool.tensor_tensor(h(m), h(m), gate(m), ALU.add).then_inc(h_out_pool, 1)

        @block.scalar
        def _(act):
            def split_hi(slot):
                act.wait_ge(raw_in[slot.pos], slot.loads)
                act.wait_ge(slot_done, slot.free)
                act.activation(wt(w_hi, slot, slot.tiles), wt(raw, slot, slot.tiles), ACT.Copy)\
                   .then_inc(w_hi_ready, slot.inc)

            def prep_hi(n, m, gain, slot):
                if slot is not None:
                    act.wait_ge(slot_read, slot.done)
                act.activation(u_hi(m), h(m), ACT.Copy, scale=gain[:, m:m + 1]).then_inc(u_hi_ready, 1)

            def rms(n, src=ot, width=D):
                act.wait_ge(stat_done, n + 1)
                act.activation(acc, src[:, :], ACT.Sqrt, scale=1.0 / width, bias=eps_t[:, 0:1]).then_inc(rms_ready, 1)

            split_hi(Slot(0, 0))
            act.wait_ge(vec0_in, 16)
            for m in range(KD):
                act.wait_ge(x_in[m // 2], 16)
                prep_hi(0, m, vec0, None)
                act.activation(sqs(m), h(m), ACT.Square).then_inc(sqs_ready, 1)
            split_hi(Slot(0, 1))
            act.wait_ge(pos_ready, 1)
            act.activation(cs, work(0), ACT.Sin).then_inc(sin_ready, 1)

            def ffn(layer, f, e):
                name = f"ffn{f + 1}"
                no = layer * 2 + f
                for g, ft in enumerate(FF_GROUPS):
                    s0 = STAGE[f"{name}_up{g}"]
                    f0 = sum(FF_GROUPS[:g])
                    if g == 0:
                        rms(norm_no(layer, e) - 1)

                    def up(it):
                        for q in range(2):
                            i = no * FF_TILES + f0 + 2 * it + q + 1
                            split_hi(Slot(layer, s0 + 2 * q + AHEAD, it, RING))
                            gated = Slot(layer, s0 + 2 * q, it, RING)
                            act.wait_ge(slot_read, gated.done)
                            act.activation(work(2 + q), work(q), ACT.Tanh, scale=0.5).then_inc(tanh_ready, 1)
                            split_hi(Slot(layer, s0 + 2 * q + 1 + AHEAD, it, RING))
                            act.wait_ge(act_ready, i)
                            act.activation(a_hi_t[:, bass.ds((2 * it + q) * S, S)], work(8 + q), ACT.Copy)\
                               .then_inc(a_hi_ready, 1)
                    repeat(act, s0, ft // 2, RING, up)
                    if g == 0:
                        act.wait_ge(c_in, 16 * (no + 1))
                        act.activation(c_th, c_b, ACT.Tanh, scale=0.5).then_inc(c_tanh, 1)
                    s0 = STAGE[f"{name}_down{g}"]
                    if g < 2:
                        def down(it):
                            for j in range(RING):
                                split_hi(Slot(layer, s0 + j + AHEAD, it, RING))
                        repeat(act, s0, KD // RING, RING, down)
                        continue
                    act.wait_ge(vec_in, 16 * (layer + 1))
                    for m in range(KD):
                        split_hi(Slot(layer, s0 + m + AHEAD))
                        prep_hi(norm_no(layer, e), m, vec[:, (V_MIX if f == 0 else V_PLE):], Slot(layer, s0 + m))

            def exp(n, qt):
                act.wait_ge(nmax_ready, n * QT + QT - qt)
                act.activation(work_t[:, (9 + qt % 2) * S:(9 + qt % 2) * S + (qt + 1) * P], sc[:, qt % 2, 0:(qt + 1) * P],
                               ACT.Exp, bias=stat_t[:, 8 + qt:9 + qt], scale=SCALE1,
                               accum_out=stat_t[:, 16 + qt:17 + qt]).then_inc(exp_ready, 1)

            def core(layer, hd, slots):
                n = layer * HEADS + hd
                split = (lambda j: split_hi(slots[j])) if slots else (lambda j: None)
                copy_pt(n, 3)
                exp(n, 1)
                split(0)
                copy_pt(n, 2)
                exp(n, 0)
                split(1)
                copy_pt(n, 1)
                split(2)
                split(3)
                copy_pt(n, 0)
                if slots:
                    exp(n + 1, 3)
                    exp(n + 1, 2)
                act.wait_ge(o_done, n + 1)
                act.activation(u_hi_t[:, bass.ds(hd * S, S)], ot[:, :], ACT.Copy).then_inc(o_hi_ready, 1)

            def copy_pt(n, qt):
                act.wait_ge(t_done, n * QT + QT - qt)
                dst = work_t[:, 11 * S:15 * S].rearrange("p (k s) -> p k s", s=S)[:, 0:qt + 1, qt * P:(qt + 1) * P]
                act.activation(dst, tr[:, 0:(qt + 1) * P].rearrange("p (k s) -> p k s", s=P), ACT.Copy)\
                   .then_inc(pt_ready, 1)

            with act.Fori(0, DEPTH) as layer:
                ffn(layer, 0, 0)
                rms(norm_no(layer, 0))
                s0 = STAGE["lora"]
                for j in range(6):
                    split_hi(Slot(layer, s0 + j + AHEAD))
                    if j < 5:
                        act.wait_ge(slot_read, Slot(layer, s0 + j).done)
                        act.activation(work(8 if j == 4 else 11 + j), work(j), ACT.Square).then_inc(lora_sq, 1)
                s0 = STAGE["conv"]
                for j in range(12):
                    split_hi(Slot(layer, s0 + j + AHEAD))
                    if j == 0:
                        act.wait_ge(lora_stat, 2 * layer + 1)
                        act.activation(work(11), ot[:, :], ACT.Sqrt, scale=1.0 / Q_LORA, bias=eps_t[:, 0:1])\
                           .then_inc(lora_rms, 1)
                        act.wait_ge(lora_stat, 2 * layer + 2)
                        act.activation(work(13), tr[:, :], ACT.Sqrt, scale=1.0 / KV_LORA, bias=eps_t[:, 0:1])\
                           .then_inc(lora_rms, 1)
                    if j >= 3 and j < 8:
                        act.wait_ge(lora_norm, 5 * layer + j - 2)
                        act.activation(a_hi(j - 3), work(j - 3), ACT.Copy).then_inc(lora_hi, 1)
                    if j % 3 == 2:
                        act.wait_ge(conv_y, 4 * layer + j // 3 + 1)
                        act.activation(a_hi(5 + j // 3), work(7), ACT.Copy).then_inc(conv_hi, 1)
                s0 = STAGE["gates"]

                def gates(it):
                    for j in range(RING):
                        split_hi(Slot(layer, s0 + j + AHEAD, it, RING))
                        act.wait_ge(slot_read, Slot(layer, s0 + j, it, RING).done)
                        act.activation(gate_t[:, bass.ds((it * RING + j) * S, S)], work(13 + j % 2), ACT.Tanh,
                                       scale=0.5).then_inc(gate_tanh, 1)
                repeat(act, s0, 4, RING, gates)
                s0 = STAGE["heads"]
                for j in range(4):
                    split_hi(Slot(layer, s0 + j + AHEAD))
                exp(layer * HEADS, 3)
                exp(layer * HEADS, 2)

                def heads(it):
                    for q in range(2):
                        last = isinstance(it, int) and q == 1
                        slots = [Slot(layer, s0 + 4 * (q + 1) + j + AHEAD + (24 if isinstance(it, int) else 0),
                                      0 if isinstance(it, int) else it, 8) for j in range(4)]
                        core(layer, 2 * it + q, None if last else slots)
                with act.Fori(0, HEADS // 2 - 1) as it:
                    heads(it)
                heads(HEADS // 2 - 1)
                s0 = STAGE["branch_out"]
                for m in range(KD):
                    split_hi(Slot(layer, s0 + 2 * m + AHEAD))
                    split_hi(Slot(layer, s0 + 2 * m + 1 + AHEAD))
                    act.wait_ge(mg_ready, KD * layer + m + 1)
                    act.activation(merged_hi(m), work(4 + m % 2), ACT.Copy).then_inc(mg_hi, 1)
                s0 = STAGE["mix_out"]
                for m in range(KD):
                    split_hi(Slot(layer, s0 + m + AHEAD))
                    prep_hi(norm_no(layer, 1), m, vec[:, V_FFN2:], Slot(layer, s0 + m))
                ffn(layer, 1, 2)
                act.wait_ge(p_in, 16 * (layer + 1))
                act.wait_ge(slot_read, Slot(layer, STAGE["ple"]).done - 1)
                act.activation(a_hi_t[:, 0:2 * S], work_t[:, 12 * S:14 * S], ACT.Copy).then_inc(p_hi_ready, 1)
                s0 = STAGE["ple"]
                gain = lambda m: vec[:, V_NEXT + m:V_NEXT + m + 1]

                def square(m):
                    act.wait_ge(ple_step, KD * layer + m + 1)
                    act.activation(sqs(m), h(m), ACT.Square).then_inc(sqs_ready, 1)
                    act.activation(sqs_gained(m), h(m), ACT.Square, scale=gain(m)).then_inc(sqs_ready, 1)
                for m in range(KD):
                    end = m == KD - 1
                    if m == 0:
                        split_hi(Slot(layer, s0 + AHEAD))
                        split_hi(Slot(layer, s0 + AHEAD + 1))
                        rms(norm_no(layer, 2))
                        split_hi(Slot(layer, s0 + AHEAD + 2))
                    elif 1 < m < KD - 1:
                        split_hi(Slot(layer, s0 + 2 * m + AHEAD))
                    act.wait_ge(slot_read, Slot(layer, s0 + 2 * m).done)
                    act.activation(gate(m), work(m % 2), ACT.Tanh, scale=0.5).then_inc(ple_tanh, 1)
                    if m:
                        split_hi(Slot(layer, s0 + 2 * m + (0 if end else 1) + AHEAD))
                    if 0 < m < KD - 1:
                        square(m - 1)
                next_hi = lambda m: act.activation(u_hi(m), h(m), ACT.Copy, scale=gain(m)).then_inc(u_hi_ready, 1)
                next_hi(0)
                square(KD - 2)
                next_hi(1)
                square(KD - 1)
                split_hi(Slot(layer, LAYER_SLOTS + 1))
                for m in range(2, KD):
                    next_hi(m)

            def ahead(s):
                if s + AHEAD < B2_SLOTS:
                    split_hi(Slot(L2, s + AHEAD))

            def shifted(n, sh):
                for m in range(KD + 1):
                    if m < KD:
                        act.activation(work(2 + m), acc, ACT.Copy, scale=mod_t[:, sh + m:sh + m + 1]).then_inc(sh_ready, 1)
                    if m:
                        act.wait_ge(tmp_ready, KD * (n == 11) + m)
                        act.activation(u_hi(m - 1), work(1 + m), ACT.Copy).then_inc(u_hi_ready, 1)

            act.wait_ge(comb_ready, 2)
            act.activation(acc, rs, ACT.Sqrt, scale=1.0 / D).then_inc(rms_ready, 1)
            act.wait_ge(rms_ready, 9)
            shifted(9, 0)
            act.activation(rms8, ot[:, :], ACT.Sqrt, scale=1.0 / D, bias=eps_t[:, 0:1]).then_inc(rms_ready, 1)
            for s in range(IN2):
                ahead(s)
                if s == 2:
                    act.wait_ge(pos_ready, 2)
                    act.activation(small2[:, 8:12], small2[:, 8:12], ACT.Exp, scale=-1.0).then_inc(lam_exp, 1)
                if 5 <= s <= 8:
                    j = s - 5
                    act.wait_ge(mods_ready, 1)
                    act.wait_ge(rg_done, j + 1)
                    act.activation(work(6 + j), sc[:, 0, :], ACT.Tanh, scale=0.5, bias=small2[:, 20 + j:21 + j]).then_inc(rg_tanh, 1)
                    act.activation(work(10 + j), sc[:, 1, :], ACT.Tanh, scale=0.5, bias=small2[:, 24 + j:25 + j]).then_inc(rg_tanh, 1)
                if 7 <= s <= 10:
                    j = s - 7
                    act.wait_ge(la_ready, j + 1)
                    if j >= 2:
                        act.wait_ge(v2_ready, j - 1)
                    act.activation(work(14 + j % 2), work(6 + j), ACT.Exp, scale=2.0).then_inc(decay_ready, 1)
                    act.activation(xr(j), work(6 + j), ACT.Exp).then_inc(decay_ready, 1)
                    act.wait_ge(decay_ready, 3 * j + 2)
                    act.activation(work(6 + j), work(6 + j), ACT.Tanh, scale=-1.0).then_inc(decay_ready, 1)
                if s == 12:
                    for j in range(4):
                        act.wait_ge(v2_ready, j + 1)
                        act.activation(work(6 + j), work(6 + j), ACT.Sqrt).then_inc(sqrt_ready, 1)
                if s == 15:
                    act.wait_ge(slot_read, Slot(L2, 14).done)
                    act.activation(gT, gT, ACT.Tanh, scale=0.5).then_inc(g_tanh, 1)
                if 13 <= s <= 16:
                    j = s - 13
                    act.wait_ge(ix_ready, 4)
                    act.activation(work(2 + j), gr(j), ACT.Square).then_inc(gel_sq, 1)
                if 14 <= s <= 17:
                    j = s - 14
                    act.wait_ge(gel_in, j + 1)
                    act.activation(work(2 + j), work(2 + j), ACT.Tanh, scale=0.7978845608028654).then_inc(gel_tanh, 1)
                if s == 17:
                    act.wait_ge(hid_in, 1)
                    act.activation(hid_t, hid_t, ACT.Tanh, scale=0.7978845608028654).then_inc(hid_tanh, 1)
            act.wait_ge(dist_ready, 2)
            act.wait_ge(slot_done, Slot(L2, IN2 - 1).done)
            for n in range(HEADS):
                head = 4 * (n % 2) + n // 2
                bc = bias_c[:, head * QT * N_CMP:(head + 1) * QT * N_CMP]
                act.activation(bc, work(0)[:, 0:QT * N_CMP], ACT.Copy, scale=-SLOPES[head]).then_inc(bias_ready, 1)
                act.activation(u_hi(head), work(1), ACT.Copy, scale=-SLOPES[head]).then_inc(bias_ready, 1)

            def copy_pt2(n, par, qt):
                for br, bank in enumerate((tr[:, :], proj[:, 3, :])):
                    act.wait_ge(t2_done, 2 * (n * QT + QT - 1 - qt) + br + 1)
                    to = pt_b(par, 0) if br else work(4)
                    dst = bass.AP(to.tensor, to.offset + qt * P, [to.ap[0], (S, qt + 1), (1, P)])
                    act.activation(dst, bank[:, 0:(qt + 1) * P].rearrange("p (k s) -> p k s", s=P), ACT.Copy).then_inc(pt2_ready, 1)

            def exp_2(n, qt):
                w, q = (qt + 1) * P, qt % 2
                act.wait_ge(nmax2, n * QT + QT - qt)
                for br, bank in enumerate((sc, proj)):
                    act.activation(work(2 * br + q)[:, 0:w], bank[:, q, 0:w], ACT.Exp,
                                   bias=stat_t[:, 8 + 2 * q + br:9 + 2 * q + br],
                                   accum_out=stat_t[:, 12 + 2 * q + br:13 + 2 * q + br]).then_inc(exp2, 1)

            def enter2(n):
                exp_2(n, 3)
                act.wait_ge(cs_sub, n + 1)
                act.activation(p_c, p_c, ACT.Exp).then_inc(cs_exp, 1)
                exp_2(n, 2)

            def core2(j, par, last):
                n = 2 * j + par
                copy_pt2(n, par, 3)
                exp_2(n, 1)
                copy_pt2(n, par, 2)
                exp_2(n, 0)
                act.wait_ge(tc_done, n + 2)
                act.activation(pt_c[0:N_CMP, :], proj[0:N_CMP, 2, :], ACT.Copy).then_inc(ptc_ready, 1)
                copy_pt2(n, par, 1)
                copy_pt2(n, par, 0)
                if not last:
                    enter2(n + 1)

            act.wait_ge(bias_ready, 2 * HEADS)
            enter2(0)
            with act.Fori(0, QT - 1) as j:
                core2(j, 0, False)
                core2(j, 1, False)
            core2(QT - 1, 0, False)
            core2(QT - 1, 1, True)
            for k in range(KD):
                if k == 4:
                    act.wait_ge(o2_ready, 2 + HEADS)
                act.wait_ge(rnn_ready, 4)
                if k == 0:
                    act.wait_ge(o2_done, HEADS)
                act.activation(work(k), gr(k) if k < 4 else work(8 + k), ACT.Square).then_inc(mix_sq, 1)
            for i in range(2):
                act.wait_ge(mix_stat, i + 1)
                act.activation(work(8 + i), sc[:, i, :], ACT.Sqrt, scale=1.0 / 512, bias=eps_t[:, 0:1]).then_inc(mix_rms, 1)
            for k in range(KD):
                act.wait_ge(mix_norm, k + 1)
                act.activation(u_hi(k), gr(k) if k < 4 else work(8 + k), ACT.Copy).then_inc(u_hi_ready, 1)
            for m in range(KD):
                ahead(B2_OUT + m)
                act.wait_ge(slot_read, Slot(L2, B2_OUT + m).done)
                act.activation(work(8 + m), gate(m), ACT.Square).then_inc(sqs_ready, 1)
                act.activation(gate(m), gate(m), ACT.Copy, scale=modc[:, 8 + m:9 + m]).then_inc(y_scaled, 1)
            act.wait_ge(comb_ready, 3)
            act.activation(sq, rs, ACT.Sqrt, scale=1.0 / D).then_inc(rms_ready, 1)
            for m in range(KD):
                act.wait_ge(h2_ready, m + 1)
                act.activation(ax(8 + m), h(m), ACT.Square).then_inc(sqs_ready, 1)
            act.wait_ge(comb_ready, 5)
            act.activation(acc, rs, ACT.Sqrt, scale=1.0 / D).then_inc(rms_ready, 1)
            act.wait_ge(rms_ready, 12)
            shifted(11, 24)

            def ff(g):
                end = isinstance(g, int)
                for i in range(2 * KD):
                    if not (end and i >= 2 * KD - AHEAD):
                        split_hi(Slot(L2, B2_FF + i + AHEAD, g, 2 * KD))
                    if i < KD:
                        act.wait_ge(slot_read, Slot(L2, B2_FF + i, g, 2 * KD).done)
                        act.activation(work(4 + i % 4), work(i % 4), ACT.Square).then_inc(relu_sq, 1)
                        act.wait_ge(relu_sq, KD * g + i + 1)
                        act.activation(a_hi(i), work(4 + i % 4), ACT.Copy).then_inc(a_hi_ready, 1)
                    elif end:
                        act.wait_ge(slot_read, Slot(L2, B2_FF + i, g, 2 * KD).done)
                        m = i - KD
                        act.activation(work(i), gate(m), ACT.Square).then_inc(sqs_ready, 1)
                        act.activation(gate(m), gate(m), ACT.Copy, scale=modc[:, 24 + m:25 + m]).then_inc(y_scaled, 1)
            with act.Fori(0, FF2_GROUPS - 1) as g:
                ff(g)
            ff(FF2_GROUPS - 1)
            rms(12)

        @block.tensor
        def _(pe):
            def three(out, w_h, w_l, x_h, x_l, first, last):
                pe.matmul(out, w_h, x_h, start=first, stop=False)
                pe.matmul(out, w_h, x_l, start=False, stop=False)
                return pe.matmul(out, w_l, x_h, start=False, stop=last)

            def slot_mm(slot, operand, before=None):
                pe.wait_ge(w_lo_ready, slot.done)
                pe.wait_ge(slot_read, slot.free)
                for k in range(slot.tiles):
                    if before:
                        before(k)
                    x_h, x_l = operand(k)
                    mm = three(proj[:, slot.pos, :], wt(w_hi, slot, 1, k), wt(w_lo, slot, 1, k), x_h, x_l,
                               k == 0, k == slot.tiles - 1)
                mm.then_inc(slot_done, slot.inc)

            u_of = lambda k: (u_hi(k), u_lo(k))
            a_of = lambda k: (a_hi(k), a_lo(k))

            def stat(n, done):
                pe.wait_ge(sum_ready, done)
                pe.matmul(ot[:, :], ones[:, :], acc, start=True, stop=True).then_inc(stat_done, 1)

            def first_u(n, slot, done):
                slot_mm(slot, u_of, lambda k: pe.wait_ge(u_ready, n * KD + k + 1))
                stat(n, done)

            pe.wait_ge(consts_ready, 12)

            def ffn(layer, f, e):
                name = f"ffn{f + 1}"
                no = layer * 2 + f
                for g, ft in enumerate(FF_GROUPS):
                    s0 = STAGE[f"{name}_up{g}"]
                    if g == 0:
                        first_u(norm_no(layer, e) - 1, Slot(layer, s0), sums_done(layer, 1) if f else sums_x(layer))
                        for j in range(1, RING):
                            slot_mm(Slot(layer, s0 + j), u_of)
                        s0 += RING
                    with pe.Fori(0, ft // 2 - (g == 0)) as it:
                        for j in range(RING):
                            slot_mm(Slot(layer, s0 + j, it, RING), u_of)
                    s0 = STAGE[f"{name}_down{g}"]
                    f0 = no * FF_TILES + sum(FF_GROUPS[:g])
                    with pe.Fori(0, KD // RING) as it:
                        for j in range(RING):
                            slot_mm(Slot(layer, s0 + j, it, RING), a_of,
                                    (lambda k: pe.wait_ge(a_lo_ready, f0 + k + 1)) if j == 0 else None)

            def scores(n, q, qt):
                w = (qt + 1) * P
                pe.wait_ge(exp_ready, n * QT + QT - qt)
                pe.matmul(sc[:, qt % 2, 0:w], work(q)[:, qt * P:w], work(4 + q)[:, 0:w], start=True, stop=False)
                pe.matmul(sc[:, qt % 2, qt * P:w], ident_r[:, :], cmask_r[:, :], start=False, stop=False)
                pe.matmul(sc[:, qt % 2, 0:w], work(2 + q)[:, qt * P:w], work(15)[:, 0:w], start=False, stop=True)\
                  .then_inc(s_done, 1)

            def turn(n, qt):
                pe.wait_ge(p_ready, n * QT + QT - qt)
                if qt == QT - 1:
                    pe.wait_ge(v_ready, n + 1)
                else:
                    pe.wait_ge(pt_ready, n * QT + QT - qt)
                for k in range(qt + 1):
                    mm = pe.transpose(tr[:, k * P:(k + 1) * P], work(9 + qt % 2)[:, k * P:(k + 1) * P], ident[:, :])
                mm.then_inc(t_done, 1)

            def enter(layer, hd, q):
                n = layer * HEADS + hd
                last = Slot(layer, STAGE["heads"]).number + RING + 4 * (hd + 1)
                pe.wait_ge(slot_read, last - 1)
                scores(n, q, 3)
                scores(n, q, 2)
                pe.wait_ge(slot_read, last)
                pe.wait_ge(pt_ready, n * QT + 1)
                for t in range(QT):
                    mm = pe.transpose(tr[:, t * P:(t + 1) * P], work(6)[:, t * P:(t + 1) * P], ident[:, :])
                mm.then_inc(v_turned, 1)

            def core(layer, hd, q, slots):
                n = layer * HEADS + hd
                run = [lambda s=s, j=j: slot_mm(s, (lambda k: (a_hi(k), a_lo(k))) if j < 2 else
                                                (lambda k: (a_hi(3 + k), a_lo(3 + k))))
                       for j, s in enumerate(slots)] if slots else [lambda: None] * 4
                turn(n, 3)
                scores(n, q, 1)
                run[0]()
                turn(n, 2)
                scores(n, q, 0)
                run[1]()
                turn(n, 1)
                run[2]()
                run[3]()
                turn(n, 0)
                if slots:
                    enter(layer, hd + 1, 1 - q)
                pe.wait_ge(pt_ready, n * QT + QT + 1)
                pe.wait_ge(o_ready, n + 1)
                for k in range(QT):
                    mm = pe.matmul(ot[:, k * P:S], work(7 + q)[:, k * P:(k + 1) * P], work(11 + k)[:, k * P:S],
                                   start=k == 0, stop=True, skip_group_check=True)
                mm.then_inc(o_done, 1)

            with pe.Fori(0, DEPTH) as layer:
                ffn(layer, 0, 0)
                s0 = STAGE["lora"]
                first_u(norm_no(layer, 0), Slot(layer, s0), sums_done(layer, 0))
                for j in range(1, 6):
                    slot_mm(Slot(layer, s0 + j), u_of)
                pe.wait_ge(rms_ready, norm_no(layer, 0) + 1)
                for j in range(5):
                    pe.wait_ge(lora_sq, 5 * layer + j + 1)
                    bank = ot if j < 3 else tr
                    mm = pe.matmul(bank[:, :], ones[:, :], work(8 if j == 4 else 11 + j), start=j in (0, 3), stop=j in (2, 4))
                    if j in (2, 4):
                        mm.then_inc(lora_stat, 1)
                s0 = STAGE["conv"]
                for j in range(12):
                    slot_mm(Slot(layer, s0 + j), u_of)
                    if j == 0:
                        pe.wait_ge(kr_rope, layer + 1)
                        pe.matmul(sc[:, 0, :], fold[:, :], work(5), start=True, stop=True).then_inc(kr_fold, 1)
                s0 = STAGE["gates"]
                with pe.Fori(0, 4) as it:
                    for j in range(RING):
                        slot_mm(Slot(layer, s0 + j, it, RING), u_of)
                s0 = STAGE["heads"]
                pe.wait_ge(lora_ready, 5 * (layer + 1))
                pe.wait_ge(kr_ready, layer + 1)
                for j in range(4):
                    slot_mm(Slot(layer, s0 + j), lambda k, o=0 if j < 2 else 3: (a_hi(o + k), a_lo(o + k)))
                enter(layer, 0, 0)
                with pe.Fori(0, HEADS // 2 - 1) as it:
                    for q in range(2):
                        core(layer, 2 * it + q, q, [Slot(layer, s0 + 4 * (q + 1) + j, it, 8) for j in range(4)])
                core(layer, HEADS - 2, 0, [Slot(layer, s0 + 28 + j) for j in range(4)])
                core(layer, HEADS - 1, 1, None)
                s0 = STAGE["branch_out"]
                pe.wait_ge(conv_ready, 1 + 4 * (layer + 1))
                slot_mm(Slot(layer, s0), lambda k: (a_hi(5 + k), a_lo(5 + k)))
                pe.wait_ge(o_ready, 1 + HEADS * (layer + 1))
                for m in range(KD):
                    if m:
                        slot_mm(Slot(layer, s0 + 2 * m), lambda k: (a_hi(5 + k), a_lo(5 + k)))
                    slot_mm(Slot(layer, s0 + 2 * m + 1), u_of)
                s0 = STAGE["mix_out"]
                slot_mm(Slot(layer, s0), lambda k: (merged_hi(k), merged_lo(k)),
                        lambda k: pe.wait_ge(merged_ready, KD * layer + k + 1))
                for m in range(1, KD):
                    slot_mm(Slot(layer, s0 + m), lambda k: (merged_hi(k), merged_lo(k)))
                ffn(layer, 1, 2)
                s0 = STAGE["ple"]
                first_u(norm_no(layer, 2), Slot(layer, s0), sums_done(layer, 2))
                for m in range(KD):
                    if m:
                        slot_mm(Slot(layer, s0 + 2 * m), u_of)
                    else:
                        pe.wait_ge(p_split, layer + 1)
                    slot_mm(Slot(layer, s0 + 2 * m + 1), a_of)

            stat(8, sums_x(DEPTH))
            pe.matmul(tr[:, :], ones[:, :], sq, start=True, stop=True).then_inc(stat_done, 1)
            for s in range(IN2):
                slot_mm(Slot(L2, s), u_of, (lambda k: pe.wait_ge(u_ready, 9 * KD + k + 1)) if s == 0 else None)
                if 5 <= s <= 8:
                    j = s - 5
                    pe.wait_ge(b2_in, 16)
                    pe.wait_ge(xf_ready, j + 1)
                    if j:
                        pe.wait_ge(rg_tanh, 2 * j)
                    pe.matmul(sc[:, 0, :], work_t[:, j * P:(j + 1) * P], work(2 + j), start=True, stop=True)
                    pe.matmul(sc[:, 1, :], work_t[:, (4 + j) * P:(5 + j) * P], work(2 + j), start=True, stop=True)\
                      .then_inc(rg_done, 1)
                if s in (14, 16):
                    kv = (s - 14) // 2
                    pe.wait_ge(w1_in, 16)
                    pe.wait_ge(x_built, 4 * (kv + 1))
                    for kt in range(CMP_K):
                        mm = pe.matmul(ot[0:62, kv * 2 * P:(kv + 1) * 2 * P], blocks[:, kt * 62:(kt + 1) * 62], w1(kv, kt),
                                       start=kt == 0, stop=kt == CMP_K - 1)
                    mm.then_inc(hid_part, 1)
                if s == 16:
                    pe.wait_ge(g_tanh, 1)
                    for t in range(QT):
                        mm = pe.transpose(tr[:, t * P:(t + 1) * P], gT[:, t * P:(t + 1) * P], ident[:, :])
                    mm.then_inc(g_turned, 1)
                if s == 17:
                    for i, v in enumerate((VS, VW)):
                        for t in range(QT):
                            mm = pe.transpose(sc[:, i, t * P:(t + 1) * P], v[:, t * P:(t + 1) * P], ident[:, :])
                        mm.then_inc(v2_turned, 1)
            pe.wait_ge(hid_ready, 1)
            pe.wait_ge(g_cols, 1)
            for i in range(4):
                mm = pe.transpose(tr[:, i * 62:(i + 1) * 62], hid_x[:, i * P:(i + 1) * P], ident[0:62, 0:62])
            mm.then_inc(hid_turned, 1)
            pe.wait_ge(hid_cols, 1)
            for m in range(2):
                pe.matmul(proj[:, 0, 0:62], w2k(m), hid(0, m), start=m == 0, stop=m == 1)
            for g in range(2):
                for m in range(2):
                    mm = pe.matmul(proj[0:N_CMP, 3, g * 64:(g + 1) * 64], hid(1, m)[:, g * N_CMP:(g + 1) * N_CMP], w2v(m),
                                   start=m == 0, stop=m == 1)
            mm.then_inc(kv_cmp_done, 1)
            pe.wait_ge(kv_cmp_ready, 3)
            pe.wait_ge(v2_copied, 2)

            half = lambda par: slice(64 * par, 64 * par + 64)

            def scores2(n, j, par, qt):
                w = (qt + 1) * P
                for br, (k, bank) in enumerate(((KS, sc), (KW, proj))):
                    pe.wait_ge(exp2, 2 * (n * QT + QT - 1 - qt) + br + 1)
                    pe.matmul(bank[:, qt % 2, 0:w], ident_r[:, :], u_hi_t[:, bass.ds((4 * par + j) * S + S - w, w)],
                              start=True, stop=False)
                    pe.matmul(bank[:, qt % 2, 0:w], qbuf[half(par), qt * P:w], k[half(par), 0:w], start=False, stop=True)\
                      .then_inc(s2_done, 1)

            def turn2(n, qt):
                i = n * QT + QT - 1 - qt
                for br, bank in enumerate((tr[:, :], proj[:, 3, :])):
                    pe.wait_ge(p2_ready, 2 * i + br + 1)
                    pe.wait_ge(pt2_ready, 2 * i + br + 1)
                    for k in range(qt + 1):
                        mm = pe.transpose(bank[:, k * P:(k + 1) * P], work(2 * br + qt % 2)[:, k * P:(k + 1) * P], ident[:, :])
                    mm.then_inc(t2_done, 1)

            def compressed(n, j, par):
                pe.wait_ge(bias_ready, 2 * (n + 1))
                if par == 0:
                    pe.wait_ge(q_ready, j + 1)
                for t in range(QT):
                    mm = pe.matmul(proj[:, 2, t * N_CMP:(t + 1) * N_CMP], qbuf[half(par), t * P:(t + 1) * P], kcmp[half(par), :],
                                   start=True, stop=True)
                mm.then_inc(cs_done, 1)

            def values(par, pt, vn):
                for k in range(QT):
                    mm = pe.matmul(ot[half(par), k * P:S], vn[:, k * P + 64 * par:k * P + 64 * par + 64], pt(k)[:, k * P:S],
                                   start=False, stop=True, skip_group_check=True)
                return mm

            def finish2(n, par):
                pe.wait_ge(pt2_ready, 2 * (n + 1) * QT + 2)
                values(par, lambda k: pt_b(par, k), vn_w).then_inc(o2_done, 1)

            def core2(j, par, first, last):
                n = 2 * j + par
                turn2(n, 3)
                scores2(n, j, par, 1)
                turn2(n, 2)
                scores2(n, j, par, 0)
                if not first:
                    finish2(n - 1, 1 - par)
                pe.wait_ge(pc_ready, n + 1)
                for t in range(QT):
                    mm = pe.transpose(proj[0:N_CMP, 2, t * P:(t + 1) * P], p_c[:, t * N_CMP:(t + 1) * N_CMP], ident[:, :])
                mm.then_inc(tc_done, 1)
                turn2(n, 1)
                pe.wait_ge(ptc_ready, n + 1)
                nj, npar = (j, 1) if par == 0 else (j + 1, 0)
                if not last:
                    compressed(n + 1, nj, npar)
                turn2(n, 0)
                if not last:
                    scores2(n + 1, nj, npar, 3)
                    scores2(n + 1, nj, npar, 2)
                pe.wait_ge(o2_ready, n + 1)
                pe.matmul(ot[half(par), :], vcmp[:, half(par)], pt_c[0:N_CMP, :], start=True, stop=True)
                pe.wait_ge(pt2_ready, 2 * (n + 1) * QT + 1)
                values(par, lambda k: work(4 + k), vn_s)

            compressed(0, 0, 0)
            scores2(0, 0, 0, 3)
            scores2(0, 0, 0, 2)
            core2(0, 0, True, False)
            core2(0, 1, False, False)
            with pe.Fori(1, QT - 1) as j:
                core2(j, 0, False, False)
                core2(j, 1, False, False)
            core2(QT - 1, 0, False, False)
            core2(QT - 1, 1, False, True)
            finish2(HEADS - 1, 1)
            for k in range(KD):
                pe.wait_ge(mix_sq, k + 1)
                mm = pe.matmul(sc[:, k // 4, :], ones[:, :], work(k), start=k % 4 == 0, stop=k % 4 == 3)
                if k % 4 == 3:
                    mm.then_inc(mix_stat, 1)
            for m in range(KD):
                slot_mm(Slot(L2, B2_OUT + m), u_of, (lambda k: pe.wait_ge(u_ready, 10 * KD + k + 1)) if m == 0 else None)
            stat(10, sums_2(10))
            for m in range(KD):
                pe.wait_ge(sqs_ready, 6 * KD + m + 1)
                mm = pe.matmul(ot[:, :], ones[:, :], ax(8 + m), start=m == 0, stop=m == KD - 1)
            mm.then_inc(stat_done, 1)
            with pe.Fori(0, FF2_GROUPS) as g:
                for j in range(KD):
                    slot_mm(Slot(L2, B2_FF + j, g, 2 * KD), u_of,
                            (lambda k: pe.wait_ge(u_ready, 11 * KD + k + 1)) if j == 0 else None)
                first = FF_TILES * 2 * DEPTH + 1
                for m in range(KD):
                    slot_mm(Slot(L2, B2_FF + KD + m, g, 2 * KD), a_of,
                            (lambda k: pe.wait_ge(a_lo_ready, KD * g + first + k)) if m == 0 else None)
            stat(12, sums_2(11))

        @block.vector
        def _(dve):
            steps = [0]

            def link(ins):
                steps[0] += 1
                ins.then_inc(start_step, 1)
                dve.wait_ge(start_step, steps[0])

            def split_lo(slot):
                dve.wait_ge(w_hi_ready, slot.number + slot.inc)
                dve.tensor_tensor(wt(w_lo, slot, slot.tiles), wt(raw, slot, slot.tiles),
                                  wt(w_hi, slot, slot.tiles).bitcast(F32), ALU.subtract).then_inc(w_lo_ready, slot.inc)

            def prep_lo(n, m, gain):
                dve.wait_ge(u_hi_ready, KD * n + m + 1)
                dve.scalar_tensor_tensor(u_lo(m), h(m), gain[:, m:m + 1], u_hi(m).bitcast(F32), ALU.mult,
                                         ALU.subtract).then_inc(u_ready, 1)

            def inv_rms(n):
                dve.wait_ge(rms_ready, n + 1)
                dve.reciprocal(rs, acc).then_inc(rs_ready, 1)

            def normed(slot, dst, n):
                dve.wait_ge(rs_ready, n + 1)
                dve.wait_ge(slot_done, slot.done)
                return dve.tensor_tensor(dst, proj[:, slot.pos, :], rs, ALU.mult)

            dve.memset(stat_t[:, 64:65], 0.0).then_inc(w_lo_ready, RING)
            dve.memset(stat_t[:, 65:66], 0.0).then_inc(slot_done, RING)
            dve.memset(stat_t[:, 66:67], 0.0).then_inc(slot_read, RING)
            dve.memset(stat_t[:, 67:68], 0.0).then_inc(exp_ready, 2)
            dve.memset(stat_t[:, 68:69], 0.0).then_inc(gate_tanh, 2)
            dve.memset(stat_t[:, 69:70], 0.0).then_inc(exp2, 4)
            dve.memset(stat_t[:, 70:71], 0.0).then_inc(pt2_ready, 2)
            dve.memset(stat_t[:, 71:72], 0.0).then_inc(o2_ready, 2)
            for i, ready in enumerate((ada_done, pt_ready, o_ready, conv_ready, tc_done)):
                dve.memset(stat_t[:, 24 + i:25 + i], 0.0).then_inc(ready, 1)
            dve.wait_ge(const_in, 32)
            wa, wb = work(0), work(1)
            link(dve.tensor_copy(wb, wa.bitcast(I32)))
            link(dve.tensor_scalar(wa, wb, stat_t[:, 0:1], None, ALU.mult))
            link(dve.tensor_scalar(wb, wa, 1.0 / TWO_PI, ROUND, ALU.mult, ALU.add))
            link(dve.tensor_scalar(wb, wb, -ROUND, None, ALU.add))
            for part in (PI_A, PI_B, PI_C):
                link(dve.scalar_tensor_tensor(wa, wb, -part, wa, ALU.mult, ALU.add))
            link(dve.tensor_scalar(wa, wa, stat_t[:, 1:2], None, ALU.add))
            link(dve.tensor_scalar(wb, wa, TWO_PI / 2, -TWO_PI, ALU.is_gt, ALU.mult))
            link(dve.tensor_tensor(wa, wa, wb, ALU.add))
            dve.tensor_scalar(wa, wa, float(np.float32(3.1415925)), -float(np.float32(3.1415925)), ALU.min, ALU.max)\
               .then_inc(pos_ready, 1)
            split_lo(Slot(0, 0))
            for m in range(KD):
                prep_lo(0, m, vec0)
            split_lo(Slot(0, 1))

            def ffn(layer, f, e):
                name = f"ffn{f + 1}"
                no = layer * 2 + f
                norm = norm_no(layer, e) - 1
                for g, ft in enumerate(FF_GROUPS):
                    s0 = STAGE[f"{name}_up{g}"]
                    f0 = sum(FF_GROUPS[:g])
                    if g == 0:
                        inv_rms(norm)

                    def up(it):
                        for q in range(2):
                            i = no * FF_TILES + f0 + 2 * it + q + 1
                            split_lo(Slot(layer, s0 + 2 * q + AHEAD, it, RING))
                            normed(Slot(layer, s0 + 2 * q, it, RING), work(q), norm).then_inc(slot_read, 1)
                            split_lo(Slot(layer, s0 + 2 * q + 1 + AHEAD, it, RING))
                            up_slot = Slot(layer, s0 + 2 * q + 1, it, RING)
                            normed(up_slot, work(6 + q), norm).then_inc(slot_read, 1)
                            dve.wait_ge(tanh_ready, i)
                            dve.scalar_tensor_tensor(work(4 + q), work(2 + q), 1.0, work(q), ALU.add, ALU.mult)\
                               .then_inc(sil_ready, 1)
                            dve.wait_ge(slot_read, up_slot.done)
                            dve.wait_ge(sil_ready, i)
                            dve.tensor_tensor(work(8 + q), work(4 + q), work(6 + q), ALU.mult).then_inc(act_ready, 1)
                            dve.wait_ge(a_hi_ready, i)
                            at = bass.ds((2 * it + q) * S, S)
                            dve.tensor_tensor(a_lo_t[:, at], work(8 + q), a_hi_t[:, at].bitcast(F32), ALU.subtract)\
                               .then_inc(a_lo_ready, 1)
                    repeat(dve, s0, ft // 2, RING, up)
                    if g < 2:
                        b = no * 2 + g
                        if g == 0:
                            dve.wait_ge(c_tanh, no + 1)
                            dve.scalar_tensor_tensor(c_b, c_th, 1.0, c_b, ALU.add, ALU.mult).then_inc(silu_ready, 1)
                            dve.wait_ge(silu_ready, no + 1)
                    s0 = STAGE[f"{name}_down{g}"]

                    def add(slot, at):
                        dve.wait_ge(slot_done, slot.done)
                        dve.scalar_tensor_tensor(at, proj[:, slot.pos, :], 0.25, at, ALU.mult, ALU.add)\
                           .then_inc(slot_read, slot.inc)
                    if g < 2:
                        for m in range(KD):
                            split_lo(Slot(layer, s0 + m + AHEAD))
                            add(Slot(layer, s0 + m), h(m))
                            if m == 0:
                                dve.wait_ge(ada_in, 16 * (b + 1))
                                dve.wait_ge(ada_done, b + 1)
                            if m < ADA_BATCH:
                                w = gate_t[:, m * D:(m + 1) * D]
                                dve.scalar_tensor_tensor(w, w, 0.5, c_b, ALU.mult, ALU.mult,
                                                         accum_out=stat_t[:, 64 + m:65 + m]).then_inc(ada_sum, 1)
                        dve.wait_ge(ada_sum, ADA_BATCH * (b + 1))
                        dve.tensor_copy(mod_t[:, bass.ds(b * ADA_BATCH, ADA_BATCH)], stat_t[:, 64:64 + ADA_BATCH])\
                           .then_inc(ada_done, 1)
                        continue
                    if f == 0:
                        dve.wait_ge(vec_in, 16 * (layer + 1))
                    gain = vec[:, (V_MIX if f == 0 else V_PLE):]
                    for m in range(KD):
                        split_lo(Slot(layer, s0 + m + AHEAD))
                        add(Slot(layer, s0 + m), h(m))
                        if m:
                            prep_lo(norm_no(layer, e), m - 1, gain)
                    prep_lo(norm_no(layer, e), KD - 1, gain)

            def evac(slot, dst, by=None):
                dve.wait_ge(slot_done, slot.done)
                if by is None:
                    dve.tensor_copy(dst, proj[:, slot.pos, :]).then_inc(slot_read, slot.inc)
                else:
                    dve.tensor_tensor(dst, proj[:, slot.pos, :], by, ALU.mult).then_inc(slot_read, slot.inc)

            def head_evac(slot, j, q):
                evac(slot, work((0, 2, 4, 6)[j] + (q if j < 3 else 0)), cs if j == 1 else None)

            def row_max(n, qt):
                i = n * QT + QT - qt
                dve.wait_ge(s_done, i)
                dve.tensor_reduce(stat_t[:, 4 + qt:5 + qt], sc[:, qt % 2, 0:(qt + 1) * P], AX, ALU.max)\
                   .then_inc(mx_ready, 1)
                dve.wait_ge(mx_ready, i)
                dve.tensor_scalar(stat_t[:, 8 + qt:9 + qt], stat_t[:, 4 + qt:5 + qt], -SCALE1, None, ALU.mult)\
                   .then_inc(nmax_ready, 1)

            def row_norm(n, qt):
                i = n * QT + QT - qt
                dve.wait_ge(exp_ready, 2 + i)
                dve.reciprocal(stat_t[:, 20 + qt:21 + qt], stat_t[:, 16 + qt:17 + qt]).then_inc(rinv_ready, 1)
                dve.wait_ge(rinv_ready, i)
                p = work(9 + qt % 2)[:, 0:(qt + 1) * P]
                dve.tensor_scalar(p, p, stat_t[:, 20 + qt:21 + qt], None, ALU.mult).then_inc(p_ready, 1)

            def enter(n, q):
                row_max(n, 3)
                row_max(n, 2)
                dve.wait_ge(v_turned, n + 1)
                dve.tensor_copy(work(7 + q), tr[:, :]).then_inc(v_ready, 1)
                row_norm(n, 3)
                row_norm(n, 2)

            def core(layer, hd, q, slots, ahead):
                n = layer * HEADS + hd

                def side(j):
                    if slots:
                        split_lo(ahead[j])
                        head_evac(slots[j], j, 1 - q)
                row_max(n, 1)
                side(0)
                row_max(n, 0)
                row_norm(n, 1)
                side(1)
                side(2)
                row_norm(n, 0)
                side(3)
                if slots:
                    enter(n + 1, 1 - q)
                dve.wait_ge(o_hi_ready, n + 1)
                at = bass.ds(hd * S, S)
                dve.tensor_tensor(u_lo_t[:, at], ot[:, :], u_hi_t[:, at].bitcast(F32), ALU.subtract).then_inc(o_ready, 1)

            with dve.Fori(0, DEPTH) as layer:
                ffn(layer, 0, 0)
                s0 = STAGE["lora"]
                for j in range(6):
                    split_lo(Slot(layer, s0 + j + AHEAD))
                    if j == 0:
                        inv_rms(norm_no(layer, 0))
                    slot = Slot(layer, s0 + j)
                    normed(slot, work(j), norm_no(layer, 0)).then_inc(slot_read, 1)
                dve.wait_ge(sin_ready, 1)
                dve.wait_ge(slot_read, Slot(layer, s0 + 5).done)
                dve.tensor_tensor(work(5), work(5), cs, ALU.mult).then_inc(kr_rope, 1)
                zs = [0]

                def zlink(ins):
                    zs[0] += 1
                    ins.then_inc(z_step, 1)
                    dve.wait_ge(z_step, Z_STEPS * layer + zs[0])
                Z_STEPS = 4 * 4

                def side(i):
                    if i < 2:
                        dve.wait_ge(lora_rms, 2 * layer + i + 1)
                        t = work(11 + 2 * i)
                        dve.reciprocal(t, t).then_inc(lora_rs, 1)
                    elif i < 7:
                        j = i - 2
                        dve.wait_ge(lora_rs, 2 * layer + 2)
                        g = V_Q + j
                        dve.scalar_tensor_tensor(work(j), work(j), vec[:, g:g + 1], work(11 if j < 3 else 13), ALU.mult,
                                                 ALU.mult).then_inc(lora_norm, 1)
                    else:
                        j = i - 7
                        dve.wait_ge(lora_hi, 5 * layer + j + 1)
                        dve.tensor_tensor(a_lo(j), work(j), a_hi(j).bitcast(F32), ALU.subtract).then_inc(lora_ready, 1)
                s0 = STAGE["conv"]
                for j in range(12):
                    t, part = divmod(j, 3)
                    split_lo(Slot(layer, s0 + j + AHEAD))
                    slot = Slot(layer, s0 + j)
                    if part == 0:
                        dve.wait_ge(conv_ready, 1 + 4 * layer + t)
                    normed(slot, work((6, 7, 10)[part]), norm_no(layer, 0)).then_inc(slot_read, 1)
                    if j == 1:
                        dve.wait_ge(kr_fold, layer + 1)
                        dve.tensor_copy(work(15), sc[:, 0, :]).then_inc(kr_ready, 1)
                    side(j)
                    if part == 1:
                        dve.wait_ge(slot_read, slot.done)
                        zlink(dve.tensor_tensor(work(9), work(6), work(7), ALU.mult))
                    if part == 2:
                        w = lambda tap: vec[:, V_CONV + 4 * tap + t:V_CONV + 4 * tap + t + 1]
                        y, z1 = work(6), work(9)
                        zlink(dve.tensor_scalar(y, z1, w(2), None, ALU.mult))
                        for back in (1, 2):
                            zlink(dve.scalar_tensor_tensor(y[:, back:S], z1[:, 0:S - back], w(2 - back), y[:, back:S],
                                                           ALU.mult, ALU.add))
                        dve.wait_ge(slot_read, slot.done)
                        dve.tensor_tensor(work(7), work(10), y, ALU.mult).then_inc(conv_y, 1)
                        dve.wait_ge(conv_hi, 4 * layer + t + 1)
                        dve.tensor_tensor(a_lo(5 + t), work(7), a_hi(5 + t).bitcast(F32), ALU.subtract)\
                           .then_inc(conv_ready, 1)
                s0 = STAGE["gates"]

                def gates(it):
                    for j in range(RING):
                        split_lo(Slot(layer, s0 + j + AHEAD, it, RING))
                        dve.wait_ge(gate_tanh, 16 * layer + it * RING + j + 1)
                        normed(Slot(layer, s0 + j, it, RING), work(13 + j % 2), norm_no(layer, 0)).then_inc(slot_read, 1)
                repeat(dve, s0, 4, RING, gates)
                s0 = STAGE["heads"]
                for j in range(4):
                    split_lo(Slot(layer, s0 + j + AHEAD))
                    head_evac(Slot(layer, s0 + j), j, 0)
                enter(layer * HEADS, 0)

                def heads(it):
                    end = isinstance(it, int)
                    for q in range(2):
                        o = s0 + 4 * (q + 1) + (24 if end else 0)
                        r = 0 if end else it
                        slots = [Slot(layer, o + j, r, 8) for j in range(4)]
                        ahead = [Slot(layer, o + j + AHEAD, r, 8) for j in range(4)]
                        core(layer, 2 * it + q, q, None if end and q else slots, ahead)
                with dve.Fori(0, HEADS // 2 - 1) as it:
                    heads(it)
                heads(HEADS // 2 - 1)
                s0 = STAGE["branch_out"]
                for m in range(KD):
                    q = m % 2
                    for br in range(2):
                        slot = Slot(layer, s0 + 2 * m + br)
                        split_lo(Slot(layer, s0 + 2 * m + br + AHEAD))
                        dve.wait_ge(gate_tanh, 16 * (layer + 1) + 2)
                        dve.wait_ge(slot_done, slot.done)
                        dve.scalar_tensor_tensor(work(2 * q + br), gate(2 * m + br), 1.0, proj[:, slot.pos, :], ALU.add,
                                                 ALU.mult).then_inc(slot_read, 1)
                    dve.wait_ge(slot_read, slot.done)
                    dve.tensor_tensor(work(4 + q), work(2 * q), work(2 * q + 1), ALU.add).then_inc(mg_ready, 1)
                    dve.wait_ge(mg_hi, KD * layer + m + 1)
                    dve.tensor_tensor(merged_lo(m), work(4 + q), merged_hi(m).bitcast(F32), ALU.subtract)\
                       .then_inc(merged_ready, 1)
                s0 = STAGE["mix_out"]
                for m in range(KD):
                    slot = Slot(layer, s0 + m)
                    split_lo(Slot(layer, s0 + m + AHEAD))
                    dve.wait_ge(slot_done, slot.done)
                    dve.scalar_tensor_tensor(h(m), proj[:, slot.pos, :], 0.5, h(m), ALU.mult, ALU.add).then_inc(slot_read, 1)
                    if m:
                        prep_lo(norm_no(layer, 1), m - 1, vec[:, V_FFN2:])
                prep_lo(norm_no(layer, 1), KD - 1, vec[:, V_FFN2:])
                ffn(layer, 1, 2)
                s0 = STAGE["ple"]
                for m in range(KD):
                    end = m == KD - 1
                    if m == 0:
                        split_lo(Slot(layer, s0 + AHEAD))
                        split_lo(Slot(layer, s0 + AHEAD + 1))
                    elif 1 < m < KD - 1:
                        split_lo(Slot(layer, s0 + 2 * m + AHEAD))
                    if m == 0:
                        dve.wait_ge(p_hi_ready, layer + 1)
                        dve.tensor_tensor(a_lo_t[:, 0:2 * S], work_t[:, 12 * S:14 * S], a_hi_t[:, 0:2 * S].bitcast(F32),
                                          ALU.subtract).then_inc(p_split, 1)
                        inv_rms(norm_no(layer, 2))
                        split_lo(Slot(layer, s0 + AHEAD + 2))
                    normed(Slot(layer, s0 + 2 * m), work(m % 2), norm_no(layer, 2)).then_inc(slot_read, 1)
                    slot = Slot(layer, s0 + 2 * m + 1)
                    if m and not end:
                        split_lo(Slot(layer, s0 + 2 * m + 1 + AHEAD))
                    dve.wait_ge(ple_tanh, KD * layer + m + 1)
                    dve.wait_ge(slot_done, slot.done)
                    dve.scalar_tensor_tensor(work(2 + m % 2), gate(m), 1.0, proj[:, slot.pos, :], ALU.add, ALU.mult)\
                       .then_inc(slot_read, slot.inc)
                    dve.wait_ge(slot_read, slot.done)
                    dve.scalar_tensor_tensor(h(m), work(2 + m % 2), 0.5, h(m), ALU.mult, ALU.add).then_inc(ple_step, 1)
                for m in range(KD):
                    if m in (0, 2):
                        split_lo(Slot(layer, LAYER_SLOTS + m // 2))
                    prep_lo(norm_no(layer, 3), m, vec[:, V_NEXT:])

            def ahead(s):
                if s + AHEAD < B2_SLOTS:
                    split_lo(Slot(L2, s + AHEAD))

            c2 = lambda at, n=1: col2[:, at:at + n]
            dve.wait_ge(ada_done, 9)
            dve.wait_ge(col2_in, 16)
            link(dve.tensor_tensor(mod_t[:, :], mod_t[:, :], c2(C_ADAB, 48), ALU.add))
            for i, (gain, part) in enumerate(((C_PRE, 1), (C_POST, 2), (C_PREM, 4), (C_POSTM, 5))):
                link(dve.scalar_tensor_tensor(modc[:, 8 * i:8 * i + 8], mod_t[:, 8 * part:8 * part + 8], 1.0, c2(gain, 8),
                                              ALU.add, ALU.mult))
            link(dve.tensor_tensor(modc[:, 0:KD], modc[:, 0:KD], vec[:, V_NEXT:V_NEXT + KD], ALU.mult))
            dve.tensor_scalar(small2[:, 20:28], c2(C_BA, 8), 0.5, None, ALU.mult).then_inc(mods_ready, 1)

            def modulated(n, gain):
                for m in range(KD + 1):
                    if m < KD:
                        dve.wait_ge(sh_ready, KD * (n == 11) + m + 1)
                        dve.scalar_tensor_tensor(work(2 + m), h(m), modc[:, gain + m:gain + m + 1], work(2 + m), ALU.mult,
                                                 ALU.add).then_inc(tmp_ready, 1)
                    if m:
                        dve.wait_ge(u_hi_ready, n * KD + m)
                        dve.tensor_tensor(u_lo(m - 1), work(1 + m), u_hi(m - 1).bitcast(F32), ALU.subtract).then_inc(u_ready, 1)

            dve.wait_ge(stat_done, 9)
            dve.tensor_scalar(rs, ot[:, :], EPS, EPS * EPS * D, ALU.mult, ALU.add).then_inc(comb_ready, 1)
            dve.wait_ge(stat_done, 10)
            dve.wait_ge(comb_ready, 1)
            dve.tensor_tensor(rs, rs, tr[:, :], ALU.add).then_inc(comb_ready, 1)
            modulated(9, 0)
            dst = [xr(j) for j in range(4)] + [gr(j) for j in range(4)] + [KC, VC, KS, VS, KW, VW, gT] + [q2(j) for j in range(4)]
            def build_blocks(kv, g):
                xv = blocks.rearrange("p (t c) -> p t c", c=62)
                for half in range(2):
                    gp, hp = slice(64 * g, 64 * g + 64), slice(64 * half, 64 * half + 64)
                    rows = (KC, VC)[kv][gp, half:half + 1]
                    tok = bass.AP(rows.tensor, rows.offset, [rows.ap[0], (2, CMP_K), (16, N_CMP)])
                    pos = pos2(kv)[gp, half:32:2].unsqueeze(2).to_broadcast([64, CMP_K, N_CMP])
                    dve.tensor_tensor(xv[hp, :, g * N_CMP:(g + 1) * N_CMP], tok, pos, ALU.add).then_inc(x_built, 1)

            for s in range(IN2):
                ahead(s)
                slot = Slot(L2, s)
                if s == 17:
                    dve.wait_ge(hid_part, 2)
                    link(dve.tensor_copy(hid_x, ot[0:62, :]))
                    link(dve.tensor_tensor(hid_t, hid_x, hid_x, ALU.mult))
                    link(dve.tensor_scalar(hid_t, hid_t, 0.044715, 1.0, ALU.mult, ALU.add))
                    dve.tensor_tensor(hid_t, hid_t, hid_x, ALU.mult).then_inc(hid_in, 1)
                if s == 0:
                    dve.wait_ge(rms_ready, 9)
                    dve.reciprocal(rs, acc).then_inc(rs_ready, 1)
                    dve.wait_ge(rs_ready, 9)
                if s == 1:
                    dve.wait_ge(rms_ready, 10)
                    dve.reciprocal(rms8, rms8).then_inc(rs_ready, 1)
                if 2 <= s <= 9:
                    m = s - 2
                    dve.wait_ge(rs_ready, 10)
                    dve.wait_ge(tmp_ready, KD)
                    dve.scalar_tensor_tensor(h(m), h(m), vec[:, V_NEXT + m:V_NEXT + m + 1], rms8, ALU.mult, ALU.mult)\
                       .then_inc(hf_ready, 1)
                if s == 1:
                    lam = col2[:, C_LAM:C_LAM + 4]
                    top, z, zz = (small2[:, 4 * i:4 * i + 4] for i in range(1, 4))
                    link(dve.tensor_scalar(top, lam, -1.0, None, ALU.mult))
                    link(dve.tensor_tensor(z, lam, top, ALU.max))
                    dve.tensor_scalar(top, top, 0.0, None, ALU.max).then_inc(pos_ready, 1)
                if s == 3:
                    dve.wait_ge(lam_exp, 1)
                    link(dve.tensor_scalar(zz, z, 2.0, None, ALU.add))
                    link(dve.reciprocal(zz, zz))
                    link(dve.tensor_tensor(z, z, zz, ALU.mult))
                    link(dve.tensor_tensor(zz, z, z, ALU.mult))
                    poly = small2[:, 16:20]
                    link(dve.tensor_scalar(poly, zz, 1.0 / 15, 1.0 / 13, ALU.mult, ALU.add))
                    for d in (11, 9, 7, 5, 3, 1):
                        link(dve.tensor_tensor(poly, poly, zz, ALU.mult))
                        link(dve.tensor_scalar(poly, poly, 1.0 / d, None, ALU.add))
                    link(dve.tensor_tensor(poly, poly, z, ALU.mult))
                    link(dve.scalar_tensor_tensor(top, poly, 2.0, top, ALU.mult, ALU.add))
                    link(dve.tensor_scalar(small2[:, 0:4], top, -4.0, None, ALU.mult))
                if 15 <= s:
                    dve.wait_ge(slot_done, slot.done)
                    dve.scalar_tensor_tensor(dst[s], proj[:, slot.pos, :], 0.125, rs, ALU.mult, ALU.mult).then_inc(slot_read, 1)
                else:
                    evac(slot, dst[s], rs)
                if 4 <= s <= 7:
                    j = s - 4
                    dve.wait_ge(slot_read, Slot(L2, j).done)
                    xf = work(2 + j)
                    w = lambda tap: c2(C_CW + 4 * tap + j)
                    link(dve.tensor_scalar(xf, xr(j), w(3), c2(C_CB + j), ALU.mult, ALU.add))
                    for back in (1, 2, 3):
                        i = dve.scalar_tensor_tensor(xf[:, back:S], xr(j)[:, 0:S - back], w(3 - back), xf[:, back:S], ALU.mult, ALU.add)
                        if back < 3:
                            link(i)
                    i.then_inc(xf_ready, 1)
                if 6 <= s <= 9:
                    j = s - 6
                    dve.wait_ge(rg_tanh, 2 * j + 2)
                    dve.tensor_scalar(work(6 + j), work(6 + j), 1.0, small2[:, j:j + 1], ALU.add, ALU.mult).then_inc(la_ready, 1)
                if 8 <= s <= 11:
                    j = s - 8
                    dve.wait_ge(decay_ready, 3 * j + 3)
                    dve.scalar_tensor_tensor(work(6 + j), work(14 + j % 2), 1.0, work(6 + j), ALU.add, ALU.mult).then_inc(v2_ready, 1)
                    dve.wait_ge(xf_ready, j + 1)
                    dve.scalar_tensor_tensor(work(10 + j), work(10 + j), 1.0, work(2 + j), ALU.add, ALU.mult).then_inc(ix_ready, 1)
                if 13 <= s <= 16:
                    j = s - 13
                    dve.wait_ge(sqrt_ready, j + 1)
                    link(dve.scalar_tensor_tensor(work(10 + j), work(10 + j), 0.5, work(6 + j), ALU.mult, ALU.mult))
                    link(dve.tensor_tensor_scan(work(6 + j), xr(j), work(10 + j), 0.0, ALU.mult, ALU.add))
                    dve.wait_ge(gel_sq, j + 1)
                    link(dve.tensor_scalar(work(2 + j), work(2 + j), 0.044715, 1.0, ALU.mult, ALU.add))
                    dve.tensor_tensor(work(2 + j), work(2 + j), gr(j), ALU.mult).then_inc(gel_in, 1)
                if 14 <= s <= 17:
                    j = s - 14
                    dve.wait_ge(gel_tanh, j + 1)
                    link(dve.scalar_tensor_tensor(gr(j), work(2 + j), 1.0, gr(j), ALU.add, ALU.mult))
                    dve.scalar_tensor_tensor(gr(j), gr(j), 0.5, work(6 + j), ALU.mult, ALU.mult).then_inc(rnn_ready, 1)
                if s in (12, 13, 15):
                    if s == 12:
                        dve.wait_ge(slot_read, Slot(L2, 9).done)
                        dve.wait_ge(w2_in, 16)
                        dve.wait_ge(v2_ready, 4)
                    if s == 15:
                        dve.wait_ge(hid_part, 1)
                    for g in ((0,), (1,), (), (0, 1))[s - 12]:
                        build_blocks(s // 15, g)
                if s == 17:
                    dve.wait_ge(hid_tanh, 1)
                    link(dve.scalar_tensor_tensor(hid_x, hid_t, 1.0, hid_x, ALU.add, ALU.mult))
                    dve.tensor_scalar(hid_x, hid_x, 0.5, None, ALU.mult).then_inc(hid_ready, 1)
                    dve.wait_ge(g_turned, 1)
                    dve.tensor_scalar(gcols.rearrange("p (t c) -> p t c", t=QT),
                                      tr[:, :].rearrange("p (t c) -> p t c", t=QT)[:, :, 0:24],
                                      1.0, 0.5, ALU.add, ALU.mult).then_inc(g_cols, 1)
            dve.wait_ge(hid_turned, 1)
            dve.tensor_copy(hid_c, tr[:, 0:248]).then_inc(hid_cols, 1)
            for i, d in enumerate((vn_s, vn_w)):
                dve.wait_ge(v2_turned, i + 1)
                dve.tensor_copy(d, sc[:, i, :]).then_inc(v2_copied, 1)
            dve.wait_ge(kv_cmp_done, 1)
            dve.tensor_copy(kcmp[0:64, :], proj[0:64, 0, 0:N_CMP]).then_inc(kv_cmp_ready, 1)
            dve.tensor_copy(kcmp[64:P, :], proj[64:P, 0, N_CMP:62]).then_inc(kv_cmp_ready, 1)
            dve.tensor_copy(vcmp, proj[0:N_CMP, 3, 0:P]).then_inc(kv_cmp_ready, 1)
            dve.wait_ge(g_ready, 1)

            gates2 = gcols.rearrange("p (t c) -> p t c", t=QT)

            def cmp_softmax(n, head):
                dve.wait_ge(cs_done, n + 1)
                dve.wait_ge(tc_done, n + 1)
                pc3 = p_c.rearrange("p (t c) -> p t c", c=N_CMP)
                mx = stat_t[:, 24:28]
                dve.tensor_tensor(p_c, proj[:, 2, 0:QT * N_CMP], bias_c[:, bass.ds(head * QT * N_CMP, QT * N_CMP)], ALU.add)\
                   .then_inc(pc_step, 1)
                dve.wait_ge(pc_step, 6 * n + 1)
                dve.tensor_reduce(mx, pc3, AX, ALU.max).then_inc(pc_step, 1)
                dve.wait_ge(pc_step, 6 * n + 2)
                dve.tensor_tensor(pc3, pc3, mx.unsqueeze(2).to_broadcast([P, QT, N_CMP]), ALU.subtract).then_inc(cs_sub, 1)

            def cmp_norm(n, head):
                pc3 = p_c.rearrange("p (t c) -> p t c", c=N_CMP)
                sm = stat_t[:, 28:32]
                dve.wait_ge(cs_exp, n + 1)
                dve.tensor_reduce(sm, pc3, AX, ALU.add).then_inc(pc_step, 1)
                dve.wait_ge(pc_step, 6 * n + 3)
                dve.reciprocal(sm, sm).then_inc(pc_step, 1)
                dve.wait_ge(pc_step, 6 * n + 4)
                dve.tensor_tensor(sm.unsqueeze(2), sm.unsqueeze(2), gates2[:, :, bass.ds(head, 1)], ALU.mult).then_inc(pc_step, 2)
                dve.wait_ge(pc_step, 6 * n + 6)
                dve.tensor_tensor(pc3, pc3, sm.unsqueeze(2).to_broadcast([P, QT, N_CMP]), ALU.mult).then_inc(pc_ready, 1)

            def row_max2(n, qt):
                w, q, i = (qt + 1) * P, qt % 2, n * QT + QT - 1 - qt
                for br, bank in enumerate((sc, proj)):
                    dve.wait_ge(s2_done, 2 * i + br + 1)
                    dve.tensor_reduce(stat_t[:, 4 + 2 * q + br:5 + 2 * q + br], bank[:, q, 0:w], AX, ALU.max).then_inc(max2, 1)
                dve.wait_ge(max2, 2 * i + 2)
                dve.tensor_scalar(stat_t[:, 8 + 2 * q:10 + 2 * q], stat_t[:, 4 + 2 * q:6 + 2 * q], -1.0, None, ALU.mult)\
                   .then_inc(nmax2, 1)

            def row_norm2(n, head, qt):
                w, q, i = (qt + 1) * P, qt % 2, n * QT + QT - 1 - qt
                dve.wait_ge(exp2, 4 + 2 * i + 2)
                inv = stat_t[:, 16 + 2 * q:18 + 2 * q]
                dve.reciprocal(inv, stat_t[:, 12 + 2 * q:14 + 2 * q]).then_inc(inv2, 1)
                dve.wait_ge(inv2, i + 1)
                g = gates4[:, qt, 1:3, bass.ds(head, 1)]
                dve.tensor_tensor(inv.unsqueeze(2), inv.unsqueeze(2), g, ALU.mult).then_inc(ginv2, 1)
                dve.wait_ge(ginv2, i + 1)
                for br in range(2):
                    pt = work(2 * br + q)[:, 0:w]
                    dve.tensor_scalar(pt, pt, inv[:, br:br + 1], None, ALU.mult).then_inc(p2_ready, 1)

            def enter2(j, par):
                n, head = 2 * j + par, 4 * par + j
                row_max2(n, 3)
                dve.wait_ge(bias_ready, 2 * (n + 1))
                cmp_softmax(n, head)
                row_max2(n, 2)
                row_norm2(n, head, 3)
                cmp_norm(n, head)
                row_norm2(n, head, 2)

            def take2(j, par):
                rows = slice(64 * par, 64 * par + 64)
                dve.wait_ge(o2_done, 2 * j + par + 1)
                dve.tensor_copy(work_t[rows, bass.ds((12 + j) * S, S)], ot[rows, :]).then_inc(o2_ready, 1)

            def queries(j):
                dve.tensor_copy(qbuf, ax_t[:, bass.ds((14 + j) * S, S)]).then_inc(q_ready, 1)

            def core2(j, par, first, last):
                n, head = 2 * j + par, 4 * par + j
                row_max2(n, 1)
                row_max2(n, 0)
                if par and not last:
                    queries(j + 1)
                row_norm2(n, head, 1)
                row_norm2(n, head, 0)
                if not first:
                    take2(*((j, 0) if par else (j - 1, 1)))
                if not last:
                    enter2(*((j, 1) if par == 0 else (j + 1, 0)))

            gates4 = gcols.rearrange("p (t b h) -> p t b h", t=QT, b=3)
            queries(0)
            enter2(0, 0)
            core2(0, 0, True, False)
            core2(0, 1, False, False)
            with dve.Fori(1, QT - 1) as j:
                core2(j, 0, False, False)
                core2(j, 1, False, False)
            core2(QT - 1, 0, False, False)
            core2(QT - 1, 1, False, True)
            take2(QT - 1, 1)
            dve.wait_ge(mix_rms, 2)
            for k in range(KD + 1):
                src = lambda k: gr(k) if k < 4 else work(8 + k)
                if k < KD:
                    dve.scalar_tensor_tensor(src(k), src(k), c2(C_RNN + k), work(9 - k // 4), ALU.mult, ALU.mult).then_inc(mix_norm, 1)
                if k:
                    dve.wait_ge(u_hi_ready, 10 * KD + k)
                    dve.tensor_tensor(u_lo(k - 1), src(k - 1), u_hi(k - 1).bitcast(F32), ALU.subtract).then_inc(u_ready, 1)
            link(dve.tensor_tensor(sq, work(8), work(9), ALU.mult))
            link(dve.scalar_tensor_tensor(rs, sq, EPS * D, sq, ALU.mult, ALU.mult))
            for m in range(KD):
                ahead(B2_OUT + m)
                evac(Slot(L2, B2_OUT + m), gate(m))

            dve.wait_ge(stat_done, 11)
            dve.tensor_tensor(rs, rs, ot[:, :], ALU.add).then_inc(comb_ready, 1)
            dve.wait_ge(rms_ready, 11)
            dve.wait_ge(hf_ready, KD)
            for m in range(KD + 1):
                if m < KD:
                    dve.tensor_tensor(h(m), h(m), sq, ALU.mult).then_inc(h_scaled, 1)
                if m:
                    dve.wait_ge(h_scaled, m)
                    dve.wait_ge(y_scaled, m)
                    dve.tensor_tensor(h(m - 1), h(m - 1), gate(m - 1), ALU.add).then_inc(h2_ready, 1)
            dve.tensor_scalar(rs, rs, EPS, None, ALU.mult).then_inc(comb_ready, 1)
            dve.wait_ge(stat_done, 12)
            dve.wait_ge(comb_ready, 4)
            dve.tensor_tensor(rs, rs, ot[:, :], ALU.add).then_inc(comb_ready, 1)
            modulated(11, 16)
            dve.wait_ge(rms_ready, 12)
            dve.reciprocal(rs, acc).then_inc(rs_ready, 1)

            def ff(g):
                end = isinstance(g, int)
                for i in range(2 * KD):
                    slot = Slot(L2, B2_FF + i, g, 2 * KD)
                    if not (end and i >= 2 * KD - AHEAD):
                        split_lo(Slot(L2, B2_FF + i + AHEAD, g, 2 * KD))
                    dve.wait_ge(slot_done, slot.done)
                    if i < KD:
                        dve.wait_ge(rs_ready, 11)
                        dve.scalar_tensor_tensor(work(i % 4), proj[:, slot.pos, :], 0.0, rs, ALU.max, ALU.mult).then_inc(slot_read, 1)
                        if i:
                            lo(g, i - 1)
                        if i == KD - 1:
                            lo(g, i)
                        if end and i == 0:
                            dve.reciprocal(sq, sq).then_inc(rs_ready, 1)
                        elif end:
                            dve.wait_ge(rs_ready, 12)
                            for m in (i - 1, KD - 1) if i == KD - 1 else (i - 1,):
                                dve.tensor_tensor(h(m), h(m), sq, ALU.mult).then_inc(hf_ready, 1)
                    else:
                        m = i - KD
                        dve.wait_ge(y_zero, KD)
                        dve.tensor_tensor(gate(m), gate(m), proj[:, slot.pos, :], ALU.add).then_inc(slot_read, 1)

            def lo(g, i):
                dve.wait_ge(a_hi_ready, FF_TILES * 2 * DEPTH + KD * g + i + 1)
                dve.tensor_tensor(a_lo(i), work(4 + i % 4), a_hi(i).bitcast(F32), ALU.subtract).then_inc(a_lo_ready, 1)
            with dve.Fori(0, FF2_GROUPS - 1) as g:
                ff(g)
            ff(FF2_GROUPS - 1)
            dve.wait_ge(rms_ready, 13)
            dve.reciprocal(rs, acc).then_inc(rs_ready, 1)
            dve.wait_ge(rs_ready, 13)
            dve.wait_ge(y_scaled, 2 * KD)
            dve.wait_ge(hf_ready, 2 * KD)
            for m in range(POST + 1):
                if m < POST:
                    dve.tensor_tensor(gate(m), gate(m), rs, ALU.mult).then_inc(y_timed, 1)
                if m:
                    dve.wait_ge(y_timed, m)
                    dve.tensor_tensor(h(m - 1), h(m - 1), gate(m - 1), ALU.add).then_inc(h_out, 1)


def columns(v):
    v = np.asarray(v)
    return np.moveaxis(v.reshape(*v.shape[:-1], -1, P), -1, -2)


def slots_of(w, width=P):
    K, N = w.shape
    return np.ascontiguousarray(w.reshape(K // P, P, N // width, width).transpose(2, 1, 0, 3)).reshape(N // width, P, -1)


def turned(x):
    t, f = x.shape
    return np.ascontiguousarray(x.T.reshape(f // P, P, t).transpose(1, 0, 2))


def lay_out(i):
    c = np.ascontiguousarray
    stack = lambda f: c(np.stack([f(l) for l in range(DEPTH)]))
    o = {}
    o["x_t"] = turned(i["x"][0]).reshape(P, -1)
    o["positions"] = c(i["positions"])
    o["p_t"] = stack(lambda l: turned(i["p"][l, 0]))
    o["vec0"] = c(columns(i["ffn1_norm"][0]))
    nxt = [i["ffn1_norm"][1], i["final_norm"]]
    o["vec"] = stack(lambda l: np.concatenate(
        [columns(v) for v in (i["mix_norm"][l], i["ffn2_norm"][l], i["ple_norm"][l], nxt[l], i["q_norm"][l], i["kv_norm"][l])]
        + [columns(i["conv_w"][l, t]) for t in range(3)], axis=1))
    gu = []
    for f in ("ffn1", "ffn2"):
        def up(l):
            g = slots_of(i[f + "_w_gu"][l])
            return np.stack([g[:FF_TILES], g[FF_TILES:]], axis=1).reshape(2 * FF_TILES, P, -1)
        gu.append(stack(up))
        w = i[f + "_w_down"]
        o[f + "_dn8"] = stack(lambda l: np.concatenate([slots_of(w[l, :D]), slots_of(w[l, D:2 * D])]))
        o[f + "_dn6"] = stack(lambda l: slots_of(w[l, 2 * D:]))

    o["ffn_gu"] = np.stack(gu)

    def w_in(l):
        w = i["w_in"][l]
        b, cc, v = (slots_of(w[:, n * CONV:(n + 1) * CONV]) for n in range(3))
        at = 3 * CONV
        lora = slots_of(w[:, at:at + Q_LORA + KV_LORA])
        at += Q_LORA + KV_LORA
        r = w[:, at:at + ROPE]
        kr = slots_of(np.concatenate([r, r[:, 32:], r[:, :32]], axis=1))
        at += ROPE
        gc, gm = slots_of(w[:, at:at + D]), slots_of(w[:, at + D:])
        return np.concatenate([lora, kr, np.stack([cc, v, b], axis=1).reshape(12, P, -1),
                               np.stack([gc, gm], axis=1).reshape(16, P, -1)])
    o["in_w"] = stack(w_in)

    def head_q(l):
        w = i["w_uq"][l].reshape(Q_LORA, HEADS, NOPE + ROPE)
        r = w[:, :, NOPE:]
        w = np.concatenate([w[:, :, :NOPE], r, r[:, :, 32:], r[:, :, :32]], axis=2)
        return slots_of(w.reshape(Q_LORA, -1))
    o["head_q"] = stack(head_q)
    o["head_kv"] = stack(lambda l: slots_of(i["w_ukv"][l]))
    o["conv_out"] = stack(lambda l: slots_of(i["w_conv_out"][l]))
    o["mla_out"] = stack(lambda l: slots_of(i["w_mla_out"][l]))
    o["mix_out"] = stack(lambda l: slots_of(i["w_o"][l]))
    o["ple_gate"] = stack(lambda l: slots_of(i["w_ple_gate"][l]))
    o["ple_proj"] = stack(lambda l: slots_of(i["w_ple_proj"][l]))
    freq = (10000.0 ** (-np.arange(0, ROPE, 2) / ROPE)).astype(np.float32)
    phase = np.repeat(np.array([np.pi / 2, np.pi / 2, np.pi, 0.0], np.float32), 32)
    o["rope_consts"] = c(np.stack([np.tile(freq, 4), phase], axis=1))
    o["c_row"] = c(i["c_2"])
    o["ada"] = c(i["ada_w_2"][0].T.reshape(8, ADA_BATCH, P, D).transpose(0, 2, 1, 3)).reshape(8, P, ADA_BATCH * D)

    def by_group(v):
        s = v.shape[:-1]
        return v.reshape(*s, 2, 4, 64).swapaxes(-3, -2).reshape(*s, 512)
    o["col2"] = c(np.concatenate(
        [columns(i[n][0]) for n in ("pre_norm_mix_2", "post_norm_mix_2", "pre_norm_mlp_2", "post_norm_mlp_2", "norm_rnn_out_2")]
        + [columns(by_group(i["norm_att_out_2"][0]))] + [columns(i["conv_w_2"][0, t]) for t in range(4)]
        + [columns(i[n][0]) for n in ("conv_b_2", "lru_ba_2", "lru_bx_2", "lru_lambda_2", "ada_b_2")], axis=1))
    w = i["w_in_2"][0]
    g_rnn, x_rnn, q, kvs, gates = np.split(w, [512, 1024, 1536, 1536 + 768], axis=1)
    gates = np.concatenate([gates, np.zeros((D, P - gates.shape[1]), w.dtype)], axis=1)
    o["in2"] = c(np.concatenate([slots_of(a) for a in (x_rnn, g_rnn, kvs, gates, by_group(q))]))
    bd = np.zeros((P, 8, P), w.dtype)
    for n, name in enumerate(("lru_wa_2", "lru_wx_2")):
        for b in range(8):
            r = 64 * (b % 2)
            bd[r:r + 64, 4 * n + b // 2, r:r + 64] = i[name][0, b]
    o["lru_w"] = bd.reshape(P, -1)
    w1 = np.stack([i["cmp_w1_k_2"][0], i["cmp_w1_v_2"][0]]).reshape(2, CMP_K, P, 256)
    o["cmp_w1"] = c(w1.transpose(2, 0, 1, 3)).reshape(P, -1)
    w2k, w2v = i["cmp_w2_k_2"][0].reshape(2, P, 64), i["cmp_w2_v_2"][0].reshape(2, P, 64)
    pos = [np.tile(i[n][0].T, (2, 1)) for n in ("cmp_pos_k_2", "cmp_pos_v_2")]
    o["cmp_w2"] = c(np.concatenate([w2k[0], w2k[0], w2k[1], w2k[1], w2v[0], w2v[1]] + pos, axis=1))
    wo = i["w_out_2"][0]
    wo = np.concatenate([wo[:512], by_group(wo[512:].T).T])
    o["out2"] = slots_of(wo)
    o["first_slots"] = c(np.stack([gu[0][0, 0], gu[0][1, 0], o["in2"][0]]))
    o["ff1"] = slots_of(i["w_ff1_2"][0])
    o["ff2"] = c(np.concatenate([slots_of(i["w_ff2_2"][0][g * D:(g + 1) * D]) for g in range(FF2_GROUPS)]))
    return o


def kernel(**inputs):
    import concourse.bacc as bacc
    from concourse.bass_utils import run_bass_kernel_spmd

    nc = bacc.Bacc("TRN2", target_bir_lowering=False, num_devices=1)
    arrays = {"in_" + n: np.ascontiguousarray(a) for n, a in lay_out({n: np.asarray(a) for n, a in inputs.items()}).items()}
    aps = {n[3:]: nc.dram_tensor(n, a.shape, mybir.dt.from_np(a.dtype), kind="ExternalInput").ap() for n, a in arrays.items()}
    out = nc.dram_tensor("out_t", (P, KD, S), F32, kind="ExternalOutput").ap()
    build(nc, aps, out)
    r = run_bass_kernel_spmd(nc, [arrays], core_ids=[0])
    got = r.results[0]["out_t"]
    return np.ascontiguousarray(got.transpose(1, 0, 2).reshape(D, S).T)[None]
```
